# Optimizing a Trainium2 kernel written in Bass

```python
import math
import jax, jax.numpy as jnp
from jax import lax
import numpy as np

D_MODEL = 1024
BATCH = 1
SEQ = 512
DEPTH = 1

GDN_HEADS = 8
GDN_HEAD_DIM = 128
GDN_WIDTH = GDN_HEADS * GDN_HEAD_DIM
SSD_HEADS = 16
SSD_HEAD_DIM = 64
SSD_WIDTH = SSD_HEADS * SSD_HEAD_DIM
SSD_GROUPS = 2
SSD_STATE = 128
BC_WIDTH = SSD_GROUPS * SSD_STATE
MIX_WIDTH = GDN_WIDTH + SSD_WIDTH
CONV_K = 7
CHUNK = 64
N_EXPERTS = 16
EXPERT_FF = 512
EC_FACTOR = 2
EPS = 1e-6
DT_MIN = 1e-3
DT_MAX = 0.1

CONV_CH = 3 * GDN_WIDTH + SSD_WIDTH + 2 * BC_WIDTH
GATE_CH = GDN_WIDTH + SSD_WIDTH
SCALAR_CH = 4 * GDN_HEADS + 2 * SSD_HEADS
PROJ_OUT = CONV_CH + GATE_CH + SCALAR_CH


F32 = jnp.float32

def rms_norm(x, w):
    xf = x.astype(F32)
    y = xf * lax.rsqrt(jnp.mean(xf * xf, axis=-1, keepdims=True) + EPS)
    return (y * w.astype(F32)).astype(x.dtype)

def l2_normalize(t):
    return t * lax.rsqrt(jnp.sum(t * t, axis=-1, keepdims=True) + EPS)

def centred_dwconv(x, w, b):
    pad = (CONV_K - 1) // 2
    L = x.shape[1]
    xp = jnp.pad(x, ((0, 0), (pad, pad), (0, 0)))
    out = xp[:, 0:L] * w[0]
    for tap in range(1, CONV_K):
        out = out + xp[:, tap:tap + L] * w[tap]
    return out + b

def flip_seq(t):
    return jnp.flip(t, axis=1)

def gated_delta_chunked(q, k, v, g, beta):
    Bsz, L, H, Dk = q.shape
    Dv = v.shape[-1]
    N = L // CHUNK

    def to_chunks(t):
        t = t.reshape((Bsz, N, CHUNK) + t.shape[2:])
        return jnp.swapaxes(t, 2, 3)

    q, k, v, g, beta = (to_chunks(t) for t in (q, k, v, g, beta))
    gc = jnp.cumsum(g, axis=-1)
    incl = jnp.tril(jnp.ones((CHUNK, CHUNK), bool))
    strict = jnp.tril(jnp.ones((CHUNK, CHUNK), bool), k=-1)
    decay = jnp.exp(jnp.where(incl, gc[..., :, None] - gc[..., None, :], -jnp.inf))
    kk = jnp.einsum('bnhid,bnhjd->bnhij', k, k)
    A = jnp.where(strict, beta[..., :, None] * kk * decay, 0.0)
    rhs = jnp.concatenate([v * beta[..., None], k * (beta * jnp.exp(gc))[..., None]], axis=-1)
    sol = lax.linalg.triangular_solve(A, rhs, left_side=True, lower=True, unit_diagonal=True)
    u_v, w_k = sol[..., :Dv], sol[..., Dv:]
    qk = jnp.einsum('bnhid,bnhjd->bnhij', q, k) * decay
    q_dec = q * jnp.exp(gc)[..., None]
    g_last = gc[..., -1]
    k_dec = k * jnp.exp(g_last[..., None] - gc)[..., None]

    def step(S, inp):
        u_c, w_c, qk_c, qd_c, kd_c, gl_c = inp
        u_new = u_c - jnp.einsum('bhik,bhkv->bhiv', w_c, S)
        o = jnp.einsum('bhik,bhkv->bhiv', qd_c, S) + jnp.einsum('bhij,bhjv->bhiv', qk_c, u_new)
        S = S * jnp.exp(gl_c)[..., None, None] + jnp.einsum('bhjk,bhjv->bhkv', kd_c, u_new)
        return S, o

    xs = tuple(jnp.moveaxis(t, 1, 0) for t in (u_v, w_k, qk, q_dec, k_dec, g_last))
    S0 = jnp.zeros((Bsz, H, Dk, Dv), F32)
    _, o = lax.scan(step, S0, xs)
    return jnp.transpose(o, (1, 0, 3, 2, 4)).reshape(Bsz, L, H, Dv)

def ssd_chunked(x, dt, A, Bm, Cm):
    Bsz, L, H, P = x.shape
    G, Ns = Bm.shape[2], Bm.shape[3]
    Hg = H // G
    N = L // CHUNK
    x = x.reshape(Bsz, N, CHUNK, G, Hg, P)
    dt = dt.reshape(Bsz, N, CHUNK, G, Hg)
    Bm = Bm.reshape(Bsz, N, CHUNK, G, Ns)
    Cm = Cm.reshape(Bsz, N, CHUNK, G, Ns)
    cs = jnp.cumsum(dt * A.reshape(G, Hg), axis=2)
    incl = jnp.tril(jnp.ones((CHUNK, CHUNK), bool))[:, :, None, None]
    Lmat = jnp.exp(jnp.where(incl, cs[:, :, :, None] - cs[:, :, None, :], -jnp.inf))
    cb = jnp.einsum('bnigs,bnjgs->bnijg', Cm, Bm)
    xdt = x * dt[..., None]
    y_intra = jnp.einsum('bnijgh,bnjghp->bnighp', cb[..., None] * Lmat, xdt)
    cs_last = cs[:, :, -1]
    w_state = jnp.exp(cs_last[:, :, None] - cs)
    chunk_states = jnp.einsum('bnjgs,bnjghp->bnghsp', Bm, xdt * w_state[..., None])

    def step(hst, inp):
        st, dec, c_c, ecs_c = inp
        y = jnp.einsum('bigs,bghsp->bighp', c_c, hst) * ecs_c[..., None]
        hst = hst * jnp.exp(dec)[..., None, None] + st
        return hst, y

    xs = tuple(jnp.moveaxis(t, 1, 0) for t in (chunk_states, cs_last, Cm, jnp.exp(cs)))
    h0 = jnp.zeros((Bsz, G, Hg, Ns, P), F32)
    _, y_inter = lax.scan(step, h0, xs)
    y = y_intra + jnp.moveaxis(y_inter, 0, 1)
    return y.reshape(Bsz, L, H, P)

def hybrid_mixer(n, w_in, conv_w, conv_b, gdn_A_log, gdn_dt_bias, gdn_norm_w,
                 ssd_A_log, ssd_dt_bias, ssd_D, ssd_norm_w, w_out):
    Bsz, L, _ = n.shape
    proj = jnp.einsum('bld,dp->blp', n, w_in)
    conv_in, gates, scal = jnp.split(proj, [CONV_CH, CONV_CH + GATE_CH], axis=-1)
    c = jax.nn.silu(centred_dwconv(conv_in, conv_w, conv_b)).astype(F32)
    q, k, v, xs, Bm, Cm = jnp.split(
        c, [GDN_WIDTH, 2 * GDN_WIDTH, 3 * GDN_WIDTH, 3 * GDN_WIDTH + SSD_WIDTH,
            3 * GDN_WIDTH + SSD_WIDTH + BC_WIDTH], axis=-1)
    g_gate, z = jnp.split(gates.astype(F32), [GDN_WIDTH], axis=-1)
    gh, sh = GDN_HEADS, SSD_HEADS
    b_f, b_b, a_f, a_b, dt_f, dt_b = jnp.split(
        scal.astype(F32), [gh, 2 * gh, 3 * gh, 4 * gh, 4 * gh + sh], axis=-1)

    q = l2_normalize(q.reshape(Bsz, L, gh, GDN_HEAD_DIM)) * (GDN_HEAD_DIM ** -0.5)
    k = l2_normalize(k.reshape(Bsz, L, gh, GDN_HEAD_DIM))
    v = v.reshape(Bsz, L, gh, GDN_HEAD_DIM)
    gA = gdn_A_log.astype(F32)
    gB = gdn_dt_bias.astype(F32)
    g_fw = -jnp.exp(gA[0]) * jax.nn.softplus(a_f + gB[0])
    g_bw = -jnp.exp(gA[1]) * jax.nn.softplus(a_b + gB[1])
    o_fw = gated_delta_chunked(q, k, v, g_fw, jax.nn.sigmoid(b_f))
    o_bw = flip_seq(gated_delta_chunked(flip_seq(q), flip_seq(k), flip_seq(v),
                                        flip_seq(g_bw), flip_seq(jax.nn.sigmoid(b_b))))
    o_gdn = rms_norm(o_fw + o_bw, gdn_norm_w) * jax.nn.silu(g_gate.reshape(Bsz, L, gh, GDN_HEAD_DIM))
    o_gdn = o_gdn.reshape(Bsz, L, GDN_WIDTH)

    x_ssd = xs.reshape(Bsz, L, sh, SSD_HEAD_DIM)
    Bm = Bm.reshape(Bsz, L, SSD_GROUPS, SSD_STATE)
    Cm = Cm.reshape(Bsz, L, SSD_GROUPS, SSD_STATE)
    sA = -jnp.exp(ssd_A_log.astype(F32))
    sB = ssd_dt_bias.astype(F32)
    dt_fw = jax.nn.softplus(dt_f + sB[0])
    dt_bw = jax.nn.softplus(dt_b + sB[1])
    y_fw = ssd_chunked(x_ssd, dt_fw, sA[0], Bm, Cm)
    y_bw = flip_seq(ssd_chunked(flip_seq(x_ssd), flip_seq(dt_bw), sA[1], flip_seq(Bm), flip_seq(Cm)))
    y = y_fw + y_bw + ssd_D.astype(F32)[:, None] * x_ssd
    y = y.reshape(Bsz, L, SSD_WIDTH) * jax.nn.silu(z)
    y = rms_norm(y.reshape(Bsz, L, SSD_GROUPS, SSD_WIDTH // SSD_GROUPS),
                 ssd_norm_w.reshape(SSD_GROUPS, SSD_WIDTH // SSD_GROUPS)).reshape(Bsz, L, SSD_WIDTH)

    mixed = jnp.concatenate([o_gdn, y], axis=-1).astype(n.dtype)
    return jnp.einsum('blm,md->bld', mixed, w_out)

def expert_choice_ffn(n, w_router, w_gate, w_up, w_down):
    Bsz, L, D = n.shape
    cap = EC_FACTOR * L // N_EXPERTS
    logits = jnp.einsum('bld,de->ble', n, w_router).astype(F32)
    aff = jax.nn.softmax(logits, axis=-1)
    vals, idx = lax.top_k(jnp.swapaxes(aff, 1, 2), cap)
    xs = jax.vmap(lambda hb, ib: hb[ib])(n, idx)
    a = jnp.einsum('becd,edf->becf', xs, w_gate)
    u = jnp.einsum('becd,edf->becf', xs, w_up)
    y = jnp.einsum('becf,efd->becd', jax.nn.silu(a) * u, w_down) * vals[..., None].astype(n.dtype)
    return jax.vmap(lambda yb, ib: jnp.zeros((L, D), yb.dtype).at[ib.reshape(-1)].add(yb.reshape(-1, D)))(y, idx)

def _inv_softplus(t):
    return t + jnp.log(-jnp.expm1(-t))

def first_inputs(seed: int = 0) -> dict:
    key = jax.random.key(seed)
    ks = jax.random.split(key, 20)

    def normal(k, shape, scale):
        return jax.random.normal(k, shape, F32) * scale

    def gain(k, shape):
        return 1.0 + 0.02 * jax.random.normal(k, shape, F32)

    def dt_bias(k, shape):
        u = jax.random.uniform(k, shape, F32)
        dt = jnp.exp(u * (math.log(DT_MAX) - math.log(DT_MIN)) + math.log(DT_MIN))
        return _inv_softplus(dt)

    def a_log(k, shape):
        return jnp.log(jax.random.uniform(k, shape, F32, 1.0, 16.0))

    return {
        "x": jax.random.normal(ks[0], (BATCH, SEQ, D_MODEL), F32),
        "norm1_w": gain(ks[1], (DEPTH, D_MODEL)),
        "w_in": normal(ks[2], (DEPTH, D_MODEL, PROJ_OUT), D_MODEL ** -0.5),
        "conv_w": normal(ks[3], (DEPTH, CONV_K, CONV_CH), CONV_K ** -0.5),
        "conv_b": normal(ks[4], (DEPTH, CONV_CH), 0.01),
        "gdn_A_log": a_log(ks[5], (DEPTH, 2, GDN_HEADS)),
        "gdn_dt_bias": dt_bias(ks[6], (DEPTH, 2, GDN_HEADS)),
        "gdn_norm_w": gain(ks[7], (DEPTH, GDN_HEAD_DIM)),
        "ssd_A_log": a_log(ks[8], (DEPTH, 2, SSD_HEADS)),
        "ssd_dt_bias": dt_bias(ks[9], (DEPTH, 2, SSD_HEADS)),
        "ssd_D": gain(ks[10], (DEPTH, SSD_HEADS)),
        "ssd_norm_w": gain(ks[11], (DEPTH, SSD_WIDTH)),
        "w_out": normal(ks[12], (DEPTH, MIX_WIDTH, D_MODEL), MIX_WIDTH ** -0.5),
        "norm2_w": gain(ks[13], (DEPTH, D_MODEL)),
        "w_router": normal(ks[14], (DEPTH, D_MODEL, N_EXPERTS), D_MODEL ** -0.5),
        "w_gate": normal(ks[15], (DEPTH, N_EXPERTS, D_MODEL, EXPERT_FF), D_MODEL ** -0.5),
        "w_up": normal(ks[16], (DEPTH, N_EXPERTS, D_MODEL, EXPERT_FF), D_MODEL ** -0.5),
        "w_down": normal(ks[17], (DEPTH, N_EXPERTS, EXPERT_FF, D_MODEL), EXPERT_FF ** -0.5),
        "final_norm_w": gain(ks[18], (D_MODEL,)),
    }

def first_block(x, norm1_w, w_in, conv_w, conv_b, gdn_A_log, gdn_dt_bias, gdn_norm_w,
              ssd_A_log, ssd_dt_bias, ssd_D, ssd_norm_w, w_out, norm2_w, w_router,
              w_gate, w_up, w_down, final_norm_w):
    h = x
    for layer in range(DEPTH):
        h = h + hybrid_mixer(rms_norm(h, norm1_w[layer]), w_in[layer], conv_w[layer], conv_b[layer],
                             gdn_A_log[layer], gdn_dt_bias[layer], gdn_norm_w[layer],
                             ssd_A_log[layer], ssd_dt_bias[layer], ssd_D[layer], ssd_norm_w[layer],
                             w_out[layer])
        h = h + expert_choice_ffn(rms_norm(h, norm2_w[layer]), w_router[layer], w_gate[layer],
                                  w_up[layer], w_down[layer])
    return rms_norm(h, final_norm_w)


DEPTH_2 = 2

HEAD_DIM = 64
MLA_HEADS = 6
MLA_NOPE = 64
MLA_ROPE = 32
MLA_V = 64
MLA_Q_LORA = 256
MLA_KV_LORA = 128
NSA_HEADS = 6
NSA_KV_HEADS = 2
NSA_GROUP = NSA_HEADS // NSA_KV_HEADS
NSA_BRANCHES = 3
CMP_LEN = 32
CMP_STRIDE = 16
CMP_HIDDEN = 128
SEL_LEN = 64
SEL_TOPK = 16
WINDOW = 512
SB_HEADS = 4
D_MIX = MLA_HEADS * MLA_V + NSA_HEADS * HEAD_DIM + SB_HEADS * HEAD_DIM
D_FF = 2816
ROPE_THETA = 500000.0
PARTIAL_ROT = HEAD_DIM // 4
Q_BLOCK = 128
NEG_INF = -1e30
FORCE_SCORE = 1e4
NSA_KV_W = NSA_KV_HEADS * HEAD_DIM
IN_WIDTHS = (MLA_Q_LORA, MLA_KV_LORA, MLA_ROPE,
             NSA_HEADS * HEAD_DIM,
             NSA_KV_W, NSA_KV_W, NSA_KV_W, NSA_KV_W, NSA_KV_W, NSA_KV_W,
             NSA_HEADS * NSA_BRANCHES,
             SB_HEADS * HEAD_DIM, SB_HEADS * HEAD_DIM, SB_HEADS * HEAD_DIM)
D_IN = sum(IN_WIDTHS)


def rmsnorm(x, g):
    xf = x.astype(jnp.float32)
    y = xf * lax.rsqrt(jnp.mean(xf * xf, axis=-1, keepdims=True) + EPS)
    return (y * g.astype(jnp.float32)).astype(x.dtype)

def rope(x, pos, rot_dim):
    half = rot_dim // 2
    inv_freq = ROPE_THETA ** (-jnp.arange(half, dtype=jnp.float32) / half)
    ang = pos.astype(jnp.float32)[:, None] * inv_freq[None, :]
    cos = jnp.cos(ang)[:, None, :]
    sin = jnp.sin(ang)[:, None, :]
    xr = x[..., :rot_dim].astype(jnp.float32)
    x1, x2 = xr[..., :half], xr[..., half:]
    rot = jnp.concatenate([x1 * cos - x2 * sin, x2 * cos + x1 * sin], axis=-1)
    return jnp.concatenate([rot.astype(x.dtype), x[..., rot_dim:]], axis=-1)

def masked_softmax(s, mask):
    return jax.nn.softmax(jnp.where(mask, s.astype(jnp.float32), NEG_INF), axis=-1)

def swiglu(h, w_gate, w_up, w_down):
    return (jax.nn.silu(h @ w_gate) * (h @ w_up)) @ w_down

def split_heads(t, n_heads):
    b, s, _ = t.shape
    return t.reshape(b, s, n_heads, -1)

def sweep_query_blocks(block_fn, n_blocks):
    out = lax.map(block_fn, jnp.arange(n_blocks, dtype=jnp.int32))
    nb, b, q, h, d = out.shape
    return out.transpose(1, 0, 2, 3, 4).reshape(b, nb * q, h, d)

def mla_attention(c_q, c_kv, k_rope, q_norm, w_uq, kv_norm, w_ukv, pos):
    b, s, _ = c_q.shape
    q = (rmsnorm(c_q, q_norm) @ w_uq).reshape(b, s, MLA_HEADS, MLA_NOPE + MLA_ROPE)
    q_nope = q[..., :MLA_NOPE]
    q_pe = rope(q[..., MLA_NOPE:], pos, MLA_ROPE)
    kv = (rmsnorm(c_kv, kv_norm) @ w_ukv).reshape(b, s, MLA_HEADS, MLA_NOPE + MLA_V)
    k_nope, v = kv[..., :MLA_NOPE], kv[..., MLA_NOPE:]
    k_pe = rope(k_rope[:, :, None, :], pos, MLA_ROPE)[:, :, 0]
    scale = (MLA_NOPE + MLA_ROPE) ** -0.5

    def block(i):
        q0 = i * Q_BLOCK
        qn = lax.dynamic_slice_in_dim(q_nope, q0, Q_BLOCK, axis=1)
        qp = lax.dynamic_slice_in_dim(q_pe, q0, Q_BLOCK, axis=1)
        sc = (jnp.einsum('bqhd,bkhd->bhqk', qn, k_nope)
              + jnp.einsum('bqhr,bkr->bhqk', qp, k_pe)).astype(jnp.float32) * scale
        qpos = q0 + jnp.arange(Q_BLOCK)
        p = masked_softmax(sc, pos[None, :] <= qpos[:, None]).astype(v.dtype)
        return jnp.einsum('bhqk,bkhd->bqhd', p, v)

    return sweep_query_blocks(block, s // Q_BLOCK)

def compress_blocks(x, pos_emb, w1, w2):
    b, s, g, d = x.shape
    chunks = x.reshape(b, s // CMP_STRIDE, CMP_STRIDE, g, d)
    blocks = jnp.concatenate([chunks[:, :-1], chunks[:, 1:]], axis=2)
    blocks = blocks + pos_emb[None, None, :, None, :]
    flat = blocks.transpose(0, 1, 3, 2, 4).reshape(b, s // CMP_STRIDE - 1, g, CMP_LEN * d)
    return jax.nn.gelu(flat @ w1) @ w2

def nsa_attention(q, k_cmp, v_cmp, k_sel, v_sel, k_win, v_win, gates,
                  cmp_pos_k, cmp_w1_k, cmp_w2_k, cmp_pos_v, cmp_w1_v, cmp_w2_v, pos):
    b, s, h, d = q.shape
    q = rope(q, pos, PARTIAL_ROT)
    k_cmp = rope(k_cmp, pos, PARTIAL_ROT)
    k_sel = rope(k_sel, pos, PARTIAL_ROT)
    k_win = rope(k_win, pos, PARTIAL_ROT)
    scale = d ** -0.5
    kc = compress_blocks(k_cmp, cmp_pos_k, cmp_w1_k, cmp_w2_k)
    vc = compress_blocks(v_cmp, cmp_pos_v, cmp_w1_v, cmp_w2_v)
    n_cmp = s // CMP_STRIDE - 1
    cmp_start = jnp.arange(n_cmp) * CMP_STRIDE
    cmp_end = cmp_start + CMP_LEN - 1
    n_slc = s // SEL_LEN
    n_top = min(SEL_TOPK, n_slc)
    slc_start = jnp.arange(n_slc) * SEL_LEN
    overlap = ((cmp_start[:, None] < slc_start[None, :] + SEL_LEN)
               & (cmp_start[:, None] + CMP_LEN > slc_start[None, :])).astype(jnp.float32)
    ksb = k_sel.reshape(b, n_slc, SEL_LEN, NSA_KV_HEADS, d).transpose(0, 3, 1, 2, 4)
    vsb = v_sel.reshape(b, n_slc, SEL_LEN, NSA_KV_HEADS, d).transpose(0, 3, 1, 2, 4)
    b_ix = jnp.arange(b)[:, None, None, None]
    g_ix = jnp.arange(NSA_KV_HEADS)[None, :, None, None]
    blk = jnp.arange(n_slc)
    kw = jnp.pad(k_win, ((0, 0), (WINDOW, 0), (0, 0), (0, 0)))
    vw = jnp.pad(v_win, ((0, 0), (WINDOW, 0), (0, 0), (0, 0)))

    def block(i):
        q0 = i * Q_BLOCK
        qpos = q0 + jnp.arange(Q_BLOCK)
        qb = lax.dynamic_slice_in_dim(q, q0, Q_BLOCK, axis=1).reshape(b, Q_BLOCK, NSA_KV_HEADS, NSA_GROUP, d)
        sc = jnp.einsum('bqgrd,bcgd->bgrqc', qb, kc).astype(jnp.float32) * scale
        cmask = cmp_end[None, :] <= qpos[:, None]
        p_cmp = masked_softmax(sc, cmask)
        p_cmp = jnp.where(cmask.any(axis=-1)[:, None], p_cmp, 0.0)
        o_cmp = jnp.einsum('bgrqc,bcgd->bqgrd', p_cmp.astype(vc.dtype), vc)
        score = jnp.einsum('bgrqc,cn->bgqn', p_cmp, overlap)
        cur = qpos // SEL_LEN
        forced = (blk[None, :] == 0) | (blk[None, :] == cur[:, None]) | (blk[None, :] == cur[:, None] - 1)
        future = blk[None, :] > cur[:, None]
        score = jnp.where(forced, FORCE_SCORE, jnp.where(future, -1.0, score))
        _, idx = lax.top_k(score, n_top)
        kg = ksb[b_ix, g_ix, idx]
        vg = vsb[b_ix, g_ix, idx]
        tok = idx[..., None] * SEL_LEN + jnp.arange(SEL_LEN)
        smask = (tok <= qpos[None, None, :, None, None])[:, :, None]
        ss = jnp.einsum('bqgrd,bgqnld->bgrqnl', qb, kg).astype(jnp.float32) * scale
        ss = jnp.where(smask, ss, NEG_INF).reshape(b, NSA_KV_HEADS, NSA_GROUP, Q_BLOCK, n_top * SEL_LEN)
        p_sel = jax.nn.softmax(ss, axis=-1).astype(vg.dtype).reshape(b, NSA_KV_HEADS, NSA_GROUP, Q_BLOCK, n_top, SEL_LEN)
        o_sel = jnp.einsum('bgrqnl,bgqnld->bqgrd', p_sel, vg)
        kwb = lax.dynamic_slice_in_dim(kw, q0, WINDOW + Q_BLOCK, axis=1)
        vwb = lax.dynamic_slice_in_dim(vw, q0, WINDOW + Q_BLOCK, axis=1)
        wpos = q0 - WINDOW + jnp.arange(WINDOW + Q_BLOCK)
        wmask = ((wpos[None, :] <= qpos[:, None]) & (wpos[None, :] > qpos[:, None] - WINDOW)
                 & (wpos[None, :] >= 0))
        sw = jnp.einsum('bqgrd,bkgd->bgrqk', qb, kwb).astype(jnp.float32) * scale
        p_win = masked_softmax(sw, wmask).astype(vwb.dtype)
        o_win = jnp.einsum('bgrqk,bkgd->bqgrd', p_win, vwb)
        g = lax.dynamic_slice_in_dim(gates, q0, Q_BLOCK, axis=1).reshape(b, Q_BLOCK, NSA_KV_HEADS, NSA_GROUP, NSA_BRANCHES)
        o = g[..., 0:1] * o_cmp + g[..., 1:2] * o_sel + g[..., 2:3] * o_win
        return o.reshape(b, Q_BLOCK, h, d)

    return sweep_query_blocks(block, s // Q_BLOCK)

def stick_breaking_attention(q, k, v):
    b, s, h, d = q.shape
    scale = d ** -0.5
    kpos = jnp.arange(s)

    def block(i):
        q0 = i * Q_BLOCK
        qpos = q0 + jnp.arange(Q_BLOCK)
        qb = lax.dynamic_slice_in_dim(q, q0, Q_BLOCK, axis=1)
        z = jnp.einsum('bqhd,bkhd->bhqk', qb, k).astype(jnp.float32) * scale
        strict = kpos[None, :] < qpos[:, None]
        log_beta = jax.nn.log_sigmoid(z)
        log_rem = jnp.where(strict, jax.nn.log_sigmoid(-z), 0.0)
        suffix = lax.cumsum(log_rem, axis=3, reverse=True) - log_rem
        a = jnp.where(strict, jnp.exp(log_beta + suffix), 0.0).astype(v.dtype)
        return jnp.einsum('bhqk,bkhd->bqhd', a, v)

    return sweep_query_blocks(block, s // Q_BLOCK)

def second_inputs(seed: int = 0) -> dict:
    key = jax.random.key(seed)
    ks = iter(jax.random.split(key, 32))
    f32 = jnp.float32
    L = DEPTH_2

    def nrm(shape, fan_in):
        return jax.random.normal(next(ks), shape, f32) * (fan_in ** -0.5)

    def gain(shape):
        return 1.0 + 0.02 * jax.random.normal(next(ks), shape, f32)

    return {
        'x': jax.random.normal(next(ks), (BATCH, SEQ, D_MODEL), f32),
        'ffn1_norm': gain((L, D_MODEL)),
        'ffn1_w_gate': nrm((L, D_MODEL, D_FF), D_MODEL),
        'ffn1_w_up': nrm((L, D_MODEL, D_FF), D_MODEL),
        'ffn1_w_down': nrm((L, D_FF, D_MODEL), D_FF),
        'mix_norm': gain((L, D_MODEL)),
        'w_in': nrm((L, D_MODEL, D_IN), D_MODEL),
        'mla_q_norm': gain((L, MLA_Q_LORA)),
        'mla_w_uq': nrm((L, MLA_Q_LORA, MLA_HEADS * (MLA_NOPE + MLA_ROPE)), MLA_Q_LORA),
        'mla_kv_norm': gain((L, MLA_KV_LORA)),
        'mla_w_ukv': nrm((L, MLA_KV_LORA, MLA_HEADS * (MLA_NOPE + MLA_V)), MLA_KV_LORA),
        'nsa_gate_bias': 0.1 * jax.random.normal(next(ks), (L, NSA_HEADS * NSA_BRANCHES), f32),
        'nsa_cmp_pos_k': 0.1 * jax.random.normal(next(ks), (L, CMP_LEN, HEAD_DIM), f32),
        'nsa_cmp_w1_k': nrm((L, CMP_LEN * HEAD_DIM, CMP_HIDDEN), CMP_LEN * HEAD_DIM),
        'nsa_cmp_w2_k': nrm((L, CMP_HIDDEN, HEAD_DIM), CMP_HIDDEN),
        'nsa_cmp_pos_v': 0.1 * jax.random.normal(next(ks), (L, CMP_LEN, HEAD_DIM), f32),
        'nsa_cmp_w1_v': nrm((L, CMP_LEN * HEAD_DIM, CMP_HIDDEN), CMP_LEN * HEAD_DIM),
        'nsa_cmp_w2_v': nrm((L, CMP_HIDDEN, HEAD_DIM), CMP_HIDDEN),
        'w_out': nrm((L, D_MIX, D_MODEL), D_MIX),
        'ffn2_norm': gain((L, D_MODEL)),
        'ffn2_w_gate': nrm((L, D_MODEL, D_FF), D_MODEL),
        'ffn2_w_up': nrm((L, D_MODEL, D_FF), D_MODEL),
        'ffn2_w_down': nrm((L, D_FF, D_MODEL), D_FF),
        'final_norm': gain((D_MODEL,)),
    }

def second_block(x, ffn1_norm, ffn1_w_gate, ffn1_w_up, ffn1_w_down, mix_norm, w_in,
              mla_q_norm, mla_w_uq, mla_kv_norm, mla_w_ukv,
              nsa_gate_bias, nsa_cmp_pos_k, nsa_cmp_w1_k, nsa_cmp_w2_k,
              nsa_cmp_pos_v, nsa_cmp_w1_v, nsa_cmp_w2_v, w_out,
              ffn2_norm, ffn2_w_gate, ffn2_w_up, ffn2_w_down, final_norm):
    b, s, _ = x.shape
    pos = jnp.arange(s, dtype=jnp.int32)
    split_at = [int(c) for c in np.cumsum(IN_WIDTHS)[:-1]]
    for l in range(DEPTH_2):
        x = x + 0.5 * swiglu(rmsnorm(x, ffn1_norm[l]), ffn1_w_gate[l], ffn1_w_up[l], ffn1_w_down[l])
        h = rmsnorm(x, mix_norm[l])
        (c_q, c_kv, k_rope, n_q, n_kc, n_vc, n_ks, n_vs, n_kw, n_vw, n_gate,
         sb_q, sb_k, sb_v) = jnp.split(h @ w_in[l], split_at, axis=-1)
        o_mla = mla_attention(c_q, c_kv, k_rope, mla_q_norm[l], mla_w_uq[l],
                              mla_kv_norm[l], mla_w_ukv[l], pos)
        gates = jax.nn.sigmoid(n_gate + nsa_gate_bias[l]).reshape(b, s, NSA_HEADS, NSA_BRANCHES)
        o_nsa = nsa_attention(split_heads(n_q, NSA_HEADS),
                              split_heads(n_kc, NSA_KV_HEADS), split_heads(n_vc, NSA_KV_HEADS),
                              split_heads(n_ks, NSA_KV_HEADS), split_heads(n_vs, NSA_KV_HEADS),
                              split_heads(n_kw, NSA_KV_HEADS), split_heads(n_vw, NSA_KV_HEADS),
                              gates, nsa_cmp_pos_k[l], nsa_cmp_w1_k[l], nsa_cmp_w2_k[l],
                              nsa_cmp_pos_v[l], nsa_cmp_w1_v[l], nsa_cmp_w2_v[l], pos)
        o_sb = stick_breaking_attention(split_heads(sb_q, SB_HEADS), split_heads(sb_k, SB_HEADS),
                                        split_heads(sb_v, SB_HEADS))
        o = jnp.concatenate([o_mla.reshape(b, s, -1), o_nsa.reshape(b, s, -1),
                             o_sb.reshape(b, s, -1)], axis=-1)
        x = x + o @ w_out[l]
        x = x + 0.5 * swiglu(rmsnorm(x, ffn2_norm[l]), ffn2_w_gate[l], ffn2_w_up[l], ffn2_w_down[l])
    return rmsnorm(x, final_norm)


def setup_inputs(seed=0):
    out = dict(first_inputs(seed))
    for name, value in second_inputs(seed + 1).items():
        if name != "x":
            out[name + "_2"] = value
    return out


def reference(
    x, norm1_w, w_in, conv_w, conv_b, gdn_A_log, gdn_dt_bias, gdn_norm_w, ssd_A_log,
    ssd_dt_bias, ssd_D, ssd_norm_w, w_out, norm2_w, w_router, w_gate, w_up, w_down,
    final_norm_w, ffn1_norm_2, ffn1_w_gate_2, ffn1_w_up_2, ffn1_w_down_2, mix_norm_2, w_in_2,
    mla_q_norm_2, mla_w_uq_2, mla_kv_norm_2, mla_w_ukv_2, nsa_gate_bias_2, nsa_cmp_pos_k_2,
    nsa_cmp_w1_k_2, nsa_cmp_w2_k_2, nsa_cmp_pos_v_2, nsa_cmp_w1_v_2, nsa_cmp_w2_v_2, w_out_2,
    ffn2_norm_2, ffn2_w_gate_2, ffn2_w_up_2, ffn2_w_down_2, final_norm_2,
):
    x = first_block(
        x, norm1_w, w_in, conv_w, conv_b, gdn_A_log, gdn_dt_bias, gdn_norm_w, ssd_A_log,
        ssd_dt_bias, ssd_D, ssd_norm_w, w_out, norm2_w, w_router, w_gate, w_up, w_down,
        final_norm_w,
    )
    return second_block(
        x, ffn1_norm_2, ffn1_w_gate_2, ffn1_w_up_2, ffn1_w_down_2, mix_norm_2, w_in_2,
        mla_q_norm_2, mla_w_uq_2, mla_kv_norm_2, mla_w_ukv_2, nsa_gate_bias_2, nsa_cmp_pos_k_2,
        nsa_cmp_w1_k_2, nsa_cmp_w2_k_2, nsa_cmp_pos_v_2, nsa_cmp_w1_v_2, nsa_cmp_w2_v_2,
        w_out_2, ffn2_norm_2, ffn2_w_gate_2, ffn2_w_up_2, ffn2_w_down_2, final_norm_2,
    )


_drawn_inputs = setup_inputs


def setup_inputs(seed=0):
    import zlib

    import numpy as np

    out = dict(_drawn_inputs(seed))
    spreads = {}
    factors = {'conv_b': 3.464,
     'gdn_norm_w': 4.628,
     'ssd_D': 6.873,
     'ssd_norm_w': 3.528,
     'norm2_w': 3.378,
     'ffn1_norm_2': 4.707,
     'mix_norm_2': 4.656,
     'mla_q_norm_2': 8.0,
     'mla_kv_norm_2': 8.0,
     'nsa_gate_bias_2': 5.224,
     'nsa_cmp_pos_k_2': 8.0,
     'ffn2_norm_2': 5.405,
     'final_norm_2': 8.184,
     'nsa_cmp_pos_v_2': 4.308}
    for name, (base, spread) in spreads.items():
        noise = np.random.default_rng([zlib.crc32(name.encode()), seed]).standard_normal(out[name].shape)
        drawn = base * np.exp(spread * noise) if base else spread * noise
        out[name] = __import__('jax').numpy.asarray(drawn.astype(out[name].dtype))
    for name, factor in factors.items():
        out[name] = (out[name] * factor).astype(out[name].dtype)
    return out
```

```python
from contextlib import ExitStack, contextmanager

import concourse.bass as bass
import numpy as np
from concourse import mybir

F32 = mybir.dt.float32
F32R = mybir.dt.float32r
U8 = mybir.dt.uint8
ALU = mybir.AluOpType
ACT = mybir.ActivationFunctionType
AX = mybir.AxisListType.X

P = 128
T = 512
D = 1024
KD = D // P
NT = T // P
SLAB = 2048
SLOTS = 4
EPS = 1e-6

GH = 8
SH = 16
SG = 2
GK = 7
NG = GH + SH
NE = 16
EF = 512
CAP = 64
FF = 2816
FT = FF // P
LAYERS = 2
MASKED = -1e30


class Buffers:
    pass


class Sems:

    def __init__(self, handles):
        self.free = list(handles)

    def __call__(self, n=None):
        if n is None:
            return self.free.pop(0)
        return [self.free.pop(0) for _ in range(n)]


@contextmanager
def stage(nc, m, name):
    with nc.Block(name) as block:
        yield block, Sems(m.signals)
    nc.all_engine_barrier(sems_to_clear=range(m.signals[0].num, m.signals[-1].num + 1))


class Chain:

    def __init__(self, eng, sem):
        self.eng, self.sem, self.n = eng, sem, 0

    def __call__(self, ins):
        ins.then_inc(self.sem, 1)
        self.n += 1
        self.eng.wait_ge(self.sem, self.n)


def cut(buf, at, *shape):
    n = int(np.prod(shape))
    flat = buf[:, at:at + n]
    if len(shape) == 1:
        return flat
    names = "abcd"[:len(shape)]
    return flat.rearrange(f"p ({' '.join(names)}) -> p {' '.join(names)}", **dict(zip(names, shape)))


def tok(t):
    return slice(t * P, (t + 1) * P)


def load_slabs(sp, m, slabs, first, n, landed, used, per_slab):
    for i in range(n):
        if i >= SLOTS:
            sp.wait_ge(used, per_slab * (i - SLOTS + 1))
        sp.dma_start(m.ring[:, i % SLOTS, :], slabs[first + i]).then_inc(landed[i % SLOTS], 16)


def slab_landed(pe, landed, i):
    pe.wait_ge(landed[i % SLOTS], 16 * (i // SLOTS + 1))


def product(pe, out, weights, moving, n=KD):
    for k in range(n):
        ins = pe.matmul(out, weights(k), moving(k), start=(k == 0), stop=(k == n - 1))
    return ins


def columns(m, i, half, width=P):
    w = m.ring[:, i % SLOTS, :].rearrange("p (k n) -> p k n", k=KD)
    return lambda k: w[:, k, half * P:half * P + width]


def norm_stage(nc, m, name, src, gain, dst, tiles=KD, width=D):
    with stage(nc, m, name) as (block, sem):
        squared, summed, rooted, mean, chain = sem(5)
        sq = cut(m.norm_tmp, 0, 2, T)
        rstd = cut(m.norm_tmp, 2 * T, T)

        @block.scalar
        def _(act):
            for k in range(tiles):
                if k >= 2:
                    act.wait_ge(summed, k - 1)
                act.activation(sq[:, k % 2, :], src[:, k, :], ACT.Square).then_inc(squared, 1)
            act.wait_ge(mean, 1)
            act.activation(rstd, rstd, ACT.Sqrt).then_inc(rooted, 1)

        @block.tensor
        def _(pe):
            for k in range(tiles):
                pe.wait_ge(squared, k + 1)
                pe.matmul(m.ps[:, 0, :], m.ones, sq[:, k % 2, :], start=(k == 0),
                          stop=(k == tiles - 1)).then_inc(summed, 1)

        @block.vector
        def _(dve):
            dve.wait_ge(summed, tiles)
            dve.tensor_scalar(rstd, m.ps[:, 0, :], 1.0 / width, EPS, ALU.mult, ALU.add).then_inc(mean, 1)
            dve.wait_ge(rooted, 1)
            link = Chain(dve, chain)
            link(dve.reciprocal(rstd, rstd))
            for k in range(tiles):
                dve.scalar_tensor_tensor(dst[:, k, :], src[:, k, :], gain[:, k:k + 1], rstd,
                                         ALU.mult, ALU.mult)


def ffn_stage(nc, m, name, gain, slabs, scale):
    with ExitStack() as ctx:
        def sb(what, *shape, dt=F32R):
            return ctx.enter_context(nc.sbuf_tensor(f"{name}_{what}", [P, *shape], dt))

        x_hi, x_lo = sb("x_hi", KD, T), sb("x_lo", KD, T)
        w_hi, w_lo = sb("w_hi", 2, SLAB), sb("w_lo", 2, SLAB)
        hid_hi, hid_lo = sb("hid_hi", FT, T), sb("hid_lo", FT, T)
        raw = sb("raw", 2, SLAB, dt=F32)
        tmp = sb("tmp", 3, T, dt=F32)
        ups, downs = FT, FT // 2
        rstd = tmp[:, 2, :]

        with stage(nc, m, name) as (block, sem):
            landed = sem(2)
            hi_done, split, gated, used, silued, multiplied, hid_hi_done, hidden = sem(8)
            squared, summed, mean, rooted, scaled, x_hi_done, x_done, chain, banked = sem(9)

            def ups_then_downs(eng, up, down, last, n_down=downs):
                for n in (0, 1):
                    up(n)
                with eng.Fori(1, ups // 2) as i:
                    for q in (0, 1):
                        up(2 * i + q, q)
                for j in (0, 1):
                    down(j)
                with eng.Fori(1, n_down // 2) as i:
                    for q in (0, 1):
                        down(2 * i + q, q)
                last(n_down - 1)

            @block.sync
            def _(sp):
                def load(i, q=None):
                    q = i if q is None else q
                    if not isinstance(i, int) or i >= 2:
                        sp.wait_ge(split, i - 1)
                    sp.dma_start(raw[:, q % 2, :], slabs[i]).then_inc(landed[q % 2], 16)
                ups_then_downs(sp, load, lambda j, q=None: load(ups + j, j if q is None else q),
                               lambda j: load(ups + j, 0))

            @block.scalar
            def _(act):
                def w_part(i, q):
                    act.wait_ge(landed[q], 8 * i + (16 - 8 * q))
                    if not isinstance(i, int) or i >= 2:
                        act.wait_ge(used, i - 1)
                    act.activation(w_hi[:, q, :], raw[:, q, :], ACT.Copy).then_inc(hi_done, 1)

                for k in range(KD):
                    if k >= 2:
                        act.wait_ge(summed, k - 1)
                    act.activation(tmp[:, k % 2, :], m.resid[:, k, :], ACT.Square).then_inc(squared, 1)
                w_part(0, 0)
                act.wait_ge(mean, 1)
                act.activation(rstd, rstd, ACT.Sqrt).then_inc(rooted, 1)
                for k in range(KD):
                    act.wait_ge(scaled, k + 1)
                    act.activation(x_hi[:, k, :], tmp[:, k % 2, :], ACT.Copy, scale=gain[:, k:k + 1])\
                        .then_inc(x_hi_done, 1)
                w_part(1, 1)

                def up(n, q=None):
                    q = n if q is None else q
                    act.wait_ge(gated, n + 1)
                    if not isinstance(n, int) or n >= 2:
                        act.wait_ge(hidden, n - 1)
                    else:
                        act.wait_ge(x_done, KD)
                    act.activation(tmp[:, q, :], m.ps[:, 2 * q, :], ACT.Silu).then_inc(silued, 1)
                    w_part(n + 2, q)
                    act.wait_ge(multiplied, n + 1)
                    act.activation(hid_hi[:, n, :], tmp[:, q, :], ACT.Copy).then_inc(hid_hi_done, 1)

                def down(j, q=None):
                    w_part(ups + j + 2, j if q is None else q)
                ups_then_downs(act, up, down, lambda j: down(j, 0), downs - 2)

            @block.vector
            def _(dve):
                def w_part(i, q):
                    dve.wait_ge(hi_done, i + 1)
                    dve.tensor_tensor(w_lo[:, q, :], raw[:, q, :], w_hi[:, q, :].bitcast(F32), ALU.subtract)\
                        .then_inc(split, 1)

                w_part(0, 0)
                dve.wait_ge(summed, KD)
                dve.tensor_scalar(rstd, m.ps[:, 7, :], 1.0 / D, EPS, ALU.mult, ALU.add).then_inc(mean, 1)
                dve.wait_ge(rooted, 1)
                dve.reciprocal(rstd, rstd).then_inc(chain, 1)
                for k in range(KD):
                    dve.wait_ge(x_hi_done, k + 1)
                    dve.scalar_tensor_tensor(x_lo[:, k, :], tmp[:, k % 2, :], gain[:, k:k + 1],
                                             x_hi[:, k, :].bitcast(F32), ALU.mult, ALU.subtract)\
                        .then_inc(x_done, 1)
                w_part(1, 1)

                def up(n, q=None):
                    q = n if q is None else q
                    dve.wait_ge(silued, n + 1)
                    dve.wait_ge(used, n + 1)
                    dve.tensor_tensor(tmp[:, q, :], tmp[:, q, :], m.ps[:, 2 * q + 1, :], ALU.mult)\
                        .then_inc(multiplied, 1)
                    w_part(n + 2, q)
                    dve.wait_ge(hid_hi_done, n + 1)
                    dve.tensor_tensor(hid_lo[:, n, :], tmp[:, q, :], hid_hi[:, n, :].bitcast(F32),
                                      ALU.subtract).then_inc(hidden, 1)

                def down(j, q=None):
                    w_part(ups + j + 2, j if q is None else q)

                ups_then_downs(dve, up, down, lambda j: down(j, 0), downs - 2)
                for o in range(KD):
                    dve.wait_ge(banked, o + 1)
                    dve.scalar_tensor_tensor(m.resid[:, o, :], m.ps[:, o, :], scale, m.resid[:, o, :],
                                             ALU.mult, ALU.add)

            @block.gpsimd
            def _(pool):
                pool.wait_ge(chain, 1)
                for k in range(KD):
                    if k >= 2:
                        pool.wait_ge(x_done, k - 1)
                    pool.tensor_tensor(tmp[:, k % 2, :], m.resid[:, k, :], rstd, ALU.mult).then_inc(scaled, 1)

            @block.tensor
            def _(pe):
                def parts(out, w, q, x, start, stop):
                    pairs = ((w_hi, x[0]), (w_hi, x[1]), (w_lo, x[0]))
                    for a, (wp, xp) in enumerate(pairs):
                        ins = pe.matmul(out, wp[:, q, w], xp, start=start and a == 0, stop=stop and a == 2)
                    return ins

                for k in range(KD):
                    pe.wait_ge(squared, k + 1)
                    pe.matmul(m.ps[:, 7, :], m.ones, tmp[:, k % 2, :], start=(k == 0), stop=(k == KD - 1))\
                        .then_inc(summed, 1)

                def up(n, q=None):
                    q = n if q is None else q
                    pe.wait_ge(split, n + 1)
                    if not isinstance(n, int) or n >= 2:
                        pe.wait_ge(multiplied, n - 1)
                    for part, done in ((0, gated), (1, used)):
                        for k in range(KD):
                            if isinstance(n, int) and n == 0 and part == 0:
                                pe.wait_ge(x_done, k + 1)
                            at = k * 2 * P + part * P
                            ins = parts(m.ps[:, 2 * q + part, :], slice(at, at + P), q,
                                        (x_hi[:, k, :], x_lo[:, k, :]), k == 0, k == KD - 1)
                        ins.then_inc(done, 1)

                def down(j, q=None, final=False):
                    q = j if q is None else q
                    pe.wait_ge(split, ups + j + 1)
                    pe.wait_ge(hidden, 2 * j + 2)
                    if isinstance(j, int) and j == 0:
                        pe.wait_ge(multiplied, ups)
                    for o in range(KD):
                        for r in range(2):
                            k = 2 * j + r
                            ins = parts(m.ps[:, o, :], slice(r * D + o * P, r * D + (o + 1) * P), q % 2,
                                        (hid_hi[:, k, :], hid_lo[:, k, :]),
                                        isinstance(j, int) and j == 0 and r == 0, final and r == 1)
                        if final:
                            ins.then_inc(banked, 1)
                    if not final:
                        ins.then_inc(used, 1)
                ups_then_downs(pe, up, down, lambda j: down(j, 0, True))


def down_stage(nc, m, name, slabs, first, src, tiles, scale):
    with stage(nc, m, name) as (block, sem):
        landed = sem(SLOTS)
        used, chain = sem(2)

        @block.sync
        def _(sp):
            load_slabs(sp, m, slabs, first, tiles // 2, landed, used, 1)

        @block.tensor
        def _(pe):
            for i in range(tiles // 2):
                slab_landed(pe, landed, i)
                w = m.ring[:, i % SLOTS, :].rearrange("p (r n) -> p r n", r=2)
                for o in range(KD):
                    for r in range(2):
                        k = 2 * i + r
                        ins = pe.matmul(m.ps[:, o, :], w[:, r, tok(o)], src[:, k, :], start=(k == 0),
                                        stop=(k == tiles - 1))
                    if i == tiles // 2 - 1 and o < KD - 1:
                        ins.then_inc(used, 1)
                ins.then_inc(used, 1)

        @block.vector
        def _(dve):
            for o in range(KD):
                dve.wait_ge(used, tiles // 2 + o)
                dve.scalar_tensor_tensor(m.resid[:, o, :], m.ps[:, o, :], scale, m.resid[:, o, :],
                                         ALU.mult, ALU.add)



def constants():
    k, j = np.arange(P)[:, None], np.arange(P)[None, :]
    c = {
        "ident": k == j, "ones": np.ones((P, P)),
        "upto_f": k <= j, "after_f": k > j,
        "upto_b": k >= j, "after_b": k < j,
        "causal": np.where(j <= k, 0.0, MASKED),
    }
    pos = np.arange(T, dtype=np.float32)

    def rope(rot, starts, width):
        half = rot // 2
        turn = np.zeros((P, P), np.float32)
        cos, sin = np.ones((P, T), np.float32), np.zeros((P, T), np.float32)
        freq = np.float32(500000.0) ** (-np.arange(half, dtype=np.float32) / np.float32(half))
        ang = (pos[None, :] * freq[:, None]).astype(np.float32)
        for s in starts:
            for r in range(half):
                turn[s + half + r, s + r] = -1.0
                turn[s + r, s + half + r] = 1.0
            cos[s:s + half] = cos[s + half:s + rot] = np.cos(ang)
            sin[s:s + half] = sin[s + half:s + rot] = np.sin(ang)
        return turn, cos, sin

    c["turn_mla"], c["cos_mla"], c["sin_mla"] = rope(32, [64], 96)
    c["turn_nsa"], c["cos_nsa"], c["sin_nsa"] = rope(16, [0, 64], 128)
    q = np.arange(T)
    ncmp = T // 16 - 1
    end = np.arange(ncmp + 1) * 16 + 31
    cm = np.where(end[None, :] <= q[:, None], 0.0, MASKED).reshape(NT, P, ncmp + 1)
    c["cmp_mask"] = cm.transpose(1, 0, 2).reshape(P, -1)
    c["cmp_any"] = (q >= 31).astype(np.float32).reshape(NT, P).T
    c["slot"] = np.broadcast_to(np.arange(CAP), (P, CAP))
    levels = []
    for b in (1, 2, 4, 8, 16, 32, 64):
        low = (k // (2 * b) == j // (2 * b)) & (k % (2 * b) >= b) & (j % (2 * b) < b)
        levels.append((low, low.T))
    bytes_ = np.concatenate([mask for pair in levels for mask in pair], 1).astype(np.float32)
    return {n: np.ascontiguousarray(v, np.float32) for n, v in c.items()}, bytes_



def scalars_stage(nc, m, io):
    s = m.scal
    raw = cut(m.work, 0, NT, 4 * GH + 2 * SH)
    w = cut(m.work, 256, KD, 4 * GH + 2 * SH)
    bias, a_log = cut(m.work, 768, 64), cut(m.work, 832, 48)
    neg, tmp, cum = cut(m.work, 896, 48), cut(m.work, 960, NT, 48), cut(m.work, 1152, NT, 48)
    flat = {n: s[n].rearrange("p t d h -> p t (d h)") for n in ("g", "step", "from_start", "to_end", "total")}
    soft = raw[:, :, 16:64]
    with stage(nc, m, "scalars") as (block, sem):
        loaded, projected, act_in, act_out, chain, summed = sem(6)

        @block.sync
        def _(sp):
            sp.dma_start(w, io["w_scal"]).then_inc(loaded, 16)
            sp.dma_start(bias, io["scal_bias"].partition_broadcast(P)).then_inc(loaded, 16)
            sp.dma_start(a_log, io["scal_a_log"].partition_broadcast(P)).then_inc(loaded, 16)

        @block.tensor
        def _(pe):
            pe.wait_ge(loaded, 48)
            for t in range(NT):
                ins = product(pe, m.ps[:, t, 0:64], lambda k: m.xT[:, k, tok(t)], lambda k: w[:, k, :])
            ins.then_inc(projected, 1)
            pe.wait_ge(act_in, 3)
            for t in range(NT):
                for d, upto in ((0, m.upto_f), (1, m.upto_b)):
                    pe.matmul(m.ps[:, 4, t * 48 + 24 * d:t * 48 + 24 * d + 24], upto, s["g"][:, t, d, :],
                              start=True, stop=True)
                ins = pe.matmul(m.ps[:, 5, t * 48:t * 48 + 48], m.ones, flat["g"][:, t, :], start=True,
                                stop=True)
            ins.then_inc(summed, 1)

        @block.scalar
        def _(act):
            act.wait_ge(loaded, 48)
            act.activation(neg, a_log, ACT.Exp).then_inc(act_out, 1)
            act.wait_ge(act_in, 1)
            act.activation(tmp, tmp, ACT.Exp).then_inc(act_out, 1)
            act.activation(s["beta"].rearrange("p t d h -> p t (d h)"), raw[:, :, 0:16], ACT.Sigmoid)
            act.wait_ge(act_out, 2)
            act.activation(tmp, tmp, ACT.Ln, bias=1.0).then_inc(act_out, 1)
            act.wait_ge(act_in, 4)
            act.activation(flat["from_start"], cum, ACT.Exp).then_inc(act_out, 1)
            act.activation(flat["total"], m.ps[:, 5, 0:192].rearrange("p (t h) -> p t h", t=NT), ACT.Exp)
            act.activation(flat["to_end"], tmp, ACT.Exp).then_inc(act_out, 1)

        @block.vector
        def _(dve):
            link = Chain(dve, chain)
            dve.wait_ge(projected, 1)
            link(dve.tensor_tensor(raw, m.ps[:, 0:NT, 0:64], bias.unsqueeze(1).to_broadcast([P, NT, 64]),
                                   ALU.add))
            link(dve.tensor_scalar(tmp, soft, -1.0, None, ALU.mult))
            dve.tensor_tensor(tmp, tmp, soft, ALU.min).then_inc(act_in, 1)
            dve.wait_ge(act_in, 1)
            dve.wait_ge(act_out, 3)
            link(dve.scalar_tensor_tensor(flat["step"], soft, 0.0, tmp, ALU.max, ALU.add))
            link(dve.tensor_scalar(neg, neg, -1.0, None, ALU.mult))
            dve.tensor_tensor(flat["g"], flat["step"], neg.unsqueeze(1).to_broadcast([P, NT, 48]),
                              ALU.mult).then_inc(act_in, 2)
            dve.wait_ge(summed, 1)
            link(dve.tensor_copy(cum, m.ps[:, 4, 0:192].rearrange("p (t h) -> p t h", t=NT)))
            dve.tensor_tensor(tmp, m.ps[:, 5, 0:192].rearrange("p (t h) -> p t h", t=NT), cum,
                              ALU.subtract).then_inc(act_in, 1)
            dve.wait_ge(act_out, 5)
            dve.tensor_tensor(s["beta_decay"], s["beta"], s["from_start"][:, :, :, 0:GH], ALU.mult)
            dve.tensor_tensor(s["step_to_end"], s["step"][:, :, :, GH:], s["to_end"][:, :, :, GH:], ALU.mult)


TAPS = [GK // 2] + [j for j in range(GK) if j != GK // 2]


def convolve(dve, m, srcs, dsts, cols, projected, counts, steps, done):
    n = len(srcs)
    for i, tap in enumerate(TAPS):
        shift = tap - GK // 2
        for s, d, col, count in zip(srcs, dsts, cols, counts):
            if i == 0:
                dve.wait_ge(projected, count)
                ins = dve.tensor_scalar(d, s, col[:, tap:tap + 1], col[:, GK:GK + 1], ALU.mult, ALU.add)
            else:
                dve.wait_ge(steps, done + 1 - n)
                lo, hi = max(0, -shift), T - max(0, shift)
                ins = dve.scalar_tensor_tensor(d[:, lo:hi], s[:, lo + shift:hi + shift],
                                               col[:, tap:tap + 1], d[:, lo:hi], ALU.mult, ALU.add)
            ins.then_inc(steps, 1)
            done += 1
    return done


def mixer_tiles(nc, m, name, slabs, group, columns_in, n_conv, n_gate, c, gate, copies):
    tiles = n_conv + n_gate
    with stage(nc, m, name) as (block, sem):
        landed = sem(SLOTS)
        projected, steps, cols_in, gate_read, silued = sem(5)

        @block.sync
        def _(sp):
            sp.dma_start(m.cols, columns_in).then_inc(cols_in, 16)
            for i in range(tiles // 2):
                if i >= SLOTS:
                    sp.wait_ge(projected, 2 * (i - SLOTS + 1))
                sp.dma_start(m.ring[:, i % SLOTS, :], slabs[group * (tiles // 2) + i])\
                    .then_inc(landed[i % SLOTS], 16)

        @block.gpsimd
        def _(pool):
            for dst, src in copies:
                pool.tensor_copy(dst, src)

        @block.tensor
        def _(pe):
            for n in range(tiles):
                if n % 2 == 0:
                    slab_landed(pe, landed, n // 2)
                if n >= 8:
                    pe.wait_ge(steps, 14)
                product(pe, m.ps[:, n % 8, :], columns(m, n // 2, n % 2), lambda k: m.xT[:, k, :])\
                    .then_inc(projected, 1)

        @block.vector
        def _(dve):
            dve.wait_ge(cols_in, 16)
            done = 0
            for a in range(0, n_conv, 2):
                two = (a, a + 1)
                done = convolve(dve, m, [m.ps[:, n, :] for n in two], [c[:, n, :] for n in two],
                                [m.cols[:, 8 * n:8 * n + 8] for n in two], projected,
                                [n + 1 for n in two], steps, done)

        @block.scalar
        def _(act):
            for n in range(n_conv):
                act.wait_ge(steps, 14 * (n // 2 + 1))
                act.activation(c[:, n, :], c[:, n, :], ACT.Silu)
            for n in range(n_gate):
                act.wait_ge(projected, n_conv + n + 1)
                act.activation(gate[:, n, :], m.ps[:, (n_conv + n) % 8, :], ACT.Silu)


def gdn_pair(nc, m, io, hp):
    w = m.work
    c = cut(w, 0, 6, T)
    gate = cut(w, 6 * T, 2, T)
    at = [8 * T]

    def four(n=4):
        piece = cut(w, at[0], n, NT, P)
        at[0] += n * T
        return piece

    k_in, k_out, v_in = four(), four(), four()
    q_dec, dec, nT, x, xt = four(), four(), four(), four(), four()
    kb, gu = (cut(m.ring, a, 4, NT, P) for a in (0, 4 * T)) if False else (
        cut(m.ring_flat, 0, 4, NT, P), cut(m.ring_flat, 4 * T, 4, NT, P))
    xp, o = cut(m.ring_flat, 8 * T, 4, NT, P), cut(m.ring_flat, 12 * T, 4, NT, P)
    cur = m.cur
    chains = [(d, hh) for d in range(2) for hh in range(2)]
    upto, after = (m.upto_f, m.upto_b), (m.after_f, m.after_b)
    heads = bass.ds(2 * hp, 2)

    mixer_tiles(nc, m, "gdn_project", io["w_gdn"], hp, io["gdn_cols"][hp], 6, 2, c, gate,
                [(cur[n], m.scal[n][:, :, :, heads]) for n in ("beta", "beta_decay", "to_end", "total", "g")])

    with stage(nc, m, "gdn_lengths") as (block, sem):
        squared, summed, shifted, rooted, chain = sem(5)
        sq = x

        @block.scalar
        def _(act):
            for n in range(4):
                act.activation(sq[:, n, :, :], c[:, n, :].rearrange("p (t i) -> p t i", t=NT), ACT.Square)\
                    .then_inc(squared, 1)
            for n in range(4):
                act.wait_ge(shifted, n + 1)
                act.activation(sq[:, n, :, :], sq[:, n, :, :], ACT.Sqrt).then_inc(rooted, 1)

        @block.tensor
        def _(pe):
            for n in range(4):
                pe.wait_ge(squared, n + 1)
                pe.matmul(m.ps[:, n, :], m.ones, sq[:, n, :, :].rearrange("p t i -> p (t i)"), start=True,
                          stop=True).then_inc(summed, 1)

        @block.vector
        def _(dve):
            link = Chain(dve, chain)
            for n in range(4):
                dve.wait_ge(summed, n + 1)
                dve.tensor_scalar(sq[:, n, :, :].rearrange("p t i -> p (t i)"), m.ps[:, n, :], EPS, None,
                                  ALU.add).then_inc(shifted, 1)
            for n in range(4):
                r = sq[:, n, :, :].rearrange("p t i -> p (t i)")
                dve.wait_ge(rooted, n + 1)
                link(dve.reciprocal(r, r))
                dve.scalar_tensor_tensor(c[:, n, :], c[:, n, :], P ** -0.5 if n < 2 else 1.0, r, ALU.mult,
                                         ALU.mult)

    def wide(col):
        return col.unsqueeze(2).to_broadcast([P, NT, P])

    with stage(nc, m, "gdn_tokens") as (block, sem):
        turned, laid, rowed, chain, freed, decays, decayed = sem(7)

        @block.gpsimd
        def _(pool):
            for i, (d, hh) in enumerate(chains):
                pool.tensor_tensor(x[:, i, :, :], m.ident.unsqueeze(1).to_broadcast([P, NT, P]),
                                   wide(cur["beta"][:, :, d, hh]), ALU.mult).then_inc(laid, 1)
            for i, (d, hh) in enumerate(chains):
                pool.tensor_tensor(gu[:, i, :, :], upto[d].unsqueeze(1).to_broadcast([P, NT, P]),
                                   wide(cur["g"][:, :, d, hh]), ALU.mult).then_inc(laid, 1)

        @block.tensor
        def _(pe):
            for n in range(4):
                for t in range(NT):
                    ins = pe.transpose(m.ps[:, n, tok(t)], c[:, 2 + n, tok(t)], m.ident)
                ins.then_inc(turned, 1)
            for i in range(4):
                pe.wait_ge(laid, i + 1)
                pe.matmul(m.ps[:, 4 + i, :], m.ones, x[:, i, :, :].rearrange("p t i -> p (t i)"), start=True,
                          stop=True).then_inc(rowed, 1)
            for i, (d, hh) in enumerate(chains):
                flat = gu[:, i, :, :].rearrange("p t i -> p (t i)")
                pe.wait_ge(laid, 5 + i)
                pe.wait_ge(freed, 16)
                pe.matmul(m.ps[:, 2 * i, :], m.ones, flat, start=True, stop=True).then_inc(decays, 1)
                pe.matmul(m.ps[:, 2 * i + 1, :], after[d], flat, start=True, stop=True).then_inc(decays, 1)

        @block.vector
        def _(dve):
            by_chunk = lambda bank: m.ps[:, bank, :].rearrange("p (t i) -> p t i", t=NT)
            for i, (d, hh) in enumerate(chains):
                dve.wait_ge(turned, hh + 1)
                dve.tensor_tensor(k_in[:, i, :, :], by_chunk(hh), wide(cur["beta_decay"][:, :, d, hh]),
                                  ALU.mult).then_inc(freed, 1)
                dve.tensor_tensor(k_out[:, i, :, :], by_chunk(hh), wide(cur["to_end"][:, :, d, hh]),
                                  ALU.mult).then_inc(freed, 1)
                dve.wait_ge(turned, 2 + hh + 1)
                dve.tensor_tensor(v_in[:, i, :, :], by_chunk(2 + hh), wide(cur["beta"][:, :, d, hh]),
                                  ALU.mult).then_inc(freed, 1)
            for i, (d, hh) in enumerate(chains):
                dve.wait_ge(rowed, i + 1)
                dve.tensor_tensor(kb[:, i, :, :].rearrange("p t i -> p (t i)"), c[:, 2 + hh, :],
                                  m.ps[:, 4 + i, :], ALU.mult).then_inc(freed, 1)
            for i, (d, hh) in enumerate(chains):
                q = q_dec[:, i, :, :].rearrange("p t i -> p (t i)")
                dve.wait_ge(decayed, 2 * i + 1)
                dve.tensor_tensor(q, q, c[:, hh, :], ALU.mult)
                dve.wait_ge(decayed, 2 * i + 2)
                dve.tensor_tensor(dec[:, i, :, :], dec[:, i, :, :],
                                  upto[d].unsqueeze(1).to_broadcast([P, NT, P]), ALU.mult)

        @block.scalar
        def _(act):
            for i in range(4):
                for half, dst in ((0, q_dec), (1, dec)):
                    act.wait_ge(decays, 2 * i + half + 1)
                    act.activation(dst[:, i, :, :].rearrange("p t i -> p (t i)"), m.ps[:, 2 * i + half, :],
                                   ACT.Exp).then_inc(decayed, 1)

    with stage(nc, m, "gdn_scores") as (block, sem):
        scored, chain = sem(2)

        @block.tensor
        def _(pe):
            for i, (d, hh) in enumerate(chains):
                for bank, rhs in ((i, lambda t: kb[:, i, t, :]), (4 + i, lambda t: c[:, hh, tok(t)])):
                    for t in range(NT):
                        ins = pe.matmul(m.ps[:, bank, tok(t)], c[:, 2 + hh, tok(t)], rhs(t), start=True,
                                        stop=True)
                    ins.then_inc(scored, 1)

        @block.vector
        def _(dve):
            link = Chain(dve, chain)
            for i in range(4):
                d_ = dec[:, i, :, :].rearrange("p t i -> p (t i)")
                dve.wait_ge(scored, 2 * i + 1)
                dve.scalar_tensor_tensor(nT[:, i, :, :].rearrange("p t i -> p (t i)"), m.ps[:, i, :], -1.0,
                                         d_, ALU.mult, ALU.mult)
                dve.wait_ge(scored, 2 * i + 2)
                dve.tensor_tensor(d_, d_, m.ps[:, 4 + i, :], ALU.mult)

        @block.gpsimd
        def _(pool):
            for piece in (x, xt):
                for i in range(4):
                    pool.tensor_copy(piece[:, i, :, :], m.ident.unsqueeze(1).to_broadcast([P, NT, P]))

    with stage(nc, m, "gdn_inverse") as (block, sem):
        first, copied, filled, updated = sem(4)
        levels = 7

        @block.tensor
        def _(pe):
            for l in range(levels):
                for i in range(4):
                    if l:
                        pe.wait_ge(updated, 8 * (l - 1) + 2 * i + 2)
                    for t in range(NT):
                        ins = pe.matmul(m.ps[:, 2 * i, tok(t)], nT[:, i, t, :], x[:, i, t, :], start=True,
                                        stop=True)
                    ins.then_inc(first, 1)
                for i in range(4):
                    pe.wait_ge(copied, 4 * l + i + 1)
                    for t in range(NT):
                        ins = pe.matmul(m.ps[:, 2 * i + 1, tok(t)], xp[:, i, t, :], xt[:, i, t, :],
                                        start=True, stop=True)
                    if l < levels - 1:
                        for t in range(NT):
                            ins = pe.matmul(m.ps[:, 2 * i, tok(t)], xt[:, i, t, :], xp[:, i, t, :],
                                            start=True, stop=True)
                    ins.then_inc(filled, 1)

        @block.scalar
        def _(act):
            for l in range(levels):
                for i in range(4):
                    act.wait_ge(first, 4 * l + i + 1)
                    act.activation(xp[:, i, :, :].rearrange("p t i -> p (t i)"), m.ps[:, 2 * i, :], ACT.Copy)\
                        .then_inc(copied, 1)

        @block.vector
        def _(dve):
            for l in range(levels):
                for i, (d, hh) in enumerate(chains):
                    dve.wait_ge(filled, 4 * l + i + 1)
                    for mask, bank, dst in ((m.upper if d == 0 else m.lower, 2 * i + 1, xt),
                                            (m.lower if d == 0 else m.upper, 2 * i, x))[:1 if l == levels - 1 else 2]:
                        dve.copy_predicated(dst[:, i, :, :], mask[:, l, :].unsqueeze(1).to_broadcast([P, NT, P]),
                                            m.ps[:, bank, :].rearrange("p (t i) -> p t i", t=NT))\
                            .then_inc(updated, 1)

    minus_w = nT
    u = cut(w, 8 * T + 4 * 4 * 6 * P, 2, 4, P) if False else x[:, 0:2, :, :]
    state = x[:, 2:4, :, :]
    with stage(nc, m, "gdn_recurrence") as (block, sem):
        w_done, w_read, u_done, u_read, o_done, o_read, s_done, s_read = sem(8)
        ub, ob, sb = (4, 7), (5, 0), (6, 1)

        @block.tensor
        def _(pe):
            for i in range(4):
                for t in range(NT):
                    ins = pe.matmul(m.ps[:, i, tok(t)], k_in[:, i, t, :], xt[:, i, t, :], start=True, stop=True)
                ins.then_inc(w_done, 1)
            for s in range(NT):
                e = s % 2
                pe.wait_ge(w_read, 4)
                for i, (d, hh) in enumerate(chains):
                    t = s if d == 0 else NT - 1 - s
                    if s >= 2:
                        pe.wait_ge(u_read, s - 1)
                    ins = pe.matmul(m.ps[:, ub[e], tok(i)], xt[:, i, t, :], v_in[:, i, t, :], start=True,
                                    stop=(s == 0))
                    if s:
                        pe.wait_ge(s_read, 4 * (s - 1) + i + 1)
                        ins = pe.matmul(m.ps[:, ub[e], tok(i)], minus_w[:, i, t, :], state[:, 1 - e, i, :],
                                        start=False, stop=True)
                ins.then_inc(u_done, 1)
                pe.wait_ge(u_read, s + 1)
                if s < NT - 1:
                    for i, (d, hh) in enumerate(chains):
                        t = s if d == 0 else NT - 1 - s
                        if s >= 2:
                            pe.wait_ge(s_read, 4 * (s - 1))
                        ins = pe.matmul(m.ps[:, sb[e], tok(i)], k_out[:, i, t, :], u[:, e, i, :], start=True,
                                        stop=True)
                    ins.then_inc(s_done, 1)
                for i, (d, hh) in enumerate(chains):
                    t = s if d == 0 else NT - 1 - s
                    if s >= 2:
                        pe.wait_ge(o_read, 2 * (s - 1))
                    if s:
                        pe.matmul(m.ps[:, ob[e], tok(i)], state[:, 1 - e, i, :], q_dec[:, i, t, :], start=True,
                                  stop=False)
                    ins = pe.matmul(m.ps[:, ob[e], tok(i)], u[:, e, i, :], dec[:, i, t, :], start=(s == 0),
                                    stop=True)
                ins.then_inc(o_done, 1)

        @block.scalar
        def _(act):
            for i in range(4):
                act.wait_ge(w_done, i + 1)
                act.activation(minus_w[:, i, :, :].rearrange("p t i -> p (t i)"), m.ps[:, i, :], ACT.Copy,
                               scale=-1.0).then_inc(w_read, 1)
            for s in range(NT):
                e = s % 2
                act.wait_ge(u_done, s + 1)
                if s >= 2:
                    act.wait_ge(o_done, s - 1)
                act.activation(u[:, e, :, :].rearrange("p t i -> p (t i)"), m.ps[:, ub[e], :], ACT.Copy)\
                    .then_inc(u_read, 1)
                act.wait_ge(o_done, s + 1)
                for d in range(2):
                    t = s if d == 0 else NT - 1 - s
                    act.activation(o[:, 2 * d:2 * d + 2, t, :],
                                   m.ps[:, ob[e], 2 * d * P:(2 * d + 2) * P].rearrange("p (h i) -> p h i", h=2),
                                   ACT.Copy).then_inc(o_read, 1)

        @block.vector
        def _(dve):
            for s in range(NT - 1):
                e = s % 2
                dve.wait_ge(s_done, s + 1)
                if s >= 2:
                    dve.wait_ge(o_done, s)
                for i, (d, hh) in enumerate(chains):
                    t = s if d == 0 else NT - 1 - s
                    if s == 0:
                        ins = dve.tensor_copy(state[:, e, i, :], m.ps[:, sb[e], tok(i)])
                    else:
                        dve.wait_ge(s_read, 4 * (s - 1) + i + 1)
                        ins = dve.scalar_tensor_tensor(state[:, e, i, :], state[:, 1 - e, i, :],
                                                       cur["total"][:, t, d, hh:hh + 1], m.ps[:, sb[e], tok(i)],
                                                       ALU.mult, ALU.add)
                    ins.then_inc(s_read, 1)

    with stage(nc, m, "gdn_out") as (block, sem):
        added, squared, summed, shifted, rooted, chain = sem(6)
        both = [o[:, hh, :, :].rearrange("p t i -> p (t i)") for hh in range(2)]
        back = [o[:, 2 + hh, :, :].rearrange("p t i -> p (t i)") for hh in range(2)]

        @block.scalar
        def _(act):
            for hh in range(2):
                act.wait_ge(added, hh + 1)
                act.activation(back[hh], both[hh], ACT.Square).then_inc(squared, 1)
            for hh in range(2):
                act.wait_ge(shifted, hh + 1)
                act.activation(back[hh], back[hh], ACT.Sqrt).then_inc(rooted, 1)

        @block.tensor
        def _(pe):
            for hh in range(2):
                pe.wait_ge(squared, hh + 1)
                pe.matmul(m.ps[:, hh, :], m.ones, back[hh], start=True, stop=True).then_inc(summed, 1)

        @block.vector
        def _(dve):
            link = Chain(dve, chain)
            for hh in range(2):
                dve.tensor_tensor(both[hh], both[hh], back[hh], ALU.add).then_inc(added, 1)
            for hh in range(2):
                dve.wait_ge(summed, hh + 1)
                dve.tensor_scalar(back[hh], m.ps[:, hh, :], 1.0 / P, EPS, ALU.mult, ALU.add)\
                    .then_inc(shifted, 1)
            for hh in range(2):
                dve.wait_ge(rooted, hh + 1)
                link(dve.reciprocal(back[hh], back[hh]))
                link(dve.scalar_tensor_tensor(both[hh], both[hh], m.gains["gdn_norm"], back[hh], ALU.mult,
                                              ALU.mult))
                dve.tensor_tensor(m.mixed[:, 2 * hp + hh, :], both[hh], gate[:, hh, :], ALU.mult)


def ssd_group(nc, m, io, g):
    w = m.work
    c, gate = cut(w, 0, 6, T), cut(w, 6 * T, 4, T)
    at = [10 * T]

    def piece(*shape):
        p = cut(w, at[0], *shape)
        at[0] += int(np.prod(shape))
        return p

    b_tok = piece(NT, P)
    x_in, x_out = piece(2, NT, T), piece(2, NT, T)
    states = piece(2, NT, T)
    cb = piece(2, NT, P)
    y = piece(4, T)
    c_dec, score = cut(m.ring_flat, 0, 8, T), cut(m.ring_flat, 8 * T, 8, T)
    gu = cut(m.norm_tmp, 0, 2, NT, P)
    cur = m.cur_ssd
    upto, after = (m.upto_f, m.upto_b), (m.after_f, m.after_b)
    heads = bass.ds(8 * g, 8)
    in_g = bass.ds(8 + 8 * g, 8)

    mixer_tiles(nc, m, "ssd_project", io["w_ssd"], g, io["ssd_cols"][g], 6, 4, c, gate,
                [(cur[n], m.scal[n][:, :, :, heads if n == "step_to_end" else in_g]) for n in cur])

    def steps_of(d):
        return list(range(NT)) if d == 0 else list(range(NT))[::-1]

    with stage(nc, m, "ssd_tokens") as (block, sem):
        turned, crossed = sem(2)

        @block.tensor
        def _(pe):
            for bank, n in enumerate((0, 2, 3, 4, 5)):
                for t in range(NT):
                    ins = pe.transpose(m.ps[:, bank, tok(t)], c[:, n, tok(t)], m.ident)
                ins.then_inc(turned, 1)
            for t in range(NT):
                ins = pe.matmul(m.ps[:, 5, tok(t)], c[:, 0, tok(t)], c[:, 1, tok(t)], start=True, stop=True)
            ins.then_inc(crossed, 1)

        @block.scalar
        def _(act):
            act.wait_ge(turned, 1)
            act.activation(b_tok.rearrange("p t i -> p (t i)"), m.ps[:, 0, :], ACT.Copy)

        @block.vector
        def _(dve):
            for j in range(4):
                dve.wait_ge(turned, j + 2)
                src = m.ps[:, 1 + j, :].rearrange("p (t h i) -> p t h i", t=NT, h=2)
                for d in range(2):
                    for dst, col in ((x_in, "step"), (x_out, "step_to_end")):
                        by = cur[col][:, :, d, 2 * j:2 * j + 2].unsqueeze(3).to_broadcast([P, NT, 2, 64])
                        dve.tensor_tensor(dst[:, d, :, tok(j)].rearrange("p t (h i) -> p t h i", h=2), src,
                                          by, ALU.mult)
            dve.wait_ge(crossed, 1)
            for d in range(2):
                dve.tensor_tensor(cb[:, d, :, :], m.ps[:, 5, :].rearrange("p (t i) -> p t i", t=NT),
                                  upto[d].unsqueeze(1).to_broadcast([P, NT, P]), ALU.mult)

    with stage(nc, m, "ssd_states") as (block, sem):
        fresh, chain = sem(2)

        @block.tensor
        def _(pe):
            for s in range(NT - 1):
                for d in range(2):
                    t = steps_of(d)[s]
                    pe.matmul(m.ps[:, 2 * s + d, :], b_tok[:, t, :], x_out[:, d, t, :], start=True,
                              stop=True).then_inc(fresh, 1)

        @block.vector
        def _(dve):
            link = Chain(dve, chain)
            for s in range(NT - 1):
                for d in range(2):
                    t = steps_of(d)[s]
                    dve.wait_ge(fresh, 2 * s + d + 1)
                    new = states[:, d, s, :]
                    if s == 0:
                        link(dve.tensor_copy(new, m.ps[:, d, :]))
                        continue
                    by = cur["total"][:, t, d, :].unsqueeze(2).to_broadcast([P, 8, 64])
                    link(dve.tensor_tensor(new.rearrange("p (h i) -> p h i", h=8),
                                           states[:, d, s - 1, :].rearrange("p (h i) -> p h i", h=8), by,
                                           ALU.mult))
                    link(dve.tensor_tensor(new, new, m.ps[:, 2 * s + d, :], ALU.add))

    with stage(nc, m, "ssd_heads") as (block, sem):
        laid, decays, decayed, scored, y_done, chain, y_read = sem(7)
        combos = [(j, hh, d) for j in range(4) for hh in range(2) for d in range(2)]

        @block.gpsimd
        def _(pool):
            for n, (j, hh, d) in enumerate(combos):
                if n >= 2:
                    pool.wait_ge(decays, 2 * (n - 1))
                col = cur["g"][:, :, d, 2 * j + hh].unsqueeze(2).to_broadcast([P, NT, P])
                pool.tensor_tensor(gu[:, n % 2, :, :], upto[d].unsqueeze(1).to_broadcast([P, NT, P]), col,
                                   ALU.mult).then_inc(laid, 1)

        @block.tensor
        def _(pe):
            for j in range(5):
                for n in range(4 * j, 4 * j + 4) if j < 4 else ():
                    d = n % 2
                    flat = gu[:, n % 2, :, :].rearrange("p t i -> p (t i)")
                    pe.wait_ge(laid, n + 1)
                    if n >= 2:
                        pe.wait_ge(decayed, 2 * (n - 1))
                    pe.matmul(m.ps[:, 2 * (n % 2), :], m.ones, flat, start=True, stop=True).then_inc(decays, 1)
                    pe.matmul(m.ps[:, 2 * (n % 2) + 1, :], after[d], flat, start=True, stop=True)\
                        .then_inc(decays, 1)
                if j == 0:
                    continue
                i = j - 1
                if i >= 2:
                    pe.wait_ge(y_read, i - 1)
                for hh in range(2):
                    out = m.ps[hh * 64:hh * 64 + 64, 4 + i % 2, :]
                    pe.wait_ge(scored, 2 * (4 * i + 2 * hh + 2))
                    for t in range(NT):
                        terms = []
                        for d in range(2):
                            slot = (4 * i + 2 * hh + d) % 8
                            s = steps_of(d).index(t)
                            lanes = slice((2 * i + hh) * 64, (2 * i + hh) * 64 + 64)
                            terms.append((x_in[:, d, t, lanes], score[:, slot, tok(t)]))
                            if s:
                                terms.append((states[:, d, s - 1, lanes], c_dec[:, slot, tok(t)]))
                        for a, (lhs, rhs) in enumerate(terms):
                            ins = pe.matmul(out[:, tok(t)], lhs, rhs, start=(a == 0), stop=(a == len(terms) - 1))
                ins.then_inc(y_done, 1)

        @block.scalar
        def _(act):
            for n in range(16):
                if n >= 8:
                    act.wait_ge(y_done, n // 4 - 1)
                for half, dst in ((0, c_dec), (1, score)):
                    act.wait_ge(decays, 2 * n + half + 1)
                    act.activation(dst[:, n % 8, :], m.ps[:, 2 * (n % 2) + half, :], ACT.Exp)\
                        .then_inc(decayed, 1)

        @block.vector
        def _(dve):
            link = Chain(dve, chain)

            def out(i):
                dve.wait_ge(y_done, i + 1)
                ins = dve.scalar_tensor_tensor(y[:, i, :], c[:, 2 + i, :], m.cols[:, 48 + i:49 + i],
                                               m.ps[:, 4 + i % 2, :], ALU.mult, ALU.add)
                ins.then_inc(y_read, 1)
                dve.wait_ge(y_read, i + 1)
                dve.tensor_tensor(y[:, i, :], y[:, i, :], gate[:, i, :], ALU.mult)

            for n, (j, hh, d) in enumerate(combos):
                dve.wait_ge(decayed, 2 * n + 1)
                dve.tensor_tensor(c_dec[:, n % 8, :], c_dec[:, n % 8, :], c[:, 1, :], ALU.mult)\
                    .then_inc(scored, 1)
                dve.wait_ge(decayed, 2 * n + 2)
                dve.tensor_tensor(score[:, n % 8, :], score[:, n % 8, :],
                                  cb[:, d, :, :].rearrange("p t i -> p (t i)"), ALU.mult).then_inc(scored, 1)
                if n % 4 == 3 and j:
                    out(j - 1)
            out(3)

    with stage(nc, m, "ssd_norm") as (block, sem):
        squared, summed, mean, rooted, chain = sem(5)
        sq = cut(m.ring_flat, 0, 4, T)
        rstd = cut(m.norm_tmp, 0, T)

        @block.scalar
        def _(act):
            for i in range(4):
                act.activation(sq[:, i, :], y[:, i, :], ACT.Square).then_inc(squared, 1)
            act.wait_ge(mean, 1)
            act.activation(rstd, rstd, ACT.Sqrt).then_inc(rooted, 1)

        @block.tensor
        def _(pe):
            for i in range(4):
                pe.wait_ge(squared, i + 1)
                ins = pe.matmul(m.ps[:, 0, :], m.ones, sq[:, i, :], start=(i == 0), stop=(i == 3))
            ins.then_inc(summed, 1)

        @block.vector
        def _(dve):
            link = Chain(dve, chain)
            dve.wait_ge(summed, 1)
            dve.tensor_scalar(rstd, m.ps[:, 0, :], 1.0 / (4 * P), EPS, ALU.mult, ALU.add).then_inc(mean, 1)
            dve.wait_ge(rooted, 1)
            link(dve.reciprocal(rstd, rstd))
            for i in range(4):
                dve.scalar_tensor_tensor(m.mixed[:, 8 + 4 * g + i, :], y[:, i, :], m.cols[:, 52 + i:53 + i],
                                         rstd, ALU.mult, ALU.mult)



def experts(nc, m, io):
    w = m.work
    pick, weighed = cut(w, 0, NT, NE * CAP), cut(w, 4096, NT, NE * CAP)
    x_tok, put = cut(w, 8192, NT, D), cut(w, 12288, NE // 2, T)
    small = 16384
    affinity, slot_of = cut(w, small, NT, NE), cut(w, small + 64, NT, NE)
    router = cut(w, small + 128, KD, NE)
    peak, total = cut(w, small + 256, NT), cut(w, small + 260, NT)
    top = cut(w, small + 264, 8)[0:NE]
    rest, chosen, ones_row, count = (cut(w, small + 288 + T * i, T)[0:NE] for i in range(4))
    xs = m.mixed[:, :, :].rearrange("p a b -> p (a b)").rearrange("p (k s) -> p k s", k=KD)
    by_expert = lambda a: a.unsqueeze(2).to_broadcast([P, NT, NE])

    with stage(nc, m, "route") as (block, sem):
        loaded, logits, exped, shifted, normed, turned, placed, back, chain = sem(9)

        @block.sync
        def _(sp):
            sp.dma_start(router, io["w_router"]).then_inc(loaded, 16)

        @block.tensor
        def _(pe):
            pe.wait_ge(loaded, 16)
            for t in range(NT):
                ins = product(pe, m.ps[:, 0, t * NE:(t + 1) * NE], lambda k: m.xT[:, k, tok(t)],
                              lambda k: router[:, k, :])
            ins.then_inc(logits, 1)
            pe.wait_ge(normed, 1)
            for t in range(NT):
                ins = pe.transpose(m.ps[0:NE, 1, tok(t)], affinity[:, t, :], m.ident)
            ins.then_inc(turned, 1)
            pe.wait_ge(placed, 1)
            for t in range(NT):
                ins = pe.transpose(m.ps[:, 2, t * NE:(t + 1) * NE], chosen[:, tok(t)], m.ident[0:NE, 0:NE])
            ins.then_inc(back, 1)

        @block.scalar
        def _(act):
            act.wait_ge(shifted, 1)
            act.activation(affinity, affinity, ACT.Exp).then_inc(exped, 1)

        @block.vector
        def _(dve):
            link = Chain(dve, chain)
            link(dve.memset(ones_row, 1.0))
            dve.wait_ge(logits, 1)
            ps = m.ps[:, 0, 0:NT * NE].rearrange("p (t e) -> p t e", t=NT)
            link(dve.tensor_reduce(peak, ps, AX, ALU.max))
            dve.tensor_tensor(affinity, ps, by_expert(peak), ALU.subtract).then_inc(shifted, 1)
            dve.wait_ge(exped, 1)
            link(dve.tensor_reduce(total, affinity, AX, ALU.add))
            link(dve.reciprocal(total, total))
            dve.tensor_tensor(affinity, affinity, by_expert(total), ALU.mult).then_inc(normed, 1)
            dve.wait_ge(turned, 1)
            link(dve.tensor_copy(rest, m.ps[0:NE, 1, :]))
            for _ in range(CAP // 8):
                link(dve.max(top, rest))
                link(dve.match_replace(rest, top, rest, -1.0))
            link(dve.tensor_scalar(chosen, rest, 0.0, None, ALU.is_lt))
            link(dve.tensor_tensor_scan(count, ones_row, chosen, 0.0, ALU.mult, ALU.add))
            link(dve.tensor_tensor(count, count, chosen, ALU.mult))
            dve.tensor_scalar(chosen, count, -1.0, None, ALU.add).then_inc(placed, 1)
            dve.wait_ge(back, 1)
            dve.tensor_copy(slot_of, m.ps[:, 2, 0:NT * NE].rearrange("p (t e) -> p t e", t=NT))

    with stage(nc, m, "pick") as (block, sem):
        turned, copied, picked, weighted, gathered, put_done, freed, put_read = sem(8)

        @block.vector
        def _(dve):
            for t in range(NT):
                dve.tensor_tensor(pick[:, t, :].rearrange("p (e s) -> p e s", e=NE),
                                  m.slot.unsqueeze(1).to_broadcast([P, NE, CAP]),
                                  slot_of[:, t, :].unsqueeze(2).to_broadcast([P, NE, CAP]),
                                  ALU.is_equal).then_inc(picked, 1)
            for n in range(16):
                dve.wait_ge(gathered, n + 1)
                k, half = divmod(n, 2)
                if n % 2 == 0:
                    dve.tensor_copy(xs[:, k, half * T:(half + 1) * T], m.ps[:, 4 + n % 4, :])\
                        .then_inc(freed, 1)
            for pair in range(0, NE // 2, 2):
                dve.wait_ge(put_done, pair + 1)
                dve.tensor_copy(put[:, pair, :], m.ps[:, pair % 4, :]).then_inc(put_read, 1)

        @block.gpsimd
        def _(pool):
            for t in range(NT):
                pool.wait_ge(picked, t + 1)
                pool.tensor_tensor(weighed[:, t, :].rearrange("p (e s) -> p e s", e=NE),
                                   pick[:, t, :].rearrange("p (e s) -> p e s", e=NE),
                                   affinity[:, t, :].unsqueeze(2).to_broadcast([P, NE, CAP]),
                                   ALU.mult).then_inc(weighted, 1)

        @block.scalar
        def _(act):
            for n in range(8):
                act.wait_ge(turned, n + 1)
                t, half = divmod(n, 2)
                act.activation(x_tok[:, t, half * T:(half + 1) * T], m.ps[:, n % 4, :], ACT.Copy)\
                    .then_inc(copied, 1)
            for n in range(1, 16, 2):
                act.wait_ge(gathered, n + 1)
                k, half = divmod(n, 2)
                act.activation(xs[:, k, half * T:(half + 1) * T], m.ps[:, 4 + n % 4, :], ACT.Copy)\
                    .then_inc(copied, 1)
            for pair in range(1, NE // 2, 2):
                act.wait_ge(put_done, pair + 1)
                act.activation(put[:, pair, :], m.ps[:, pair % 4, :], ACT.Copy).then_inc(copied, 1)

        @block.tensor
        def _(pe):
            for n in range(8):
                if n >= 4:
                    pe.wait_ge(copied, n - 3)
                t, half = divmod(n, 2)
                for k in range(4):
                    ins = pe.transpose(m.ps[:, n % 4, tok(k)], m.xT[:, 4 * half + k, tok(t)], m.ident)
                ins.then_inc(turned, 1)
            pe.wait_ge(copied, 8)
            pe.wait_ge(picked, NT)
            for n in range(16):
                k, half = divmod(n, 2)
                if n >= 4:
                    pe.wait_ge(freed if n % 2 == 0 else copied, (n - 4) // 2 + 1 + (8 if n % 2 else 0))
                product(pe, m.ps[:, 4 + n % 4, :], lambda t: x_tok[:, t, tok(k)],
                        lambda t: pick[:, t, half * T:(half + 1) * T], NT).then_inc(gathered, 1)
            pe.wait_ge(weighted, NT)
            for pair in range(NE // 2):
                if pair >= 4:
                    pe.wait_ge(put_read if pair % 2 == 0 else copied,
                               (pair - 4) // 2 + 1 + (16 if pair % 2 else 0))
                for t in range(NT):
                    ins = pe.transpose(m.ps[:, pair % 4, tok(t)], weighed[:, t, tok(pair)], m.ident)
                ins.then_inc(put_done, 1)

    hid, silu = cut(w, 16384, 2, 4 * CAP), cut(w, 16384 + 512, 2, 4 * CAP)
    y = cut(w, 0, NE // 2, D)
    with stage(nc, m, "experts") as (block, sem):
        landed = sem(SLOTS)
        slabs_done, silued, hidden, y_read = sem(4)

        def repeat(eng, body):
            body(0, True)
            with eng.Fori(1, NE // 2) as i:
                body(i, False)

        @block.sync
        def _(sp):
            def body(i, first):
                for s in range(12):
                    if not first or s >= SLOTS:
                        sp.wait_ge(slabs_done, 12 * i + s - SLOTS + 1)
                    sp.dma_start(m.ring[:, s % SLOTS, :], io["w_experts"][12 * i + s])\
                        .then_inc(landed[s % SLOTS], 16)
            repeat(sp, body)

        @block.tensor
        def _(pe):
            def slab(i, s):
                pe.wait_ge(landed[s % SLOTS], 48 * i + 16 * (s // SLOTS + 1))

            def body(i, first):
                for e in range(2):
                    if not first:
                        pe.wait_ge(hidden, 2 * i - 1 + e)
                    for s in range(4):
                        slab(i, 4 * e + s)
                        for half in range(2):
                            f = 2 * (s % 2) + half
                            ins = product(pe, m.ps[:, 2 * e + s // 2, f * CAP:(f + 1) * CAP],
                                          columns(m, 4 * e + s, half),
                                          lambda k: xs[:, k, bass.ds((2 * i + e) * CAP, CAP)])
                        ins.then_inc(slabs_done, 1)
                if not first:
                    pe.wait_ge(y_read, 2 * i)
                for e in range(2):
                    pe.wait_ge(hidden, 2 * i + e + 1)
                    for s in range(2):
                        slab(i, 8 + 2 * e + s)
                        rows = m.ring[:, (8 + 2 * e + s) % SLOTS, :].rearrange("p (r n) -> p r n", r=2)
                        for r in range(2):
                            f = 2 * s + r
                            for half in range(2):
                                ins = pe.matmul(m.ps[e * CAP:(e + 1) * CAP, 4 + half, :],
                                                hid[:, e, f * CAP:(f + 1) * CAP],
                                                rows[:, r, half * T:(half + 1) * T], start=(f == 0),
                                                stop=(f == 3))
                        ins.then_inc(slabs_done, 1)
            repeat(pe, body)

        @block.scalar
        def _(act):
            def body(i, first):
                for e in range(2):
                    act.wait_ge(slabs_done, 12 * i + 4 * e + 2)
                    act.activation(silu[:, e, :], m.ps[:, 2 * e, 0:4 * CAP], ACT.Silu).then_inc(silued, 1)
                act.wait_ge(slabs_done, 12 * i + 12)
                for half in range(2):
                    act.activation(y[:, i, half * T:(half + 1) * T], m.ps[:, 4 + half, :], ACT.Copy)\
                        .then_inc(y_read, 1)
            repeat(act, body)

        @block.vector
        def _(dve):
            def body(i, first):
                for e in range(2):
                    dve.wait_ge(slabs_done, 12 * i + 4 * e + 4)
                    dve.wait_ge(silued, 2 * i + e + 1)
                    dve.tensor_tensor(hid[:, e, :], silu[:, e, :], m.ps[:, 2 * e + 1, 0:4 * CAP], ALU.mult)\
                        .then_inc(hidden, 1)
            repeat(dve, body)

    with stage(nc, m, "scatter") as (block, sem):
        done, chain = sem(2)

        @block.tensor
        def _(pe):
            for k in range(KD):
                product(pe, m.ps[:, k, :], lambda pair: y[:, pair, tok(k)], lambda pair: put[:, pair, :],
                        NE // 2).then_inc(done, 1)

        @block.vector
        def _(dve):
            for k in range(KD):
                dve.wait_ge(done, k + 1)
                dve.tensor_tensor(m.resid[:, k, :], m.ps[:, k, :], m.resid[:, k, :], ALU.add)



MLA_H, NSA_H, SB_H = 6, 6, 4
HD = 64
NOPE, ROPE = 64, 32
QK = NOPE + ROPE
NCMP = T // 16 - 1
CMP_LEN = 32
GATES = 3 * NSA_H
C_Q, C_KV, K_PE, N_Q, N_KC, N_KS, N_KW, N_VC, S_Q, S_K, TILES2 = 0, 2, 3, 4, 7, 8, 9, 10, 11, 13, 15
V_SEL, V_WIN, V_SB = 0, 2 * HD, 4 * HD


def mixer2_memory(m):
    w, o = m.work, m.mixed[:, :, :].rearrange("p a b -> p (a b)")
    b = Buffers()
    b.f = cut(w, 0, TILES2, T)
    b.v = cut(w, 7680, NT, T)
    b.swapped = cut(w, 9728, 2, T)
    b.prob, b.prob_t = cut(w, 10752, 2, T), cut(w, 11776, 2, T)
    b.q, b.k, b.v_mla = cut(w, 12800, MLA_H, T), cut(w, 15872, MLA_H, T), cut(w, 18944, NT, MLA_H * HD)
    b.gates = cut(w, 20480, NT, GATES)
    b.stats = cut(w, 20592, 4, 8)
    b.kc, b.vc = cut(w, 20640, 2, 32), cut(w, 20704, 2, HD)
    b.hidden, b.tmp = cut(w, 20832, 4 * NCMP), cut(w, 20960, 4 * NCMP)
    b.sb = [cut(w, 12800 + i * NT * T, NT, T) for i in range(3)]
    b.o = cut(o, 0, NT, D)
    b.blocks = cut(o, 4096, 2, CMP_LEN, NCMP)
    b.turn_tmp = cut(o, 6144, 2, T)
    b.col = m.col
    return b


LAYER_COLS = (("ffn1", KD), ("mix", KD), ("ffn2", KD), ("q_norm", 2), ("kv_norm", 1), ("pos_k", CMP_LEN),
              ("pos_v", CMP_LEN), ("w2_k", HD), ("w2_v", HD))
LAYER_WIDTH = sum(w for _, w in LAYER_COLS)


def project2(nc, m, b, slabs):
    with stage(nc, m, "mix_project") as (block, sem):
        landed = sem(SLOTS)
        projected, read_v, read_a, chain = sem(4)

        @block.sync
        def _(sp):
            for i in range(10):
                if i >= SLOTS:
                    sp.wait_ge(projected, 2 * (i - SLOTS + 1))
                sp.dma_start(m.ring[:, i % SLOTS, :], slabs[i]).then_inc(landed[i % SLOTS], 16)

        @block.tensor
        def _(pe):
            for n in range(TILES2 + 1):
                if n % 2 == 0:
                    slab_landed(pe, landed, n // 2)
                if n >= 4:
                    pe.wait_ge(read_a if n % 2 else read_v, (n - 4) // 2 + 1)
                if n < TILES2:
                    ins = product(pe, m.ps[:, n % 4, :], columns(m, n // 2, n % 2), lambda k: m.xT[:, k, :])
                else:
                    w = columns(m, n // 2, 1, GATES)
                    for t in range(NT):
                        ins = product(pe, m.ps[:, 3, t * GATES:(t + 1) * GATES], lambda k: m.xT[:, k, tok(t)], w)
                ins.then_inc(projected, 1)
            for i in (8, 9):
                slab_landed(pe, landed, i)
                w = m.ring[:, i % SLOTS, :].rearrange("p (k n) -> p k n", k=4)
                for t in range(NT):
                    for k in range(4):
                        ins = pe.matmul(m.ps[:, 4 + t, :], m.xT[:, 4 * (i - 8) + k, tok(t)], w[:, k, :],
                                        start=(i == 8 and k == 0), stop=(i == 9 and k == 3))
                    if i == 9:
                        ins.then_inc(projected, 1)

        @block.vector
        def _(dve):
            for n in range(0, TILES2, 2):
                dve.wait_ge(projected, n + 1)
                dve.tensor_copy(b.f[:, n, :], m.ps[:, n % 4, :]).then_inc(read_v, 1)
            dve.wait_ge(projected, TILES2 + 1)
            dve.tensor_tensor(b.gates, m.ps[:, 3, 0:NT * GATES].rearrange("p (t n) -> p t n", t=NT),
                              m.gate_bias.unsqueeze(1).to_broadcast([P, NT, GATES]), ALU.add)\
                .then_inc(read_v, 1)
            for t in (0, 2):
                dve.wait_ge(projected, TILES2 + 2 + t)
                dve.tensor_copy(b.v[:, t, :], m.ps[:, 4 + t, :])

        @block.scalar
        def _(act):
            for n in range(1, TILES2, 2):
                act.wait_ge(projected, n + 1)
                act.activation(b.f[:, n, :], m.ps[:, n % 4, :], ACT.Copy).then_inc(read_a, 1)
            for t in (1, 3):
                act.wait_ge(projected, TILES2 + 2 + t)
                act.activation(b.v[:, t, :], m.ps[:, 4 + t, :], ACT.Copy)
            act.wait_ge(read_v, 9)
            act.activation(b.gates, b.gates, ACT.Sigmoid)


def rope_stage(nc, m, name, tiles, tmp, after=None):
    with stage(nc, m, name) as (block, sem):
        turned, read, scaled, chain, done, swapped = sem(6)

        @block.tensor
        def _(pe):
            for n, (x, turn, _, _) in enumerate(tiles):
                if n >= 4:
                    pe.wait_ge(read, n - 3)
                rows = x.shape[0]
                pe.matmul(m.ps[0:rows, n % 4, :], turn[0:rows, 0:rows], x, start=True, stop=True)\
                    .then_inc(turned, 1)

        @block.gpsimd
        def _(pool):
            for n, (x, _, cos, _) in enumerate(tiles):
                pool.wait_ge(turned, n + 1)
                pool.tensor_tensor(x, x, cos[0:x.shape[0]], ALU.mult).then_inc(scaled, 1)

        @block.vector
        def _(dve):
            for n, (x, _, _, sin) in enumerate(tiles):
                rows = x.shape[0]
                dve.wait_ge(turned, n + 1)
                dve.tensor_tensor(tmp[0:rows, n % 2, :], m.ps[0:rows, n % 4, :], sin[0:rows], ALU.mult)\
                    .then_inc(read, 1)
                dve.wait_ge(read, n + 1)
                dve.wait_ge(scaled, n + 1)
                dve.tensor_tensor(x, x, tmp[0:rows, n % 2, :], ALU.add).then_inc(done, 1)

        if after:
            @block.sync
            def _(sp):
                sp.wait_ge(done, len(tiles))
                for dst, src in after:
                    sp.dma_start(dst, src).then_inc(swapped, 16)
                sp.wait_ge(swapped, 16 * len(after))


def mla_project(nc, m, b, slabs):
    with stage(nc, m, "mla_project") as (block, sem):
        landed, projected, read_v, read_a = sem(4)
        w_q = cut(m.ring_flat, 0, 2, MLA_H * QK)
        w_kv = cut(m.ring_flat, 2 * MLA_H * QK, MLA_H, NOPE + HD)

        @block.sync
        def _(sp):
            sp.dma_start(m.ring[:, 0, :], slabs[10]).then_inc(landed, 16)

        @block.tensor
        def _(pe):
            pe.wait_ge(landed, 16)
            for n in range(2 * MLA_H):
                h = n // 2
                if n >= 4:
                    pe.wait_ge(read_a if n % 2 else read_v, (n - 4) // 2 + 1)
                if n % 2 == 0:
                    ins = product(pe, m.ps[0:QK, n % 4, :], lambda k: w_q[:, k, h * QK:(h + 1) * QK],
                                  lambda k: b.f[:, C_Q + k, :], 2)
                else:
                    ins = pe.matmul(m.ps[0:NOPE, n % 4, :], w_kv[:, h, 0:NOPE], b.f[:, C_KV, :], start=True,
                                    stop=True)
                ins.then_inc(projected, 1)
            for t in range(NT):
                pe.matmul(m.ps[:, 4 + t, 0:MLA_H * HD].rearrange("p (h n) -> p h n", h=MLA_H),
                          b.f[:, C_KV, tok(t)], w_kv[:, :, NOPE:], start=True, stop=True)\
                    .then_inc(projected, 1)

        @block.vector
        def _(dve):
            for h in range(MLA_H):
                dve.wait_ge(projected, 2 * h + 1)
                dve.tensor_copy(b.q[0:QK, h, :], m.ps[0:QK, 2 * h % 4, :]).then_inc(read_v, 1)
            for t in range(NT):
                dve.wait_ge(projected, 2 * MLA_H + t + 1)
                dve.tensor_copy(b.v_mla[:, t, :], m.ps[:, 4 + t, 0:MLA_H * HD])

        @block.scalar
        def _(act):
            for h in range(MLA_H):
                act.wait_ge(projected, 2 * h + 2)
                act.activation(b.k[0:NOPE, h, :], m.ps[0:NOPE, (2 * h + 1) % 4, :], ACT.Copy).then_inc(read_a, 1)

        @block.gpsimd
        def _(pool):
            for h in range(MLA_H):
                pool.tensor_copy(b.k[NOPE:QK, h, :], b.f[NOPE:QK, K_PE, :])


def compress(nc, m, b, slabs):
    with stage(nc, m, "compress") as (block, sem):
        landed = sem(4)
        blocks_in, hidden_done, copied, cubed, tanhed, ready, small_done, chain = sem(8)

        @block.sync
        def _(sp):
            for i in range(4):
                sp.dma_start(m.ring[:, i, :], slabs[11 + i]).then_inc(landed[i], 16)

        @block.vector
        def _(dve):
            link = Chain(dve, chain)
            for n, (tile, pos) in enumerate(((N_KC, "pos_k"), (N_VC, "pos_v"))):
                x = b.f[:, tile, :].rearrange("p (n l) -> p l n", l=16)
                for half in range(2):
                    dve.tensor_tensor(b.blocks[:, n, 16 * half:16 * half + 16, :], x[:, :, half:half + NCMP],
                                      b.col[pos][:, 16 * half:16 * half + 16].unsqueeze(2)
                                      .to_broadcast([P, 16, NCMP]), ALU.add).then_inc(blocks_in, 1)
            dve.wait_ge(hidden_done, 4)
            hid, tmp = b.hidden, b.tmp
            link(dve.tensor_copy(hid.rearrange("p (n c) -> p n c", n=4), m.ps[:, 0:4, 0:NCMP]))
            link(dve.tensor_tensor(tmp, hid, hid, ALU.mult))
            link(dve.tensor_scalar(tmp, tmp, 0.044715, 1.0, ALU.mult, ALU.add))
            dve.tensor_tensor(tmp, tmp, hid, ALU.mult).then_inc(cubed, 1)
            dve.wait_ge(tanhed, 1)
            link(dve.tensor_scalar(tmp, tmp, 0.5, 0.5, ALU.mult, ALU.add))
            dve.tensor_tensor(hid, hid, tmp, ALU.mult).then_inc(ready, 1)
            dve.wait_ge(small_done, 1)
            dve.tensor_copy(b.kc[:, :, 0:NCMP], m.ps[:, 4, 0:2 * NCMP].rearrange("p (g c) -> p g c", g=2))
            dve.tensor_copy(b.vc[0:NCMP, :, :], m.ps[0:NCMP, 5, 0:2 * HD].rearrange("p (g d) -> p g d", g=2))

        @block.scalar
        def _(act):
            act.wait_ge(cubed, 1)
            act.activation(b.tmp, b.tmp, ACT.Tanh, scale=0.7978845608028654).then_inc(tanhed, 1)

        @block.tensor
        def _(pe):
            for n in range(2):
                for half in range(2):
                    pe.wait_ge(landed[2 * n + half], 16)
                pe.wait_ge(blocks_in, 2 * n + 2)
                for g in range(2):
                    rows = slice(g * HD, (g + 1) * HD)
                    for l in range(CMP_LEN):
                        w = m.ring[rows, 2 * n + l // 16, (l % 16) * P:(l % 16 + 1) * P]
                        ins = pe.matmul(m.ps[:, 2 * n + g, 0:NCMP], w, b.blocks[rows, n, l, :],
                                        start=(l == 0), stop=(l == CMP_LEN - 1))
                    ins.then_inc(hidden_done, 1)
            pe.wait_ge(ready, 1)
            hid = b.hidden.rearrange("p (n c) -> p n c", n=4)
            for g in range(2):
                for base in (0, HD):
                    pe.matmul(m.ps[base:base + HD, 4, g * NCMP:(g + 1) * NCMP], b.col["w2_k"], hid[:, g, :],
                              start=True, stop=True)
                ins = pe.matmul(m.ps[0:NCMP, 5, g * HD:(g + 1) * HD], hid[:, 2 + g, :], b.col["w2_v"],
                                start=True, stop=True)
            ins.then_inc(small_done, 1)


def attention_items(m, b):
    items = []
    for h in range(MLA_H):
        for i in range(NT):
            items.append(dict(
                q=b.q[0:QK, h, tok(i)], k=b.k[0:QK, h, 0:(i + 1) * P], width=(i + 1) * P,
                v=[b.v_mla[:, t, h * HD:(h + 1) * HD] for t in range(i + 1)], mask=(i * P, m.causal),
                scale=QK ** -0.5, out=b.o[:, i, h * HD:(h + 1) * HD], gate=None, first=True))
    for h in range(NSA_H):
        g, rows = h // 3, slice(h % 2 * HD, h % 2 * HD + HD)
        for i in range(NT):
            q = b.f[rows, N_Q + h // 2, tok(i)]
            out = b.o[:, i, (MLA_H + h) * HD:(MLA_H + h + 1) * HD]
            gate = lambda n: b.gates[:, i, 3 * h + n:3 * h + n + 1]
            items.append(dict(
                q=q, k=b.kc[rows, g, 0:NCMP], width=NCMP, v=[b.vc[0:NCMP, g, :]],
                mask=(0, m.cmp_mask.rearrange("p (t c) -> p t c", t=NT)[:, i, 0:NCMP]), scale=HD ** -0.5,
                out=out, gate=gate(0), first=True, any=m.cmp_any[:, i:i + 1]))
            for n, tile, v in ((1, N_KS, V_SEL), (2, N_KW, V_WIN)):
                src = b.f[rows, tile, :] if g == h % 2 else b.swapped[rows, tile - N_KS, :]
                items.append(dict(
                    q=q, k=src[:, 0:(i + 1) * P], width=(i + 1) * P,
                    v=[b.v[:, t, v + g * HD:v + (g + 1) * HD] for t in range(i + 1)], mask=(i * P, m.causal),
                    scale=HD ** -0.5, out=out, gate=gate(n), first=False))
    return items


def attention(nc, m, b):
    items = attention_items(m, b)
    with stage(nc, m, "attention") as (block, sem):
        scored, maxed, exped, turned, copied, summed, out_done, chain = sem(8)
        n_items = len(items)

        @block.tensor
        def _(pe):
            for step in range(n_items + 2):
                n = step
                if n < n_items:
                    it = items[n]
                    if n >= 2:
                        pe.wait_ge(exped, n - 1)
                    pe.matmul(m.ps[:, n % 2, 0:it["width"]], it["q"], it["k"], start=True, stop=True)\
                        .then_inc(scored, 1)
                n = step - 1
                if 0 <= n < n_items:
                    it = items[n]
                    pe.wait_ge(exped, n + 1)
                    if n >= 2:
                        pe.wait_ge(copied, n - 1)
                    for t in range(len(it["v"])):
                        keys = min(P, it["width"] - t * P)
                        ins = pe.transpose(m.ps[0:keys, 2 + n % 2, tok(t)],
                                           b.prob[:, n % 2, t * P:t * P + keys], m.ident)
                    ins.then_inc(turned, 1)
                n = step - 2
                if 0 <= n < n_items:
                    it = items[n]
                    pe.wait_ge(copied, n + 1)
                    if n >= 2:
                        pe.wait_ge(out_done, n - 1)
                    for t, v in enumerate(it["v"]):
                        keys = min(P, it["width"] - t * P)
                        ins = pe.matmul(m.ps[:, 4 + n % 2, 0:HD], b.prob_t[0:keys, n % 2, tok(t)], v,
                                        start=(t == 0), stop=(t == len(it["v"]) - 1))
                    ins.then_inc(summed, 1)

        @block.scalar
        def _(act):
            for step in range(n_items + 1):
                n = step
                if n < n_items:
                    it = items[n]
                    act.wait_ge(maxed, n + 1)
                    if n >= 2:
                        act.wait_ge(turned, n - 1)
                    if n >= 4:
                        act.wait_ge(out_done, n - 3)
                    act.activation(b.prob[:, n % 2, 0:it["width"]], m.ps[:, n % 2, 0:it["width"]], ACT.Exp,
                                   bias=b.stats[:, n % 4, 0:1], scale=it["scale"],
                                   accum_out=b.stats[:, n % 4, 1:2]).then_inc(exped, 1)
                n = step - 1
                if 0 <= n < n_items:
                    it = items[n]
                    act.wait_ge(turned, n + 1)
                    if n >= 2:
                        act.wait_ge(summed, n - 1)
                    rows, width = min(P, it["width"]), P * len(it["v"])
                    act.activation(b.prob_t[0:rows, n % 2, 0:width], m.ps[0:rows, 2 + n % 2, 0:width],
                                   ACT.Copy).then_inc(copied, 1)

        @block.vector
        def _(dve):
            link = Chain(dve, chain)
            for step in range(n_items + 2):
                n = step
                if n < n_items:
                    it = items[n]
                    at, mask = it["mask"]
                    s = m.ps[:, n % 2, at:at + mask.shape[1]]
                    dve.wait_ge(scored, n + 1)
                    link(dve.tensor_tensor(s, s, mask, ALU.add))
                    if n >= 4:
                        dve.wait_ge(exped, n - 3)
                    link(dve.tensor_reduce(b.stats[:, n % 4, 2:3], m.ps[:, n % 2, 0:it["width"]], AX, ALU.max))
                    dve.tensor_scalar(b.stats[:, n % 4, 0:1], b.stats[:, n % 4, 2:3], -it["scale"], None,
                                      ALU.mult).then_inc(maxed, 1)
                n = step - 2
                if 0 <= n < n_items:
                    it = items[n]
                    by = b.stats[:, n % 4, 3:4]
                    dve.wait_ge(exped, n + 1)
                    link(dve.reciprocal(by, b.stats[:, n % 4, 1:2]))
                    for factor in (it["gate"], it.get("any")):
                        if factor is not None:
                            link(dve.tensor_tensor(by, by, factor, ALU.mult))
                    dve.wait_ge(summed, n + 1)
                    src = m.ps[:, 4 + n % 2, 0:HD]
                    if it["first"]:
                        ins = dve.tensor_scalar(it["out"], src, by, None, ALU.mult)
                    else:
                        dve.wait_ge(out_done, n)
                        ins = dve.scalar_tensor_tensor(it["out"], src, by, it["out"], ALU.mult, ALU.add)
                    ins.then_inc(out_done, 1)


def stick_breaking(nc, m, b, h):
    rows = slice(h % 2 * HD, h % 2 * HD + HD)
    q, k = b.f[rows, S_Q + h // 2, :], b.f[rows, S_K + h // 2, :]
    soft, beta, rem = b.sb
    scale = HD ** -0.5
    strict = m.after_b
    with stage(nc, m, f"sticks_{h}") as (block, sem):
        scored, absed, logged, rem_done, suffixed, added, exped, masked, summed, chain, scaled, mins = sem(12)
        span = lambda t: slice(t * P, T)

        @block.tensor
        def _(pe):
            for t in range(NT):
                pe.matmul(m.ps[:, t, span(t)], k[:, tok(t)], q[:, span(t)], start=True, stop=True)\
                    .then_inc(scored, 1)
            pe.wait_ge(rem_done, NT)
            for t in range(NT):
                ins = pe.matmul(m.ps[:, 4 + t, span(t)], m.after_f, rem[:, t, span(t)], start=True,
                                stop=(t == NT - 1))
                for later in range(t + 1, NT):
                    ins = pe.matmul(m.ps[:, 4 + t, span(later)], m.ones, rem[:, later, span(later)],
                                    start=False, stop=(later == NT - 1))
                ins.then_inc(suffixed, 1)
            pe.wait_ge(masked, NT)
            for i in range(NT):
                for t in range(i + 1):
                    ins = pe.matmul(m.ps[:, 0, i * HD:(i + 1) * HD], beta[:, t, tok(i)],
                                    b.v[:, t, V_SB + h * HD:V_SB + (h + 1) * HD], start=(t == 0), stop=(t == i))
            ins.then_inc(summed, 1)

        @block.scalar
        def _(act):
            for t in range(NT):
                act.wait_ge(scored, t + 1)
                act.activation(rem[:, t, span(t)], m.ps[:, t, span(t)], ACT.Copy, scale=scale).then_inc(scaled, 1)
            for t in range(NT):
                act.wait_ge(scaled, t + 1)
                act.activation(soft[:, t, span(t)], rem[:, t, span(t)], ACT.Abs).then_inc(absed, 1)
            for t in range(NT):
                act.wait_ge(absed, t + 1)
                act.activation(soft[:, t, span(t)], soft[:, t, span(t)], ACT.Exp, scale=-1.0).then_inc(absed, 1)
            for t in range(NT):
                act.wait_ge(absed, NT + t + 1)
                act.activation(soft[:, t, span(t)], soft[:, t, span(t)], ACT.Ln, bias=1.0).then_inc(logged, 1)
            for t in range(NT):
                act.wait_ge(added, t + 1)
                act.activation(beta[:, t, span(t)], beta[:, t, span(t)], ACT.Exp).then_inc(exped, 1)

        @block.vector
        def _(dve):
            link = Chain(dve, chain)
            for t in range(NT):
                dve.wait_ge(scaled, t + 1)
                dve.tensor_scalar(beta[:, t, span(t)], rem[:, t, span(t)], 0.0, None, ALU.min).then_inc(mins, 1)
            for t in range(NT):
                dve.wait_ge(logged, t + 1)
                dve.wait_ge(mins, t + 1)
                link(dve.tensor_tensor(beta[:, t, span(t)], beta[:, t, span(t)], soft[:, t, span(t)],
                                       ALU.subtract))
                link(dve.tensor_tensor(rem[:, t, span(t)], beta[:, t, span(t)], rem[:, t, span(t)],
                                       ALU.subtract))
                dve.tensor_tensor(rem[:, t, tok(t)], rem[:, t, tok(t)], strict, ALU.mult).then_inc(rem_done, 1)
            for t in range(NT):
                dve.wait_ge(suffixed, t + 1)
                dve.tensor_tensor(beta[:, t, span(t)], beta[:, t, span(t)], m.ps[:, 4 + t, span(t)], ALU.add)\
                    .then_inc(added, 1)
            for t in range(NT):
                dve.wait_ge(exped, t + 1)
                dve.tensor_tensor(beta[:, t, tok(t)], beta[:, t, tok(t)], strict, ALU.mult).then_inc(masked, 1)
            dve.wait_ge(summed, 1)
            at = (MLA_H + NSA_H + h) * HD
            dve.tensor_copy(b.o[:, :, at:at + HD], m.ps[:, 0, 0:NT * HD].rearrange("p (t n) -> p t n", t=NT))


def turn_stage(nc, m, name, src, dst):
    with stage(nc, m, name) as (block, sem):
        turned = sem()

        @block.tensor
        def _(pe):
            for k in range(KD):
                for t in range(NT):
                    ins = pe.transpose(m.ps[:, k, tok(t)], src[:, t, tok(k)], m.ident)
                ins.then_inc(turned, 1)

        @block.vector
        def _(dve):
            for k in range(0, KD, 2):
                dve.wait_ge(turned, k + 1)
                dve.tensor_copy(dst[:, k, :], m.ps[:, k, :])

        @block.scalar
        def _(act):
            for k in range(1, KD, 2):
                act.wait_ge(turned, k + 1)
                act.activation(dst[:, k, :], m.ps[:, k, :], ACT.Copy)


def mixer2(nc, m, b, io, l):
    slabs = io["w_mix2"][l]
    project2(nc, m, b, slabs)
    f = b.f
    halves = [(b.swapped[0:HD, n, :], f[HD:P, N_KS + n, :]) for n in range(2)] + \
             [(b.swapped[HD:P, n, :], f[0:HD, N_KS + n, :]) for n in range(2)]
    rope_stage(nc, m, "rope", [(f[:, K_PE, :], m.turn_mla, m.cos_mla, m.sin_mla)] +
               [(f[:, n, :], m.turn_nsa, m.cos_nsa, m.sin_nsa) for n in range(N_Q, N_KW + 1)], b.turn_tmp, halves)
    norm_stage(nc, m, "q_norm", f[:, C_Q:C_Q + 2, :], b.col["q_norm"], f[:, C_Q:C_Q + 2, :], 2, 2 * P)
    norm_stage(nc, m, "kv_norm", f[:, C_KV:C_KV + 1, :], b.col["kv_norm"], f[:, C_KV:C_KV + 1, :], 1, P)
    mla_project(nc, m, b, slabs)
    rope_stage(nc, m, "rope_q", [(b.q[0:QK, h, :], m.turn_mla, m.cos_mla, m.sin_mla) for h in range(MLA_H)],
               b.turn_tmp)
    compress(nc, m, b, slabs)
    attention(nc, m, b)
    for h in range(SB_H):
        stick_breaking(nc, m, b, h)
    turn_stage(nc, m, "turn_out", b.o, m.xT)
    down_stage(nc, m, "mix2_out", slabs, 15, m.xT, KD, 1.0)


def layer(nc, m, io, l):
    with stage(nc, m, "layer_in") as (block, sem):
        loaded = sem()

        @block.sync
        def _(sp):
            sp.dma_start(m.layer_cols, io["layer_cols"][l]).then_inc(loaded, 16)
            sp.dma_start(m.gate_bias, io["gate_bias"][l].partition_broadcast(P)).then_inc(loaded, 16)
            sp.wait_ge(loaded, 32)
    ffn_stage(nc, m, "ffn1", m.col["ffn1"], io["w_ffn1"][l], 0.5)
    with mixer_memory(nc, m, "mix2"):
        b = mixer2_memory(m)
        norm_stage(nc, m, "mix_norm", m.resid, b.col["mix"], m.xT)
        mixer2(nc, m, b, io, l)
    ffn_stage(nc, m, "ffn2", m.col["ffn2"], io["w_ffn2"][l], 0.5)



def memory(nc, ctx):
    m = Buffers()

    def sb(name, *shape, dt=F32):
        return ctx.enter_context(nc.sbuf_tensor(name + "_sb", [P, *shape], dt))

    m.signals = [ctx.enter_context(nc.semaphore(f"signal_{i}")) for i in range(24)]
    m.ps = ctx.enter_context(nc.psum_tensor("psum", [P, 8, T], F32))
    m.resid = sb("resid", KD, T)
    floats, _ = constants()
    m.const = sb("const", sum(v.shape[1] for v in floats.values()))
    at = 0
    view = {}
    for n, v in floats.items():
        view[n] = m.const[:, at:at + v.shape[1]]
        at += v.shape[1]
    m.ident, m.ones, m.causal = view["ident"], view["ones"], view["causal"]
    m.upto_f, m.after_f, m.upto_b, m.after_b = (view[n] for n in ("upto_f", "after_f", "upto_b", "after_b"))
    m.turn_mla, m.cos_mla, m.sin_mla = view["turn_mla"], view["cos_mla"], view["sin_mla"]
    m.turn_nsa, m.cos_nsa, m.sin_nsa = view["turn_nsa"], view["cos_nsa"], view["sin_nsa"]
    m.cmp_mask, m.cmp_any, m.slot = view["cmp_mask"], view["cmp_any"], view["slot"]
    m.gain_buf = sb("gains", GAIN_WIDTH)
    m.gains, at = {}, 0
    for n, width in GAINS:
        m.gains[n] = m.gain_buf[:, at:at + width]
        at += width
    m.layer_cols = sb("layer_cols", LAYER_WIDTH)[:, :]
    m.gate_bias = sb("gate_bias", GATES)[:, :]
    m.col, at = {}, 0
    for n, width in LAYER_COLS:
        m.col[n] = m.layer_cols[:, at:at + width]
        at += width
    return m


@contextmanager
def mixer_memory(nc, m, name, first=False):
    with ExitStack() as ctx:
        def sb(what, *shape, dt=F32):
            return ctx.enter_context(nc.sbuf_tensor(f"{name}_{what}", [P, *shape], dt))

        m.xT = sb("normed", KD, T)
        m.ring_flat = sb("ring", SLOTS * SLAB)
        m.ring = m.ring_flat[:, :].rearrange("p (s n) -> p s n", s=SLOTS)
        m.mixed = sb("mixed", 2 * KD, T)
        m.norm_tmp = sb("norm_tmp", 3 * T)
        if first:
            m.cols = sb("group_cols", 64)[:, :]
            m.masks = sb("masks", 14 * P, dt=U8)
            by_level = m.masks[:, :].rearrange("p (l s n) -> p l s n", s=2, n=P)
            m.lower, m.upper = by_level[:, :, 0, :], by_level[:, :, 1, :]
            m.scal_buf = sb("scalars", 4 * 192 + 192 + 2 * 64 + 128)
            m.scal, at = {}, 0
            for n, heads in (("g", NG), ("step", NG), ("from_start", NG), ("to_end", NG), ("total", NG),
                             ("beta", GH), ("beta_decay", GH), ("step_to_end", SH)):
                m.scal[n] = cut(m.scal_buf, at, NT, 2, heads)
                at += NT * 2 * heads
            m.cur_buf = sb("group_scalars", 4 * NT * 2 * 8)
            m.cur = {n: cut(m.cur_buf, i * NT * 2 * 2, NT, 2, 2)
                     for i, n in enumerate(("beta", "beta_decay", "to_end", "total", "g"))}
            m.cur_ssd = {n: cut(m.cur_buf, i * NT * 2 * 8, NT, 2, 8)
                         for i, n in enumerate(("step", "step_to_end", "total", "g"))}
        left = nc.sbuf_bytes_remaining
        left = left() if callable(left) else left
        m.work = sb("work", min(left // 4 // 64 * 64, 21504))
        yield


GAINS = (("norm1", KD), ("norm2", KD), ("final", KD), ("gdn_norm", 1), ("final_2", KD))
GAIN_WIDTH = sum(w for _, w in GAINS)


def as_columns(v):
    return np.ascontiguousarray(np.asarray(v).reshape(-1, P).T)


def column_slabs(w, width=256):
    n = w.shape[1] // width
    k = w.shape[0] // P
    return np.ascontiguousarray(w.reshape(k, P, n, width).transpose(2, 1, 0, 3).reshape(n, P, k * width))


def row_slabs(w, rows=2):
    n = w.shape[0] // (rows * P)
    return np.ascontiguousarray(w.reshape(n, rows, P, w.shape[1]).transpose(0, 2, 1, 3).reshape(n, P, -1))


def layout_first(a):
    w_in = a["w_in"][0]
    conv = np.concatenate([a["conv_w"][0], a["conv_b"]], 0)
    q, k, v, xs, b, c = np.split(np.arange(3 * D + D + 512), [D, 2 * D, 3 * D, 4 * D, 4 * D + 256])
    gate, z = 4608 + np.arange(D), 4608 + D + np.arange(D)
    s = 6656
    scal = np.concatenate([s + np.arange(16), s + 16 + np.arange(8), s + 32 + np.arange(16),
                           s + 24 + np.arange(8), s + 48 + np.arange(16)])
    two = lambda x, g: x[g * 256:(g + 1) * 256]
    gdn = [np.concatenate([two(q, g), two(k, g), two(v, g), two(gate, g)]) for g in range(4)]
    ssd = [np.concatenate([b[g * P:(g + 1) * P], c[g * P:(g + 1) * P], xs[g * 512:(g + 1) * 512],
                           z[g * 512:(g + 1) * 512]]) for g in range(2)]

    def conv_cols(cols):
        return conv[:, cols[:6 * P]].reshape(8, 6, P).transpose(2, 1, 0).reshape(P, 48)

    gdn_cols = np.zeros((4, P, 64), np.float32)
    ssd_cols = np.zeros((2, P, 64), np.float32)
    for g in range(4):
        gdn_cols[g, :, :48] = conv_cols(gdn[g])
    for g in range(2):
        ssd_cols[g, :, :48] = conv_cols(ssd[g])
        ssd_cols[g, :, 48:52] = np.repeat(a["ssd_D"][0, 8 * g:8 * g + 8], 64).reshape(4, P).T
        ssd_cols[g, :, 52:56] = as_columns(a["ssd_norm_w"][0, 512 * g:512 * g + 512])
    ga, gb, sa, sb_ = a["gdn_A_log"][0], a["gdn_dt_bias"][0], a["ssd_A_log"][0], a["ssd_dt_bias"][0]
    return {
        "w_gdn": column_slabs(w_in[:, np.concatenate(gdn)]),
        "w_ssd": column_slabs(w_in[:, np.concatenate(ssd)]),
        "w_scal": np.ascontiguousarray(w_in[:, scal].reshape(KD, P, 64).transpose(1, 0, 2)),
        "scal_bias": np.concatenate([np.zeros(16, np.float32), gb[0], sb_[0], gb[1], sb_[1]]),
        "scal_a_log": np.concatenate([ga[0], sa[0], ga[1], sa[1]]),
        "gdn_cols": gdn_cols, "ssd_cols": ssd_cols,
        "w_out_1": row_slabs(a["w_out"][0]),
        "gains": np.concatenate([as_columns(a["norm1_w"][0]), as_columns(a["norm2_w"][0]),
                                 as_columns(a["final_norm_w"]), as_columns(a["gdn_norm_w"][0]),
                                 as_columns(a["final_norm_2"])], 1),
    }


def expert_slabs(gate, up, down):
    e = gate.shape[0]
    g, u = (np.stack([column_slabs(x[i]) for i in range(e)]) for x in (gate, up))
    d = np.stack([row_slabs(down[i]) for i in range(e)])
    g, u, d = (x.reshape(e // 2, 2, 2, P, SLAB) for x in (g, u, d))
    order = [g[:, 0], u[:, 0], g[:, 1], u[:, 1], d[:, 0], d[:, 1]]
    return np.ascontiguousarray(np.stack(order, 1).reshape(e * 6, P, SLAB))


def layout_experts(a):
    return {
        "w_router": np.ascontiguousarray(a["w_router"][0].reshape(KD, P, NE).transpose(1, 0, 2)),
        "w_experts": expert_slabs(a["w_gate"][0], a["w_up"][0], a["w_down"][0]),
    }


def ffn_slabs(gate, up, down):
    k = D // P
    both = np.stack([gate.reshape(k, P, FT, P), up.reshape(k, P, FT, P)], 3)
    return np.concatenate([both.transpose(2, 1, 0, 3, 4).reshape(FT, P, SLAB), row_slabs(down)])


def layout_second(a):
    mix, cols = [], []
    z = lambda *s: np.zeros(s, np.float32)
    for l in range(LAYERS):
        w = a["w_in_2"][l]
        part = dict(zip(("c_q", "c_kv", "k_pe", "q", "kc", "vc", "ks", "vs", "kw", "vw", "gate", "sq", "sk", "sv"),
                        np.split(w, np.cumsum([256, 128, 32, 384, 128, 128, 128, 128, 128, 128, 18, 256, 256]), 1)))
        k_pe = np.concatenate([z(D, NOPE), part["k_pe"], z(D, P - QK)], 1)
        gate = np.concatenate([part["gate"], z(D, P - GATES)], 1)
        tiles = np.concatenate([part["c_q"], part["c_kv"], k_pe, part["q"], part["kc"], part["ks"], part["kw"],
                                part["vc"], part["sq"], part["sk"], gate], 1)
        by_token = np.concatenate([part["vs"], part["vw"], part["sv"]], 1)
        by_token = by_token.reshape(2, 4, P, T).transpose(0, 2, 1, 3).reshape(2, P, SLAB)
        uq = a["mla_w_uq_2"][l].reshape(2, P, MLA_H * QK).transpose(1, 0, 2).reshape(P, -1)
        mla = np.concatenate([uq, a["mla_w_ukv_2"][l], z(P, SLAB - 1920)], 1)[None]
        cmp = []
        for n in ("k", "v"):
            w1 = a[f"nsa_cmp_w1_{n}_2"][l].reshape(2, 16, HD, P).transpose(0, 2, 1, 3).reshape(2, HD, SLAB)
            cmp.append(np.concatenate([w1, w1], 1))
        mix.append(np.concatenate([column_slabs(tiles), by_token, mla, *cmp, row_slabs(a["w_out_2"][l])]))
        twice = lambda x: np.concatenate([x.T, x.T], 0)
        cols.append(np.concatenate([
            as_columns(a["ffn1_norm_2"][l]), as_columns(a["mix_norm_2"][l]), as_columns(a["ffn2_norm_2"][l]),
            as_columns(a["mla_q_norm_2"][l]), as_columns(a["mla_kv_norm_2"][l]),
            twice(a["nsa_cmp_pos_k_2"][l]), twice(a["nsa_cmp_pos_v_2"][l]),
            a["nsa_cmp_w2_k_2"][l], a["nsa_cmp_w2_v_2"][l]], 1))
    return {
        "w_ffn1": np.stack([ffn_slabs(a["ffn1_w_gate_2"][l], a["ffn1_w_up_2"][l], a["ffn1_w_down_2"][l])
                            for l in range(LAYERS)]),
        "w_ffn2": np.stack([ffn_slabs(a["ffn2_w_gate_2"][l], a["ffn2_w_up_2"][l], a["ffn2_w_down_2"][l])
                            for l in range(LAYERS)]),
        "w_mix2": np.stack(mix), "layer_cols": np.stack(cols), "gate_bias": a["nsa_gate_bias_2"],
    }


def layout_consts():
    floats, bytes_ = constants()
    return {"const_f": np.concatenate(list(floats.values()), 1), "level_masks": bytes_}


def start_stage(nc, m, io):
    x = cut(m.work, 0, NT, D)
    mask_in = cut(m.work, NT * D, m.masks.shape[1])
    with stage(nc, m, "start") as (block, sem):
        x_in, const_in, turned, turned_b = sem(4)

        @block.sync
        def _(sp):
            sp.dma_start(m.const[:, :], io["const_f"]).then_inc(const_in, 16)
            sp.dma_start(x, io["x_in"].rearrange("(t p) d -> p t d", p=P)).then_inc(x_in, 16)
            sp.dma_start(mask_in, io["level_masks"]).then_inc(const_in, 16)
            sp.dma_start(m.gain_buf[:, :], io["gains"]).then_inc(const_in, 16)
            sp.wait_ge(const_in, 48)

        @block.tensor
        def _(pe):
            pe.wait_ge(const_in, 48)
            pe.wait_ge(x_in, 16)
            for k in range(KD):
                for t in range(NT):
                    ins = pe.transpose(m.ps[:, k, tok(t)], x[:, t, tok(k)], m.ident)
                ins.then_inc(turned, 1)

        @block.gpsimd
        def _(pool):
            pool.wait_ge(const_in, 48)
            pool.tensor_copy(m.masks[:, :], mask_in)

        @block.vector
        def _(dve):
            for k in range(0, KD, 2):
                dve.wait_ge(turned, k + 1)
                dve.tensor_copy(m.resid[:, k, :], m.ps[:, k, :])

        @block.scalar
        def _(act):
            for k in range(1, KD, 2):
                act.wait_ge(turned, k + 1)
                act.activation(m.resid[:, k, :], m.ps[:, k, :], ACT.Copy)



def end_stage(nc, m, out):
    by_token = cut(m.work, 0, NT, D)
    with stage(nc, m, "end") as (block, sem):
        turned, copied_v, copied_a, stored = sem(4)

        @block.tensor
        def _(pe):
            for n in range(2 * NT):
                t, half = divmod(n, 2)
                for k in range(4):
                    ins = pe.transpose(m.ps[:, n, tok(k)], m.resid[:, 4 * half + k, tok(t)], m.ident)
                ins.then_inc(turned, 1)

        @block.vector
        def _(dve):
            for t in range(NT):
                dve.wait_ge(turned, 2 * t + 1)
                dve.tensor_copy(by_token[:, t, 0:T], m.ps[:, 2 * t, :]).then_inc(copied_v, 1)

        @block.scalar
        def _(act):
            for t in range(NT):
                act.wait_ge(turned, 2 * t + 2)
                act.activation(by_token[:, t, T:D], m.ps[:, 2 * t + 1, :], ACT.Copy).then_inc(copied_a, 1)

        @block.sync
        def _(sp):
            for t in range(NT):
                sp.wait_ge(copied_v, t + 1)
                sp.wait_ge(copied_a, t + 1)
                sp.dma_start(out[t * P:(t + 1) * P, :], by_token[:, t, :]).then_inc(stored, 16)
            sp.wait_ge(stored, 16 * NT)


def program(nc, io):
    with ExitStack() as ctx:
        m = memory(nc, ctx)
        with mixer_memory(nc, m, "mix1", True):
            start_stage(nc, m, io)
            norm_stage(nc, m, "norm1", m.resid, m.gains["norm1"], m.xT)
            scalars_stage(nc, m, io)
            with nc.Fori(0, GH // 2) as pair:
                gdn_pair(nc, m, io, pair)
            with nc.Fori(0, SG) as g:
                ssd_group(nc, m, io, g)
            down_stage(nc, m, "mix1_out", io["w_out_1"], 0, m.mixed, 2 * KD, 1.0)
            norm_stage(nc, m, "norm2", m.resid, m.gains["norm2"], m.xT)
            experts(nc, m, io)
            norm_stage(nc, m, "final", m.resid, m.gains["final"], m.resid)
        with nc.Fori(0, LAYERS) as l:
            layer(nc, m, io, l)
        with mixer_memory(nc, m, "out"):
            norm_stage(nc, m, "final_2", m.resid, m.gains["final_2"], m.resid)
            end_stage(nc, m, io["out"])


def layout(inputs):
    a = {n: np.asarray(v) for n, v in inputs.items()}
    return {"x_in": a["x"][0], **layout_consts(), **layout_first(a), **layout_experts(a), **layout_second(a)}


def kernel(**inputs):
    import concourse.bacc as bacc
    from concourse.bass_utils import run_bass_kernel_spmd

    nc = bacc.Bacc("TRN2", target_bir_lowering=False, num_devices=1)
    arrays = {n: np.ascontiguousarray(v) for n, v in layout(inputs).items()}
    io = {n: nc.dram_tensor(n, v.shape, mybir.dt.from_np(v.dtype), kind="ExternalInput").ap()
          for n, v in arrays.items()}
    io["out"] = nc.dram_tensor("out", (T, D), F32, kind="ExternalOutput").ap()
    program(nc, io)
    r = run_bass_kernel_spmd(nc, [arrays], core_ids=[0])
    return r.results[0]["out"].reshape(1, T, D)
```

```python
from contextlib import ExitStack, contextmanager

import concourse.bass as bass
import numpy as np
from concourse import mybir

F32 = mybir.dt.float32
F32R = mybir.dt.float32r
U8 = mybir.dt.uint8
ALU = mybir.AluOpType
ACT = mybir.ActivationFunctionType
AX = mybir.AxisListType.X

P = 128
T = 512
D = 1024
KD = D // P
NT = T // P
SLAB = 2048
SLOTS = 4
EPS = 1e-6

GH = 8
SH = 16
SG = 2
GK = 7
NG = GH + SH
NE = 16
EF = 512
CAP = 64
FF = 2816
FT = FF // P
LAYERS = 2
MASKED = -1e30


class Buffers:
    pass


class Sems:

    def __init__(self, handles):
        self.free = list(handles)

    def __call__(self, n=None):
        if n is None:
            return self.free.pop(0)
        return [self.free.pop(0) for _ in range(n)]


@contextmanager
def stage(nc, m, name):
    with nc.Block(name) as block:
        yield block, Sems(m.signals)
    nc.all_engine_barrier(sems_to_clear=range(m.signals[0].num, m.signals[-1].num + 1))


class Chain:

    def __init__(self, eng, sem):
        self.eng, self.sem, self.n = eng, sem, 0

    def __call__(self, ins):
        ins.then_inc(self.sem, 1)
        self.n += 1
        self.eng.wait_ge(self.sem, self.n)


def cut(buf, at, *shape):
    n = int(np.prod(shape))
    flat = buf[:, at:at + n]
    if len(shape) == 1:
        return flat
    names = "abcd"[:len(shape)]
    return flat.rearrange(f"p ({' '.join(names)}) -> p {' '.join(names)}", **dict(zip(names, shape)))


def tok(t):
    return slice(t * P, (t + 1) * P)


def slab_landed(pe, landed, i):
    pe.wait_ge(landed[i % SLOTS], 16 * (i // SLOTS + 1))


def product(pe, out, weights, moving, n=KD):
    for k in range(n):
        ins = pe.matmul(out, weights(k), moving(k), start=(k == 0), stop=(k == n - 1))
    return ins


def columns(m, i, half, width=P):
    w = m.ring[:, i % SLOTS, :].rearrange("p (k n) -> p k n", k=KD)
    return lambda k: w[:, k, half * P:half * P + width]


def norm_stage(nc, m, name, src, gain, dst, tiles=KD, width=D):
    with stage(nc, m, name) as (block, sem):
        squared, summed, rooted, mean, chain = sem(5)
        sq = cut(m.norm_tmp, 0, 2, T)
        rstd = cut(m.norm_tmp, 2 * T, T)

        @block.scalar
        def _(act):
            for k in range(tiles):
                if k >= 2:
                    act.wait_ge(summed, k - 1)
                act.activation(sq[:, k % 2, :], src[:, k, :], ACT.Square).then_inc(squared, 1)
            act.wait_ge(mean, 1)
            act.activation(rstd, rstd, ACT.Sqrt).then_inc(rooted, 1)

        @block.tensor
        def _(pe):
            for k in range(tiles):
                pe.wait_ge(squared, k + 1)
                pe.matmul(m.ps[:, 0, :], m.ones, sq[:, k % 2, :], start=(k == 0),
                          stop=(k == tiles - 1)).then_inc(summed, 1)

        @block.vector
        def _(dve):
            dve.wait_ge(summed, tiles)
            dve.tensor_scalar(rstd, m.ps[:, 0, :], 1.0 / width, EPS, ALU.mult, ALU.add).then_inc(mean, 1)
            dve.wait_ge(rooted, 1)
            link = Chain(dve, chain)
            link(dve.reciprocal(rstd, rstd))
            for k in range(tiles):
                dve.scalar_tensor_tensor(dst[:, k, :], src[:, k, :], gain[:, k:k + 1], rstd,
                                         ALU.mult, ALU.mult)


def ffn_stage(nc, m, name, gain, slabs, scale):
    with ExitStack() as ctx:
        def sb(what, *shape, dt=F32R):
            return ctx.enter_context(nc.sbuf_tensor(f"{name}_{what}", [P, *shape], dt))

        x_hi, x_lo = sb("x_hi", KD, T), sb("x_lo", KD, T)
        w_hi, w_lo = sb("w_hi", 2, SLAB), sb("w_lo", 2, SLAB)
        hid_hi, hid_lo = sb("hid_hi", FT, T), sb("hid_lo", FT, T)
        raw = sb("raw", 2, SLAB, dt=F32)
        tmp = sb("tmp", 3, T, dt=F32)
        ups, downs = FT, FT // 2
        rstd = tmp[:, 2, :]

        with stage(nc, m, name) as (block, sem):
            landed = sem(2)
            hi_done, split, gated, used, silued, multiplied, hid_hi_done, hidden = sem(8)
            squared, summed, mean, rooted, scaled, x_hi_done, x_done, chain, banked = sem(9)

            def ups_then_downs(eng, up, down, last, n_down=downs):
                for n in (0, 1):
                    up(n)
                with eng.Fori(1, ups // 2) as i:
                    for q in (0, 1):
                        up(2 * i + q, q)
                for j in (0, 1):
                    down(j)
                with eng.Fori(1, n_down // 2) as i:
                    for q in (0, 1):
                        down(2 * i + q, q)
                last(n_down - 1)

            @block.sync
            def _(sp):
                def load(i, q=None):
                    q = i if q is None else q
                    if not isinstance(i, int) or i >= 2:
                        sp.wait_ge(split, i - 1)
                    sp.dma_start(raw[:, q % 2, :], slabs[i]).then_inc(landed[q % 2], 16)
                ups_then_downs(sp, load, lambda j, q=None: load(ups + j, j if q is None else q),
                               lambda j: load(ups + j, 0))

            @block.scalar
            def _(act):
                def w_part(i, q):
                    act.wait_ge(landed[q], 8 * i + (16 - 8 * q))
                    if not isinstance(i, int) or i >= 2:
                        act.wait_ge(used, i - 1)
                    act.activation(w_hi[:, q, :], raw[:, q, :], ACT.Copy).then_inc(hi_done, 1)

                for k in range(KD):
                    if k >= 2:
                        act.wait_ge(summed, k - 1)
                    act.activation(tmp[:, k % 2, :], m.resid[:, k, :], ACT.Square).then_inc(squared, 1)
                w_part(0, 0)
                act.wait_ge(mean, 1)
                act.activation(rstd, rstd, ACT.Sqrt).then_inc(rooted, 1)
                for k in range(KD):
                    act.wait_ge(scaled, k + 1)
                    act.activation(x_hi[:, k, :], tmp[:, k % 2, :], ACT.Copy, scale=gain[:, k:k + 1])\
                        .then_inc(x_hi_done, 1)
                w_part(1, 1)

                def up(n, q=None):
                    q = n if q is None else q
                    act.wait_ge(gated, n + 1)
                    if not isinstance(n, int) or n >= 2:
                        act.wait_ge(hidden, n - 1)
                    else:
                        act.wait_ge(x_done, KD)
                    act.activation(tmp[:, q, :], m.ps[:, 2 * q, :], ACT.Silu).then_inc(silued, 1)
                    w_part(n + 2, q)
                    act.wait_ge(multiplied, n + 1)
                    act.activation(hid_hi[:, n, :], tmp[:, q, :], ACT.Copy).then_inc(hid_hi_done, 1)

                def down(j, q=None):
                    w_part(ups + j + 2, j if q is None else q)
                ups_then_downs(act, up, down, lambda j: down(j, 0), downs - 2)

            @block.vector
            def _(dve):
                def w_part(i, q):
                    dve.wait_ge(hi_done, i + 1)
                    dve.tensor_tensor(w_lo[:, q, :], raw[:, q, :], w_hi[:, q, :].bitcast(F32), ALU.subtract)\
                        .then_inc(split, 1)

                w_part(0, 0)
                dve.wait_ge(summed, KD)
                dve.tensor_scalar(rstd, m.ps[:, 7, :], 1.0 / D, EPS, ALU.mult, ALU.add).then_inc(mean, 1)
                dve.wait_ge(rooted, 1)
                dve.reciprocal(rstd, rstd).then_inc(chain, 1)
                for k in range(KD):
                    dve.wait_ge(x_hi_done, k + 1)
                    dve.scalar_tensor_tensor(x_lo[:, k, :], tmp[:, k % 2, :], gain[:, k:k + 1],
                                             x_hi[:, k, :].bitcast(F32), ALU.mult, ALU.subtract)\
                        .then_inc(x_done, 1)
                w_part(1, 1)

                def up(n, q=None):
                    q = n if q is None else q
                    dve.wait_ge(silued, n + 1)
                    dve.wait_ge(used, n + 1)
                    dve.tensor_tensor(tmp[:, q, :], tmp[:, q, :], m.ps[:, 2 * q + 1, :], ALU.mult)\
                        .then_inc(multiplied, 1)
                    w_part(n + 2, q)
                    dve.wait_ge(hid_hi_done, n + 1)
                    dve.tensor_tensor(hid_lo[:, n, :], tmp[:, q, :], hid_hi[:, n, :].bitcast(F32),
                                      ALU.subtract).then_inc(hidden, 1)

                def down(j, q=None):
                    w_part(ups + j + 2, j if q is None else q)

                ups_then_downs(dve, up, down, lambda j: down(j, 0), downs - 2)
                for o in range(KD):
                    dve.wait_ge(banked, o + 1)
                    dve.scalar_tensor_tensor(m.resid[:, o, :], m.ps[:, o, :], scale, m.resid[:, o, :],
                                             ALU.mult, ALU.add)

            @block.gpsimd
            def _(pool):
                pool.wait_ge(chain, 1)
                for k in range(KD):
                    if k >= 2:
                        pool.wait_ge(x_done, k - 1)
                    pool.tensor_tensor(tmp[:, k % 2, :], m.resid[:, k, :], rstd, ALU.mult).then_inc(scaled, 1)

            @block.tensor
            def _(pe):
                def parts(out, w, q, x, start, stop):
                    pairs = ((w_hi, x[0]), (w_hi, x[1]), (w_lo, x[0]))
                    for a, (wp, xp) in enumerate(pairs):
                        ins = pe.matmul(out, wp[:, q, w], xp, start=start and a == 0, stop=stop and a == 2)
                    return ins

                for k in range(KD):
                    pe.wait_ge(squared, k + 1)
                    pe.matmul(m.ps[:, 7, :], m.ones, tmp[:, k % 2, :], start=(k == 0), stop=(k == KD - 1))\
                        .then_inc(summed, 1)

                def up(n, q=None):
                    q = n if q is None else q
                    pe.wait_ge(split, n + 1)
                    if not isinstance(n, int) or n >= 2:
                        pe.wait_ge(multiplied, n - 1)
                    for part, done in ((0, gated), (1, used)):
                        for k in range(KD):
                            if isinstance(n, int) and n == 0 and part == 0:
                                pe.wait_ge(x_done, k + 1)
                            at = k * 2 * P + part * P
                            ins = parts(m.ps[:, 2 * q + part, :], slice(at, at + P), q,
                                        (x_hi[:, k, :], x_lo[:, k, :]), k == 0, k == KD - 1)
                        ins.then_inc(done, 1)

                def down(j, q=None, final=False):
                    q = j if q is None else q
                    pe.wait_ge(split, ups + j + 1)
                    pe.wait_ge(hidden, 2 * j + 2)
                    if isinstance(j, int) and j == 0:
                        pe.wait_ge(multiplied, ups)
                    for o in range(KD):
                        for r in range(2):
                            k = 2 * j + r
                            ins = parts(m.ps[:, o, :], slice(r * D + o * P, r * D + (o + 1) * P), q % 2,
                                        (hid_hi[:, k, :], hid_lo[:, k, :]),
                                        isinstance(j, int) and j == 0 and r == 0, final and r == 1)
                        if final:
                            ins.then_inc(banked, 1)
                    if not final:
                        ins.then_inc(used, 1)
                ups_then_downs(pe, up, down, lambda j: down(j, 0, True))


def three_parts(pe, out, a, b, start, stop):
    pe.matmul(out, a[0], b[0], start=start, stop=False)
    pe.matmul(out, a[0], b[1], start=False, stop=False)
    return pe.matmul(out, a[1], b[0], start=False, stop=stop)


def down_stage(nc, m, name, slabs, first, src, tiles, scale):
    n_slabs = tiles // 2
    with ExitStack() as ctx:
        def sb(what, *shape):
            return ctx.enter_context(nc.sbuf_tensor(f"{name}_{what}", [P, *shape], F32R))

        w_hi, w_lo = sb("w_hi", 2, SLAB), sb("w_lo", 2, SLAB)
        s_hi, s_lo = sb("s_hi", 2, 2, T), sb("s_lo", 2, 2, T)
        with stage(nc, m, name) as (block, sem):
            landed = sem(SLOTS)
            hi_done, split, used, banked = sem(4)

            @block.sync
            def _(sp):
                for i in range(n_slabs):
                    if i >= SLOTS:
                        sp.wait_ge(split, 2 * (i - SLOTS + 1))
                    sp.dma_start(m.ring[:, i % SLOTS, :], slabs[first + i]).then_inc(landed[i % SLOTS], 16)

            @block.scalar
            def _(act):
                for i in range(n_slabs):
                    q = i % 2
                    if i >= 2:
                        act.wait_ge(used, i - 1)
                    act.activation(s_hi[:, q, :, :], src[:, 2 * i:2 * i + 2, :], ACT.Copy).then_inc(hi_done, 1)
                    slab_landed(act, landed, i)
                    act.activation(w_hi[:, q, :], m.ring[:, i % SLOTS, :], ACT.Copy).then_inc(hi_done, 1)

            @block.vector
            def _(dve):
                for i in range(n_slabs):
                    q = i % 2
                    dve.wait_ge(hi_done, 2 * i + 1)
                    dve.tensor_tensor(s_lo[:, q, :, :], src[:, 2 * i:2 * i + 2, :],
                                      s_hi[:, q, :, :].bitcast(F32), ALU.subtract).then_inc(split, 1)
                    dve.wait_ge(hi_done, 2 * i + 2)
                    dve.tensor_tensor(w_lo[:, q, :], m.ring[:, i % SLOTS, :], w_hi[:, q, :].bitcast(F32),
                                      ALU.subtract).then_inc(split, 1)
                for o in range(KD):
                    dve.wait_ge(banked, o + 1)
                    dve.scalar_tensor_tensor(m.resid[:, o, :], m.ps[:, o, :], scale, m.resid[:, o, :],
                                             ALU.mult, ALU.add)

            @block.tensor
            def _(pe):
                for i in range(n_slabs):
                    q, final = i % 2, i == n_slabs - 1
                    pe.wait_ge(split, 2 * i + 2)
                    for o in range(KD):
                        for r in range(2):
                            at = slice(r * D + o * P, r * D + (o + 1) * P)
                            ins = three_parts(pe, m.ps[:, o, :], (w_hi[:, q, at], w_lo[:, q, at]),
                                              (s_hi[:, q, r, :], s_lo[:, q, r, :]), i == 0 and r == 0,
                                              final and r == 1)
                        if final:
                            ins.then_inc(banked, 1)
                    if not final:
                        ins.then_inc(used, 1)



def constants():
    k, j = np.arange(P)[:, None], np.arange(P)[None, :]
    c = {
        "ident": k == j, "ones": np.ones((P, P)),
        "upto_f": k <= j, "after_f": k > j,
        "upto_b": k >= j, "after_b": k < j,
        "causal": np.where(j <= k, 0.0, MASKED),
    }
    pos = np.arange(T, dtype=np.float32)

    def rope(rot, starts, width):
        half = rot // 2
        turn = np.zeros((P, P), np.float32)
        cos, sin = np.ones((P, T), np.float32), np.zeros((P, T), np.float32)
        freq = np.float32(500000.0) ** (-np.arange(half, dtype=np.float32) / np.float32(half))
        ang = (pos[None, :] * freq[:, None]).astype(np.float32)
        for s in starts:
            for r in range(half):
                turn[s + half + r, s + r] = -1.0
                turn[s + r, s + half + r] = 1.0
            cos[s:s + half] = cos[s + half:s + rot] = np.cos(ang)
            sin[s:s + half] = sin[s + half:s + rot] = np.sin(ang)
        return turn, cos, sin

    c["turn_mla"], c["cos_mla"], c["sin_mla"] = rope(32, [64], 96)
    c["turn_nsa"], c["cos_nsa"], c["sin_nsa"] = rope(16, [0, 64], 128)
    q = np.arange(T)
    ncmp = T // 16 - 1
    end = np.arange(ncmp + 1) * 16 + 31
    cm = np.where(end[None, :] <= q[:, None], 0.0, MASKED).reshape(NT, P, ncmp + 1)
    c["cmp_mask"] = cm.transpose(1, 0, 2).reshape(P, -1)
    c["cmp_any"] = (q >= 31).astype(np.float32).reshape(NT, P).T
    c["slot"] = np.broadcast_to(np.arange(CAP), (P, CAP))
    levels = []
    for b in (1, 2, 4, 8, 16, 32, 64):
        low = (k // (2 * b) == j // (2 * b)) & (k % (2 * b) >= b) & (j % (2 * b) < b)
        levels.append((low, low.T))
    bytes_ = np.concatenate([mask for pair in levels for mask in pair], 1).astype(np.float32)
    return {n: np.ascontiguousarray(v, np.float32) for n, v in c.items()}, bytes_



def scalars_stage(nc, m, io):
    s = m.scal
    raw = cut(m.work, 0, NT, 4 * GH + 2 * SH)
    w = cut(m.work, 256, KD, 4 * GH + 2 * SH)
    bias, a_log = cut(m.work, 768, 64), cut(m.work, 832, 48)
    neg, tmp, cum = cut(m.work, 896, 48), cut(m.work, 960, NT, 48), cut(m.work, 1152, NT, 48)
    flat = {n: s[n].rearrange("p t d h -> p t (d h)") for n in ("g", "step", "from_start", "to_end", "total")}
    soft = raw[:, :, 16:64]
    with stage(nc, m, "scalars") as (block, sem):
        loaded, projected, act_in, act_out, chain, summed = sem(6)

        @block.sync
        def _(sp):
            sp.dma_start(w, io["w_scal"]).then_inc(loaded, 16)
            sp.dma_start(bias, io["scal_bias"].partition_broadcast(P)).then_inc(loaded, 16)
            sp.dma_start(a_log, io["scal_a_log"].partition_broadcast(P)).then_inc(loaded, 16)

        @block.tensor
        def _(pe):
            pe.wait_ge(loaded, 48)
            for t in range(NT):
                ins = product(pe, m.ps[:, t, 0:64], lambda k: m.xT[:, k, tok(t)], lambda k: w[:, k, :])
            ins.then_inc(projected, 1)
            pe.wait_ge(act_in, 3)
            for t in range(NT):
                for d, upto in ((0, m.upto_f), (1, m.upto_b)):
                    pe.matmul(m.ps[:, 4, t * 48 + 24 * d:t * 48 + 24 * d + 24], upto, s["g"][:, t, d, :],
                              start=True, stop=True)
                ins = pe.matmul(m.ps[:, 5, t * 48:t * 48 + 48], m.ones, flat["g"][:, t, :], start=True,
                                stop=True)
            ins.then_inc(summed, 1)

        @block.scalar
        def _(act):
            act.wait_ge(loaded, 48)
            act.activation(neg, a_log, ACT.Exp).then_inc(act_out, 1)
            act.wait_ge(act_in, 1)
            act.activation(tmp, tmp, ACT.Exp).then_inc(act_out, 1)
            act.activation(s["beta"].rearrange("p t d h -> p t (d h)"), raw[:, :, 0:16], ACT.Sigmoid)
            act.wait_ge(act_out, 2)
            act.activation(tmp, tmp, ACT.Ln, bias=1.0).then_inc(act_out, 1)
            act.wait_ge(act_in, 4)
            act.activation(flat["from_start"], cum, ACT.Exp).then_inc(act_out, 1)
            act.activation(flat["total"], m.ps[:, 5, 0:192].rearrange("p (t h) -> p t h", t=NT), ACT.Exp)
            act.activation(flat["to_end"], tmp, ACT.Exp).then_inc(act_out, 1)

        @block.vector
        def _(dve):
            link = Chain(dve, chain)
            dve.wait_ge(projected, 1)
            link(dve.tensor_tensor(raw, m.ps[:, 0:NT, 0:64], bias.unsqueeze(1).to_broadcast([P, NT, 64]),
                                   ALU.add))
            link(dve.tensor_scalar(tmp, soft, -1.0, None, ALU.mult))
            dve.tensor_tensor(tmp, tmp, soft, ALU.min).then_inc(act_in, 1)
            dve.wait_ge(act_in, 1)
            dve.wait_ge(act_out, 3)
            link(dve.scalar_tensor_tensor(flat["step"], soft, 0.0, tmp, ALU.max, ALU.add))
            link(dve.tensor_scalar(neg, neg, -1.0, None, ALU.mult))
            dve.tensor_tensor(flat["g"], flat["step"], neg.unsqueeze(1).to_broadcast([P, NT, 48]),
                              ALU.mult).then_inc(act_in, 2)
            dve.wait_ge(summed, 1)
            link(dve.tensor_copy(cum, m.ps[:, 4, 0:192].rearrange("p (t h) -> p t h", t=NT)))
            dve.tensor_tensor(tmp, m.ps[:, 5, 0:192].rearrange("p (t h) -> p t h", t=NT), cum,
                              ALU.subtract).then_inc(act_in, 1)
            dve.wait_ge(act_out, 5)
            dve.tensor_tensor(s["beta_decay"], s["beta"], s["from_start"][:, :, :, 0:GH], ALU.mult)
            dve.tensor_tensor(s["step_to_end"], s["step"][:, :, :, GH:], s["to_end"][:, :, :, GH:], ALU.mult)


TAPS = [GK // 2] + [j for j in range(GK) if j != GK // 2]


def convolve(dve, m, srcs, dsts, cols, projected, counts, steps, done):
    n = len(srcs)
    for i, tap in enumerate(TAPS):
        shift = tap - GK // 2
        for s, d, col, count in zip(srcs, dsts, cols, counts):
            if i == 0:
                dve.wait_ge(projected, count)
                ins = dve.tensor_scalar(d, s, col[:, tap:tap + 1], col[:, GK:GK + 1], ALU.mult, ALU.add)
            else:
                dve.wait_ge(steps, done + 1 - n)
                lo, hi = max(0, -shift), T - max(0, shift)
                ins = dve.scalar_tensor_tensor(d[:, lo:hi], s[:, lo + shift:hi + shift],
                                               col[:, tap:tap + 1], d[:, lo:hi], ALU.mult, ALU.add)
            ins.then_inc(steps, 1)
            done += 1
    return done


def mixer_tiles(nc, m, name, slabs, group, columns_in, n_conv, n_gate, c, gate, copies):
    tiles = n_conv + n_gate
    with stage(nc, m, name) as (block, sem):
        landed = sem(SLOTS)
        projected, steps, cols_in, gate_read, silued = sem(5)

        @block.sync
        def _(sp):
            sp.dma_start(m.cols, columns_in).then_inc(cols_in, 16)
            for i in range(tiles // 2):
                if i >= SLOTS:
                    sp.wait_ge(projected, 2 * (i - SLOTS + 1))
                sp.dma_start(m.ring[:, i % SLOTS, :], slabs[group * (tiles // 2) + i])\
                    .then_inc(landed[i % SLOTS], 16)

        @block.gpsimd
        def _(pool):
            for dst, src in copies:
                pool.tensor_copy(dst, src)

        @block.tensor
        def _(pe):
            for n in range(tiles):
                if n % 2 == 0:
                    slab_landed(pe, landed, n // 2)
                if n >= 8:
                    pe.wait_ge(steps, 14)
                product(pe, m.ps[:, n % 8, :], columns(m, n // 2, n % 2), lambda k: m.xT[:, k, :])\
                    .then_inc(projected, 1)

        @block.vector
        def _(dve):
            dve.wait_ge(cols_in, 16)
            done = 0
            for a in range(0, n_conv, 2):
                two = (a, a + 1)
                done = convolve(dve, m, [m.ps[:, n, :] for n in two], [c[:, n, :] for n in two],
                                [m.cols[:, 8 * n:8 * n + 8] for n in two], projected,
                                [n + 1 for n in two], steps, done)

        @block.scalar
        def _(act):
            for n in range(n_conv):
                act.wait_ge(steps, 14 * (n // 2 + 1))
                act.activation(c[:, n, :], c[:, n, :], ACT.Silu)
            for n in range(n_gate):
                act.wait_ge(projected, n_conv + n + 1)
                act.activation(gate[:, n, :], m.ps[:, (n_conv + n) % 8, :], ACT.Silu)


def gdn_pair(nc, m, io, hp):
    w = m.work
    c = cut(w, 0, 6, T)
    gate = cut(w, 6 * T, 2, T)
    at = [8 * T]

    def four(n=4):
        piece = cut(w, at[0], n, NT, P)
        at[0] += n * T
        return piece

    k_in, k_out, v_in = four(), four(), four()
    q_dec, dec, nT, x, xt = four(), four(), four(), four(), four()
    kb, gu = cut(m.ring_flat, 0, 4, NT, P), cut(m.ring_flat, 4 * T, 4, NT, P)
    xp, o = cut(m.ring_flat, 8 * T, 4, NT, P), cut(m.ring_flat, 12 * T, 4, NT, P)
    cur = m.cur
    chains = [(d, hh) for d in range(2) for hh in range(2)]
    upto, after = (m.upto_f, m.upto_b), (m.after_f, m.after_b)
    heads = bass.ds(2 * hp, 2)

    mixer_tiles(nc, m, "gdn_project", io["w_gdn"], hp, io["gdn_cols"][hp], 6, 2, c, gate,
                [(cur[n], m.scal[n][:, :, :, heads]) for n in ("beta", "beta_decay", "to_end", "total", "g")])

    with stage(nc, m, "gdn_lengths") as (block, sem):
        squared, summed, shifted, rooted, chain = sem(5)
        sq = x

        @block.scalar
        def _(act):
            for n in range(4):
                act.activation(sq[:, n, :, :], c[:, n, :].rearrange("p (t i) -> p t i", t=NT), ACT.Square)\
                    .then_inc(squared, 1)
            for n in range(4):
                act.wait_ge(shifted, n + 1)
                act.activation(sq[:, n, :, :], sq[:, n, :, :], ACT.Sqrt).then_inc(rooted, 1)

        @block.tensor
        def _(pe):
            for n in range(4):
                pe.wait_ge(squared, n + 1)
                pe.matmul(m.ps[:, n, :], m.ones, sq[:, n, :, :].rearrange("p t i -> p (t i)"), start=True,
                          stop=True).then_inc(summed, 1)

        @block.vector
        def _(dve):
            link = Chain(dve, chain)
            for n in range(4):
                dve.wait_ge(summed, n + 1)
                dve.tensor_scalar(sq[:, n, :, :].rearrange("p t i -> p (t i)"), m.ps[:, n, :], EPS, None,
                                  ALU.add).then_inc(shifted, 1)
            for n in range(4):
                r = sq[:, n, :, :].rearrange("p t i -> p (t i)")
                dve.wait_ge(rooted, n + 1)
                link(dve.reciprocal(r, r))
                dve.scalar_tensor_tensor(c[:, n, :], c[:, n, :], P ** -0.5 if n < 2 else 1.0, r, ALU.mult,
                                         ALU.mult)

    def wide(col):
        return col.unsqueeze(2).to_broadcast([P, NT, P])

    with stage(nc, m, "gdn_tokens") as (block, sem):
        turned, laid, rowed, chain, freed, decays, decayed = sem(7)

        @block.gpsimd
        def _(pool):
            for i, (d, hh) in enumerate(chains):
                pool.tensor_tensor(x[:, i, :, :], m.ident.unsqueeze(1).to_broadcast([P, NT, P]),
                                   wide(cur["beta"][:, :, d, hh]), ALU.mult).then_inc(laid, 1)
            for i, (d, hh) in enumerate(chains):
                pool.tensor_tensor(gu[:, i, :, :], upto[d].unsqueeze(1).to_broadcast([P, NT, P]),
                                   wide(cur["g"][:, :, d, hh]), ALU.mult).then_inc(laid, 1)

        @block.tensor
        def _(pe):
            for n in range(4):
                for t in range(NT):
                    ins = pe.transpose(m.ps[:, n, tok(t)], c[:, 2 + n, tok(t)], m.ident)
                ins.then_inc(turned, 1)
            for i in range(4):
                pe.wait_ge(laid, i + 1)
                pe.matmul(m.ps[:, 4 + i, :], m.ones, x[:, i, :, :].rearrange("p t i -> p (t i)"), start=True,
                          stop=True).then_inc(rowed, 1)
            for i, (d, hh) in enumerate(chains):
                flat = gu[:, i, :, :].rearrange("p t i -> p (t i)")
                pe.wait_ge(laid, 5 + i)
                pe.wait_ge(freed, 16)
                pe.matmul(m.ps[:, 2 * i, :], m.ones, flat, start=True, stop=True).then_inc(decays, 1)
                pe.matmul(m.ps[:, 2 * i + 1, :], after[d], flat, start=True, stop=True).then_inc(decays, 1)

        @block.vector
        def _(dve):
            by_chunk = lambda bank: m.ps[:, bank, :].rearrange("p (t i) -> p t i", t=NT)
            for i, (d, hh) in enumerate(chains):
                dve.wait_ge(turned, hh + 1)
                dve.tensor_tensor(k_in[:, i, :, :], by_chunk(hh), wide(cur["beta_decay"][:, :, d, hh]),
                                  ALU.mult).then_inc(freed, 1)
                dve.tensor_tensor(k_out[:, i, :, :], by_chunk(hh), wide(cur["to_end"][:, :, d, hh]),
                                  ALU.mult).then_inc(freed, 1)
                dve.wait_ge(turned, 2 + hh + 1)
                dve.tensor_tensor(v_in[:, i, :, :], by_chunk(2 + hh), wide(cur["beta"][:, :, d, hh]),
                                  ALU.mult).then_inc(freed, 1)
            for i, (d, hh) in enumerate(chains):
                dve.wait_ge(rowed, i + 1)
                dve.tensor_tensor(kb[:, i, :, :].rearrange("p t i -> p (t i)"), c[:, 2 + hh, :],
                                  m.ps[:, 4 + i, :], ALU.mult).then_inc(freed, 1)
            for i, (d, hh) in enumerate(chains):
                q = q_dec[:, i, :, :].rearrange("p t i -> p (t i)")
                dve.wait_ge(decayed, 2 * i + 1)
                dve.tensor_tensor(q, q, c[:, hh, :], ALU.mult)
                dve.wait_ge(decayed, 2 * i + 2)
                dve.tensor_tensor(dec[:, i, :, :], dec[:, i, :, :],
                                  upto[d].unsqueeze(1).to_broadcast([P, NT, P]), ALU.mult)

        @block.scalar
        def _(act):
            for i in range(4):
                for half, dst in ((0, q_dec), (1, dec)):
                    act.wait_ge(decays, 2 * i + half + 1)
                    act.activation(dst[:, i, :, :].rearrange("p t i -> p (t i)"), m.ps[:, 2 * i + half, :],
                                   ACT.Exp).then_inc(decayed, 1)

    with stage(nc, m, "gdn_scores") as (block, sem):
        scored, chain = sem(2)

        @block.tensor
        def _(pe):
            for i, (d, hh) in enumerate(chains):
                for bank, rhs in ((i, lambda t: kb[:, i, t, :]), (4 + i, lambda t: c[:, hh, tok(t)])):
                    for t in range(NT):
                        ins = pe.matmul(m.ps[:, bank, tok(t)], c[:, 2 + hh, tok(t)], rhs(t), start=True,
                                        stop=True)
                    ins.then_inc(scored, 1)

        @block.vector
        def _(dve):
            link = Chain(dve, chain)
            for i in range(4):
                d_ = dec[:, i, :, :].rearrange("p t i -> p (t i)")
                dve.wait_ge(scored, 2 * i + 1)
                dve.scalar_tensor_tensor(nT[:, i, :, :].rearrange("p t i -> p (t i)"), m.ps[:, i, :], -1.0,
                                         d_, ALU.mult, ALU.mult)
                dve.wait_ge(scored, 2 * i + 2)
                dve.tensor_tensor(d_, d_, m.ps[:, 4 + i, :], ALU.mult)

        @block.gpsimd
        def _(pool):
            for piece in (x, xt):
                for i in range(4):
                    pool.tensor_copy(piece[:, i, :, :], m.ident.unsqueeze(1).to_broadcast([P, NT, P]))

    with stage(nc, m, "gdn_inverse") as (block, sem):
        first, copied, filled, updated = sem(4)
        levels = 7

        @block.tensor
        def _(pe):
            for l in range(levels):
                for i in range(4):
                    if l:
                        pe.wait_ge(updated, 8 * (l - 1) + 2 * i + 2)
                    for t in range(NT):
                        ins = pe.matmul(m.ps[:, 2 * i, tok(t)], nT[:, i, t, :], x[:, i, t, :], start=True,
                                        stop=True)
                    ins.then_inc(first, 1)
                for i in range(4):
                    pe.wait_ge(copied, 4 * l + i + 1)
                    for t in range(NT):
                        ins = pe.matmul(m.ps[:, 2 * i + 1, tok(t)], xp[:, i, t, :], xt[:, i, t, :],
                                        start=True, stop=True)
                    if l < levels - 1:
                        for t in range(NT):
                            ins = pe.matmul(m.ps[:, 2 * i, tok(t)], xt[:, i, t, :], xp[:, i, t, :],
                                            start=True, stop=True)
                    ins.then_inc(filled, 1)

        @block.scalar
        def _(act):
            for l in range(levels):
                for i in range(4):
                    act.wait_ge(first, 4 * l + i + 1)
                    act.activation(xp[:, i, :, :].rearrange("p t i -> p (t i)"), m.ps[:, 2 * i, :], ACT.Copy)\
                        .then_inc(copied, 1)

        @block.vector
        def _(dve):
            for l in range(levels):
                for i, (d, hh) in enumerate(chains):
                    dve.wait_ge(filled, 4 * l + i + 1)
                    for mask, bank, dst in ((m.upper if d == 0 else m.lower, 2 * i + 1, xt),
                                            (m.lower if d == 0 else m.upper, 2 * i, x))[:1 if l == levels - 1 else 2]:
                        dve.copy_predicated(dst[:, i, :, :], mask[:, l, :].unsqueeze(1).to_broadcast([P, NT, P]),
                                            m.ps[:, bank, :].rearrange("p (t i) -> p t i", t=NT))\
                            .then_inc(updated, 1)

    minus_w = nT
    u = x[:, 0:2, :, :]
    state = x[:, 2:4, :, :]
    with stage(nc, m, "gdn_recurrence") as (block, sem):
        w_done, w_read, u_done, u_read, o_done, o_read, s_done, s_read = sem(8)
        ub, ob, sb = (4, 7), (5, 0), (6, 1)

        @block.tensor
        def _(pe):
            for i in range(4):
                for t in range(NT):
                    ins = pe.matmul(m.ps[:, i, tok(t)], k_in[:, i, t, :], xt[:, i, t, :], start=True, stop=True)
                ins.then_inc(w_done, 1)
            for s in range(NT):
                e = s % 2
                pe.wait_ge(w_read, 4)
                for i, (d, hh) in enumerate(chains):
                    t = s if d == 0 else NT - 1 - s
                    if s >= 2:
                        pe.wait_ge(u_read, s - 1)
                    ins = pe.matmul(m.ps[:, ub[e], tok(i)], xt[:, i, t, :], v_in[:, i, t, :], start=True,
                                    stop=(s == 0))
                    if s:
                        pe.wait_ge(s_read, 4 * (s - 1) + i + 1)
                        ins = pe.matmul(m.ps[:, ub[e], tok(i)], minus_w[:, i, t, :], state[:, 1 - e, i, :],
                                        start=False, stop=True)
                ins.then_inc(u_done, 1)
                pe.wait_ge(u_read, s + 1)
                if s < NT - 1:
                    for i, (d, hh) in enumerate(chains):
                        t = s if d == 0 else NT - 1 - s
                        if s >= 2:
                            pe.wait_ge(s_read, 4 * (s - 1))
                        ins = pe.matmul(m.ps[:, sb[e], tok(i)], k_out[:, i, t, :], u[:, e, i, :], start=True,
                                        stop=True)
                    ins.then_inc(s_done, 1)
                for i, (d, hh) in enumerate(chains):
                    t = s if d == 0 else NT - 1 - s
                    if s >= 2:
                        pe.wait_ge(o_read, 2 * (s - 1))
                    if s:
                        pe.matmul(m.ps[:, ob[e], tok(i)], state[:, 1 - e, i, :], q_dec[:, i, t, :], start=True,
                                  stop=False)
                    ins = pe.matmul(m.ps[:, ob[e], tok(i)], u[:, e, i, :], dec[:, i, t, :], start=(s == 0),
                                    stop=True)
                ins.then_inc(o_done, 1)

        @block.scalar
        def _(act):
            for i in range(4):
                act.wait_ge(w_done, i + 1)
                act.activation(minus_w[:, i, :, :].rearrange("p t i -> p (t i)"), m.ps[:, i, :], ACT.Copy,
                               scale=-1.0).then_inc(w_read, 1)
            for s in range(NT):
                e = s % 2
                act.wait_ge(u_done, s + 1)
                if s >= 2:
                    act.wait_ge(o_done, s - 1)
                act.activation(u[:, e, :, :].rearrange("p t i -> p (t i)"), m.ps[:, ub[e], :], ACT.Copy)\
                    .then_inc(u_read, 1)
                act.wait_ge(o_done, s + 1)
                for d in range(2):
                    t = s if d == 0 else NT - 1 - s
                    act.activation(o[:, 2 * d:2 * d + 2, t, :],
                                   m.ps[:, ob[e], 2 * d * P:(2 * d + 2) * P].rearrange("p (h i) -> p h i", h=2),
                                   ACT.Copy).then_inc(o_read, 1)

        @block.vector
        def _(dve):
            for s in range(NT - 1):
                e = s % 2
                dve.wait_ge(s_done, s + 1)
                if s >= 2:
                    dve.wait_ge(o_done, s)
                for i, (d, hh) in enumerate(chains):
                    t = s if d == 0 else NT - 1 - s
                    if s == 0:
                        ins = dve.tensor_copy(state[:, e, i, :], m.ps[:, sb[e], tok(i)])
                    else:
                        dve.wait_ge(s_read, 4 * (s - 1) + i + 1)
                        ins = dve.scalar_tensor_tensor(state[:, e, i, :], state[:, 1 - e, i, :],
                                                       cur["total"][:, t, d, hh:hh + 1], m.ps[:, sb[e], tok(i)],
                                                       ALU.mult, ALU.add)
                    ins.then_inc(s_read, 1)

    with stage(nc, m, "gdn_out") as (block, sem):
        added, squared, summed, shifted, rooted, chain = sem(6)
        both = [o[:, hh, :, :].rearrange("p t i -> p (t i)") for hh in range(2)]
        back = [o[:, 2 + hh, :, :].rearrange("p t i -> p (t i)") for hh in range(2)]

        @block.scalar
        def _(act):
            for hh in range(2):
                act.wait_ge(added, hh + 1)
                act.activation(back[hh], both[hh], ACT.Square).then_inc(squared, 1)
            for hh in range(2):
                act.wait_ge(shifted, hh + 1)
                act.activation(back[hh], back[hh], ACT.Sqrt).then_inc(rooted, 1)

        @block.tensor
        def _(pe):
            for hh in range(2):
                pe.wait_ge(squared, hh + 1)
                pe.matmul(m.ps[:, hh, :], m.ones, back[hh], start=True, stop=True).then_inc(summed, 1)

        @block.vector
        def _(dve):
            link = Chain(dve, chain)
            for hh in range(2):
                dve.tensor_tensor(both[hh], both[hh], back[hh], ALU.add).then_inc(added, 1)
            for hh in range(2):
                dve.wait_ge(summed, hh + 1)
                dve.tensor_scalar(back[hh], m.ps[:, hh, :], 1.0 / P, EPS, ALU.mult, ALU.add)\
                    .then_inc(shifted, 1)
            for hh in range(2):
                dve.wait_ge(rooted, hh + 1)
                link(dve.reciprocal(back[hh], back[hh]))
                link(dve.scalar_tensor_tensor(both[hh], both[hh], m.gains["gdn_norm"], back[hh], ALU.mult,
                                              ALU.mult))
                dve.tensor_tensor(m.mixed[:, 2 * hp + hh, :], both[hh], gate[:, hh, :], ALU.mult)


def ssd_group(nc, m, io, g):
    w = m.work
    c, gate = cut(w, 0, 6, T), cut(w, 6 * T, 4, T)
    at = [10 * T]

    def piece(*shape):
        p = cut(w, at[0], *shape)
        at[0] += int(np.prod(shape))
        return p

    b_tok = piece(NT, P)
    x_in, x_out = piece(2, NT, T), piece(2, NT, T)
    states = piece(2, NT, T)
    cb = piece(2, NT, P)
    y = piece(4, T)
    c_dec, score = cut(m.ring_flat, 0, 8, T), cut(m.ring_flat, 8 * T, 8, T)
    gu = cut(m.norm_tmp, 0, 2, NT, P)
    cur = m.cur_ssd
    upto, after = (m.upto_f, m.upto_b), (m.after_f, m.after_b)
    heads = bass.ds(8 * g, 8)
    in_g = bass.ds(8 + 8 * g, 8)

    mixer_tiles(nc, m, "ssd_project", io["w_ssd"], g, io["ssd_cols"][g], 6, 4, c, gate,
                [(cur[n], m.scal[n][:, :, :, heads if n == "step_to_end" else in_g]) for n in cur])

    def steps_of(d):
        return list(range(NT)) if d == 0 else list(range(NT))[::-1]

    with stage(nc, m, "ssd_tokens") as (block, sem):
        turned, crossed = sem(2)

        @block.tensor
        def _(pe):
            for bank, n in enumerate((0, 2, 3, 4, 5)):
                for t in range(NT):
                    ins = pe.transpose(m.ps[:, bank, tok(t)], c[:, n, tok(t)], m.ident)
                ins.then_inc(turned, 1)
            for t in range(NT):
                ins = pe.matmul(m.ps[:, 5, tok(t)], c[:, 0, tok(t)], c[:, 1, tok(t)], start=True, stop=True)
            ins.then_inc(crossed, 1)

        @block.scalar
        def _(act):
            act.wait_ge(turned, 1)
            act.activation(b_tok.rearrange("p t i -> p (t i)"), m.ps[:, 0, :], ACT.Copy)

        @block.vector
        def _(dve):
            for j in range(4):
                dve.wait_ge(turned, j + 2)
                src = m.ps[:, 1 + j, :].rearrange("p (t h i) -> p t h i", t=NT, h=2)
                for d in range(2):
                    for dst, col in ((x_in, "step"), (x_out, "step_to_end")):
                        by = cur[col][:, :, d, 2 * j:2 * j + 2].unsqueeze(3).to_broadcast([P, NT, 2, 64])
                        dve.tensor_tensor(dst[:, d, :, tok(j)].rearrange("p t (h i) -> p t h i", h=2), src,
                                          by, ALU.mult)
            dve.wait_ge(crossed, 1)
            for d in range(2):
                dve.tensor_tensor(cb[:, d, :, :], m.ps[:, 5, :].rearrange("p (t i) -> p t i", t=NT),
                                  upto[d].unsqueeze(1).to_broadcast([P, NT, P]), ALU.mult)

    with stage(nc, m, "ssd_states") as (block, sem):
        fresh, chain = sem(2)

        @block.tensor
        def _(pe):
            for s in range(NT - 1):
                for d in range(2):
                    t = steps_of(d)[s]
                    pe.matmul(m.ps[:, 2 * s + d, :], b_tok[:, t, :], x_out[:, d, t, :], start=True,
                              stop=True).then_inc(fresh, 1)

        @block.vector
        def _(dve):
            link = Chain(dve, chain)
            for s in range(NT - 1):
                for d in range(2):
                    t = steps_of(d)[s]
                    dve.wait_ge(fresh, 2 * s + d + 1)
                    new = states[:, d, s, :]
                    if s == 0:
                        link(dve.tensor_copy(new, m.ps[:, d, :]))
                        continue
                    by = cur["total"][:, t, d, :].unsqueeze(2).to_broadcast([P, 8, 64])
                    link(dve.tensor_tensor(new.rearrange("p (h i) -> p h i", h=8),
                                           states[:, d, s - 1, :].rearrange("p (h i) -> p h i", h=8), by,
                                           ALU.mult))
                    link(dve.tensor_tensor(new, new, m.ps[:, 2 * s + d, :], ALU.add))

    with stage(nc, m, "ssd_heads") as (block, sem):
        laid, decays, decayed, scored, y_done, chain, y_read = sem(7)
        combos = [(j, hh, d) for j in range(4) for hh in range(2) for d in range(2)]

        @block.gpsimd
        def _(pool):
            for n, (j, hh, d) in enumerate(combos):
                if n >= 2:
                    pool.wait_ge(decays, 2 * (n - 1))
                col = cur["g"][:, :, d, 2 * j + hh].unsqueeze(2).to_broadcast([P, NT, P])
                pool.tensor_tensor(gu[:, n % 2, :, :], upto[d].unsqueeze(1).to_broadcast([P, NT, P]), col,
                                   ALU.mult).then_inc(laid, 1)

        @block.tensor
        def _(pe):
            for j in range(5):
                for n in range(4 * j, 4 * j + 4) if j < 4 else ():
                    d = n % 2
                    flat = gu[:, n % 2, :, :].rearrange("p t i -> p (t i)")
                    pe.wait_ge(laid, n + 1)
                    if n >= 2:
                        pe.wait_ge(decayed, 2 * (n - 1))
                    pe.matmul(m.ps[:, 2 * (n % 2), :], m.ones, flat, start=True, stop=True).then_inc(decays, 1)
                    pe.matmul(m.ps[:, 2 * (n % 2) + 1, :], after[d], flat, start=True, stop=True)\
                        .then_inc(decays, 1)
                if j == 0:
                    continue
                i = j - 1
                if i >= 2:
                    pe.wait_ge(y_read, i - 1)
                for hh in range(2):
                    out = m.ps[hh * 64:hh * 64 + 64, 4 + i % 2, :]
                    pe.wait_ge(scored, 2 * (4 * i + 2 * hh + 2))
                    for t in range(NT):
                        terms = []
                        for d in range(2):
                            slot = (4 * i + 2 * hh + d) % 8
                            s = steps_of(d).index(t)
                            lanes = slice((2 * i + hh) * 64, (2 * i + hh) * 64 + 64)
                            terms.append((x_in[:, d, t, lanes], score[:, slot, tok(t)]))
                            if s:
                                terms.append((states[:, d, s - 1, lanes], c_dec[:, slot, tok(t)]))
                        for a, (lhs, rhs) in enumerate(terms):
                            ins = pe.matmul(out[:, tok(t)], lhs, rhs, start=(a == 0), stop=(a == len(terms) - 1))
                ins.then_inc(y_done, 1)

        @block.scalar
        def _(act):
            for n in range(16):
                if n >= 8:
                    act.wait_ge(y_done, n // 4 - 1)
                for half, dst in ((0, c_dec), (1, score)):
                    act.wait_ge(decays, 2 * n + half + 1)
                    act.activation(dst[:, n % 8, :], m.ps[:, 2 * (n % 2) + half, :], ACT.Exp)\
                        .then_inc(decayed, 1)

        @block.vector
        def _(dve):
            link = Chain(dve, chain)

            def out(i):
                dve.wait_ge(y_done, i + 1)
                ins = dve.scalar_tensor_tensor(y[:, i, :], c[:, 2 + i, :], m.cols[:, 48 + i:49 + i],
                                               m.ps[:, 4 + i % 2, :], ALU.mult, ALU.add)
                ins.then_inc(y_read, 1)
                dve.wait_ge(y_read, i + 1)
                dve.tensor_tensor(y[:, i, :], y[:, i, :], gate[:, i, :], ALU.mult)

            for n, (j, hh, d) in enumerate(combos):
                dve.wait_ge(decayed, 2 * n + 1)
                dve.tensor_tensor(c_dec[:, n % 8, :], c_dec[:, n % 8, :], c[:, 1, :], ALU.mult)\
                    .then_inc(scored, 1)
                dve.wait_ge(decayed, 2 * n + 2)
                dve.tensor_tensor(score[:, n % 8, :], score[:, n % 8, :],
                                  cb[:, d, :, :].rearrange("p t i -> p (t i)"), ALU.mult).then_inc(scored, 1)
                if n % 4 == 3 and j:
                    out(j - 1)
            out(3)

    with stage(nc, m, "ssd_norm") as (block, sem):
        squared, summed, mean, rooted, chain = sem(5)
        sq = cut(m.ring_flat, 0, 4, T)
        rstd = cut(m.norm_tmp, 0, T)

        @block.scalar
        def _(act):
            for i in range(4):
                act.activation(sq[:, i, :], y[:, i, :], ACT.Square).then_inc(squared, 1)
            act.wait_ge(mean, 1)
            act.activation(rstd, rstd, ACT.Sqrt).then_inc(rooted, 1)

        @block.tensor
        def _(pe):
            for i in range(4):
                pe.wait_ge(squared, i + 1)
                ins = pe.matmul(m.ps[:, 0, :], m.ones, sq[:, i, :], start=(i == 0), stop=(i == 3))
            ins.then_inc(summed, 1)

        @block.vector
        def _(dve):
            link = Chain(dve, chain)
            dve.wait_ge(summed, 1)
            dve.tensor_scalar(rstd, m.ps[:, 0, :], 1.0 / (4 * P), EPS, ALU.mult, ALU.add).then_inc(mean, 1)
            dve.wait_ge(rooted, 1)
            link(dve.reciprocal(rstd, rstd))
            for i in range(4):
                dve.scalar_tensor_tensor(m.mixed[:, 8 + 4 * g + i, :], y[:, i, :], m.cols[:, 52 + i:53 + i],
                                         rstd, ALU.mult, ALU.mult)



def experts(nc, m, io):
    w = m.work
    pick, weighed = cut(w, 0, NT, NE * CAP), cut(w, 4096, NT, NE * CAP)
    x_tok, put = cut(w, 8192, NT, D), cut(w, 12288, NE // 2, T)
    small = 16384
    affinity, slot_of = cut(w, small, NT, NE), cut(w, small + 64, NT, NE)
    router = cut(w, small + 128, KD, NE)
    peak, total = cut(w, small + 256, NT), cut(w, small + 260, NT)
    top = cut(w, small + 264, 8)[0:NE]
    rest, chosen, ones_row, count = (cut(w, small + 288 + T * i, T)[0:NE] for i in range(4))
    xs = m.mixed[:, :, :].rearrange("p a b -> p (a b)").rearrange("p (k s) -> p k s", k=KD)
    by_expert = lambda a: a.unsqueeze(2).to_broadcast([P, NT, NE])

    with stage(nc, m, "route") as (block, sem):
        loaded, logits, exped, shifted, normed, turned, placed, back, chain = sem(9)

        @block.sync
        def _(sp):
            sp.dma_start(router, io["w_router"]).then_inc(loaded, 16)

        @block.tensor
        def _(pe):
            pe.wait_ge(loaded, 16)
            for t in range(NT):
                ins = product(pe, m.ps[:, 0, t * NE:(t + 1) * NE], lambda k: m.xT[:, k, tok(t)],
                              lambda k: router[:, k, :])
            ins.then_inc(logits, 1)
            pe.wait_ge(normed, 1)
            for t in range(NT):
                ins = pe.transpose(m.ps[0:NE, 1, tok(t)], affinity[:, t, :], m.ident)
            ins.then_inc(turned, 1)
            pe.wait_ge(placed, 1)
            for t in range(NT):
                ins = pe.transpose(m.ps[:, 2, t * NE:(t + 1) * NE], chosen[:, tok(t)], m.ident[0:NE, 0:NE])
            ins.then_inc(back, 1)

        @block.scalar
        def _(act):
            act.wait_ge(shifted, 1)
            act.activation(affinity, affinity, ACT.Exp).then_inc(exped, 1)

        @block.vector
        def _(dve):
            link = Chain(dve, chain)
            link(dve.memset(ones_row, 1.0))
            dve.wait_ge(logits, 1)
            ps = m.ps[:, 0, 0:NT * NE].rearrange("p (t e) -> p t e", t=NT)
            link(dve.tensor_reduce(peak, ps, AX, ALU.max))
            dve.tensor_tensor(affinity, ps, by_expert(peak), ALU.subtract).then_inc(shifted, 1)
            dve.wait_ge(exped, 1)
            link(dve.tensor_reduce(total, affinity, AX, ALU.add))
            link(dve.reciprocal(total, total))
            dve.tensor_tensor(affinity, affinity, by_expert(total), ALU.mult).then_inc(normed, 1)
            dve.wait_ge(turned, 1)
            link(dve.tensor_copy(rest, m.ps[0:NE, 1, :]))
            for _ in range(CAP // 8):
                link(dve.max(top, rest))
                link(dve.match_replace(rest, top, rest, -1.0))
            link(dve.tensor_scalar(chosen, rest, 0.0, None, ALU.is_lt))
            link(dve.tensor_tensor_scan(count, ones_row, chosen, 0.0, ALU.mult, ALU.add))
            link(dve.tensor_tensor(count, count, chosen, ALU.mult))
            dve.tensor_scalar(chosen, count, -1.0, None, ALU.add).then_inc(placed, 1)
            dve.wait_ge(back, 1)
            dve.tensor_copy(slot_of, m.ps[:, 2, 0:NT * NE].rearrange("p (t e) -> p t e", t=NT))

    with stage(nc, m, "pick") as (block, sem):
        turned, copied, picked, weighted, gathered, put_done, freed, put_read = sem(8)

        @block.vector
        def _(dve):
            for t in range(NT):
                dve.tensor_tensor(pick[:, t, :].rearrange("p (e s) -> p e s", e=NE),
                                  m.slot.unsqueeze(1).to_broadcast([P, NE, CAP]),
                                  slot_of[:, t, :].unsqueeze(2).to_broadcast([P, NE, CAP]),
                                  ALU.is_equal).then_inc(picked, 1)
            for n in range(16):
                dve.wait_ge(gathered, n + 1)
                k, half = divmod(n, 2)
                if n % 2 == 0:
                    dve.tensor_copy(xs[:, k, half * T:(half + 1) * T], m.ps[:, 4 + n % 4, :])\
                        .then_inc(freed, 1)
            for pair in range(0, NE // 2, 2):
                dve.wait_ge(put_done, pair + 1)
                dve.tensor_copy(put[:, pair, :], m.ps[:, pair % 4, :]).then_inc(put_read, 1)

        @block.gpsimd
        def _(pool):
            for t in range(NT):
                pool.wait_ge(picked, t + 1)
                pool.tensor_tensor(weighed[:, t, :].rearrange("p (e s) -> p e s", e=NE),
                                   pick[:, t, :].rearrange("p (e s) -> p e s", e=NE),
                                   affinity[:, t, :].unsqueeze(2).to_broadcast([P, NE, CAP]),
                                   ALU.mult).then_inc(weighted, 1)

        @block.scalar
        def _(act):
            for n in range(8):
                act.wait_ge(turned, n + 1)
                t, half = divmod(n, 2)
                act.activation(x_tok[:, t, half * T:(half + 1) * T], m.ps[:, n % 4, :], ACT.Copy)\
                    .then_inc(copied, 1)
            for n in range(1, 16, 2):
                act.wait_ge(gathered, n + 1)
                k, half = divmod(n, 2)
                act.activation(xs[:, k, half * T:(half + 1) * T], m.ps[:, 4 + n % 4, :], ACT.Copy)\
                    .then_inc(copied, 1)
            for pair in range(1, NE // 2, 2):
                act.wait_ge(put_done, pair + 1)
                act.activation(put[:, pair, :], m.ps[:, pair % 4, :], ACT.Copy).then_inc(copied, 1)

        @block.tensor
        def _(pe):
            for n in range(8):
                if n >= 4:
                    pe.wait_ge(copied, n - 3)
                t, half = divmod(n, 2)
                for k in range(4):
                    ins = pe.transpose(m.ps[:, n % 4, tok(k)], m.xT[:, 4 * half + k, tok(t)], m.ident)
                ins.then_inc(turned, 1)
            pe.wait_ge(copied, 8)
            pe.wait_ge(picked, NT)
            for n in range(16):
                k, half = divmod(n, 2)
                if n >= 4:
                    pe.wait_ge(freed if n % 2 == 0 else copied, (n - 4) // 2 + 1 + (8 if n % 2 else 0))
                product(pe, m.ps[:, 4 + n % 4, :], lambda t: x_tok[:, t, tok(k)],
                        lambda t: pick[:, t, half * T:(half + 1) * T], NT).then_inc(gathered, 1)
            pe.wait_ge(weighted, NT)
            for pair in range(NE // 2):
                if pair >= 4:
                    pe.wait_ge(put_read if pair % 2 == 0 else copied,
                               (pair - 4) // 2 + 1 + (16 if pair % 2 else 0))
                for t in range(NT):
                    ins = pe.transpose(m.ps[:, pair % 4, tok(t)], weighed[:, t, tok(pair)], m.ident)
                ins.then_inc(put_done, 1)

    hid, silu = cut(w, 16384, 2, 4 * CAP), cut(w, 16384 + 512, 2, 4 * CAP)
    y = cut(w, 0, NE // 2, D)
    spare = m.xT[:, :, :].rearrange("p k t -> p (k t)")
    ring = [m.ring[:, s, :] for s in range(SLOTS)] + [spare[:, s * SLAB:(s + 1) * SLAB] for s in range(2)]
    slots = len(ring)
    with stage(nc, m, "experts") as (block, sem):
        landed = sem(slots)
        slabs_done, silued, hidden, y_read = sem(4)

        def repeat(eng, body):
            body(0, True)
            with eng.Fori(1, NE // 2) as i:
                body(i, False)

        @block.sync
        def _(sp):
            def body(i, first):
                for s in range(12):
                    if not first or s >= slots:
                        sp.wait_ge(slabs_done, 12 * i + s - slots + 1)
                    sp.dma_start(ring[s % slots], io["w_experts"][12 * i + s]).then_inc(landed[s % slots], 16)
            repeat(sp, body)

        @block.tensor
        def _(pe):
            def slab(i, s):
                pe.wait_ge(landed[s % slots], 16 * (12 // slots) * i + 16 * (s // slots + 1))

            def weights(s, k, f):
                return ring[s % slots].rearrange("p (k n) -> p k n", k=KD)[:, k, f * P:(f + 1) * P]

            def body(i, first):
                for e in range(2):
                    if not first:
                        pe.wait_ge(hidden, 2 * i - 1 + e)
                    for s in range(4):
                        slab(i, 4 * e + s)
                        for half in range(2):
                            f = 2 * (s % 2) + half
                            ins = product(pe, m.ps[:, 2 * e + s // 2, f * CAP:(f + 1) * CAP],
                                          lambda k: weights(4 * e + s, k, half),
                                          lambda k: xs[:, k, bass.ds((2 * i + e) * CAP, CAP)])
                        ins.then_inc(slabs_done, 1)
                if not first:
                    pe.wait_ge(y_read, 2 * i)
                for e in range(2):
                    pe.wait_ge(hidden, 2 * i + e + 1)
                    for s in range(2):
                        slab(i, 8 + 2 * e + s)
                        rows = ring[(8 + 2 * e + s) % slots].rearrange("p (r n) -> p r n", r=2)
                        for r in range(2):
                            f = 2 * s + r
                            for half in range(2):
                                ins = pe.matmul(m.ps[e * CAP:(e + 1) * CAP, 4 + half, :],
                                                hid[:, e, f * CAP:(f + 1) * CAP],
                                                rows[:, r, half * T:(half + 1) * T], start=(f == 0),
                                                stop=(f == 3))
                        ins.then_inc(slabs_done, 1)
            repeat(pe, body)

        @block.scalar
        def _(act):
            def body(i, first):
                for e in range(2):
                    act.wait_ge(slabs_done, 12 * i + 4 * e + 2)
                    act.activation(silu[:, e, :], m.ps[:, 2 * e, 0:4 * CAP], ACT.Silu).then_inc(silued, 1)
                act.wait_ge(slabs_done, 12 * i + 12)
                for half in range(2):
                    act.activation(y[:, i, half * T:(half + 1) * T], m.ps[:, 4 + half, :], ACT.Copy)\
                        .then_inc(y_read, 1)
            repeat(act, body)

        @block.vector
        def _(dve):
            def body(i, first):
                for e in range(2):
                    dve.wait_ge(slabs_done, 12 * i + 4 * e + 4)
                    dve.wait_ge(silued, 2 * i + e + 1)
                    dve.tensor_tensor(hid[:, e, :], silu[:, e, :], m.ps[:, 2 * e + 1, 0:4 * CAP], ALU.mult)\
                        .then_inc(hidden, 1)
            repeat(dve, body)

    with stage(nc, m, "scatter") as (block, sem):
        done, chain = sem(2)

        @block.tensor
        def _(pe):
            for k in range(KD):
                product(pe, m.ps[:, k, :], lambda pair: y[:, pair, tok(k)], lambda pair: put[:, pair, :],
                        NE // 2).then_inc(done, 1)

        @block.vector
        def _(dve):
            for k in range(KD):
                dve.wait_ge(done, k + 1)
                dve.tensor_tensor(m.resid[:, k, :], m.ps[:, k, :], m.resid[:, k, :], ALU.add)



MLA_H, NSA_H, SB_H = 6, 6, 4
HD = 64
NOPE, ROPE = 64, 32
QK = NOPE + ROPE
NCMP = T // 16 - 1
CMP_LEN = 32
GATES = 3 * NSA_H
C_Q, C_KV, K_PE, N_Q, N_KC, N_KS, N_KW, N_VC, S_Q, S_K, TILES2 = 0, 2, 3, 4, 7, 8, 9, 10, 11, 13, 15
V_SEL, V_WIN, V_SB = 0, 2 * HD, 4 * HD


@contextmanager
def mixer2_memory(nc, m):
    with ExitStack() as ctx:
        def sb(what, *shape):
            return ctx.enter_context(nc.sbuf_tensor(f"mix2_{what}", [P, *shape], F32))

        b = Buffers()
        b.col = m.col
        m.ring = sb("ring", SLOTS, SLAB)
        m.norm_tmp = sb("norm_tmp", 3 * T)
        b.projected = sb("projected", TILES2 * T)
        b.f = cut(b.projected, 0, TILES2, T)
        b.v = sb("values", NT, T)[:, :, :]
        b.gates = sb("gates", NT, GATES)[:, :, :]
        yield b


@contextmanager
def heads_memory(nc, m, b):
    with nc.sbuf_tensor("mix2_heads_out", [P, NT * D + 4096], F32) as o, \
            nc.sbuf_tensor("mix2_work", [P, 10752], F32) as w:
        b.swapped = cut(w, 0, 2, T)
        b.prob_t = cut(w, 1024, 2, T)
        b.stats = cut(w, 2048, 8, 4)
        b.kc, b.vc = cut(w, 2080, 2, 32), cut(w, 2144, 2, HD)
        b.hidden, b.tmp = cut(w, 2272, 4 * NCMP), cut(w, 2400, 4 * NCMP)
        b.q, b.k, b.v_mla = cut(w, 2560, MLA_H, T), cut(w, 5632, MLA_H, T), cut(w, 8704, NT, MLA_H * HD)
        b.sb = [[cut(w, at, NT, T) for at in (2560, 4608, 6656)],
                [cut(b.projected, 0, NT, T), cut(b.projected, 2048, NT, T), cut(w, 8704, NT, T)]]
        b.o = cut(o, 0, NT, D)
        b.blocks = cut(o, 4096, 2, CMP_LEN, 2 * NCMP)
        b.turn_tmp = cut(o, 6144, 2, T)
        b.prob = cut(o, 4096, 4, T)
        yield


LAYER_COLS = (("ffn1", KD), ("mix", KD), ("ffn2", KD), ("q_norm", 2), ("kv_norm", 1), ("pos_k", CMP_LEN),
              ("pos_v", CMP_LEN), ("w2_k", HD), ("w2_v", HD))
LAYER_WIDTH = sum(w for _, w in LAYER_COLS)


def project2(nc, m, b, slabs):
    n_slabs = 10
    x = m.ring[:, 2:4, :].rearrange("p s n -> p (s n)").rearrange("p (k t) -> p k t", k=KD)
    with ExitStack() as ctx:
        def sb(what, *shape):
            return ctx.enter_context(nc.sbuf_tensor(f"project_{what}", [P, *shape], F32R))

        x_hi, x_lo = sb("x_hi", KD, T), sb("x_lo", KD, T)
        w_hi, w_lo = sb("w_hi", 2, SLAB), sb("w_lo", 2, SLAB)
        with stage(nc, m, "mix_project") as (block, sem):
            landed = sem(2)
            x_hi_done, x_done, hi_done, split, projected, read_v, read_a = sem(7)

            @block.sync
            def _(sp):
                for i in range(n_slabs):
                    if i >= 2:
                        sp.wait_ge(split, i - 1)
                    sp.dma_start(m.ring[:, i % 2, :], slabs[i]).then_inc(landed[i % 2], 16)

            @block.tensor
            def _(pe):
                xs = lambda k, at=slice(0, T): (x_hi[:, k, at], x_lo[:, k, at])

                def ws(i, k, at, width=P, n=KD):
                    lo = k * (SLAB // n) + at
                    return w_hi[:, i % 2, lo:lo + width], w_lo[:, i % 2, lo:lo + width]

                for n in range(TILES2 + 1):
                    i, at = n // 2, n % 2 * P
                    pe.wait_ge(split, i + 1)
                    if n >= 4:
                        pe.wait_ge(read_a if n % 2 else read_v, (n - 4) // 2 + 1)
                    if n < TILES2:
                        for k in range(KD):
                            if n == 0:
                                pe.wait_ge(x_done, k + 1)
                            ins = three_parts(pe, m.ps[:, n % 4, :], ws(i, k, at), xs(k), k == 0, k == KD - 1)
                    else:
                        for t in range(NT):
                            for k in range(KD):
                                ins = three_parts(pe, m.ps[:, 3, t * GATES:(t + 1) * GATES], xs(k, tok(t)),
                                                  ws(i, k, at, GATES), k == 0, k == KD - 1)
                    ins.then_inc(projected, 1)
                for i in (8, 9):
                    pe.wait_ge(split, i + 1)
                    for t in range(NT):
                        for k in range(4):
                            ins = three_parts(pe, m.ps[:, 4 + t, :], xs(4 * (i - 8) + k, tok(t)),
                                              ws(i, k, 0, T, 4), i == 8 and k == 0, i == 9 and k == 3)
                        if i == 9:
                            ins.then_inc(projected, 1)

            @block.scalar
            def _(act):
                def hi_part(i):
                    act.wait_ge(landed[i % 2], 16 * (i // 2 + 1))
                    if i >= 2:
                        act.wait_ge(projected, 2 * (i - 1))
                    act.activation(w_hi[:, i % 2, :], m.ring[:, i % 2, :], ACT.Copy).then_inc(hi_done, 1)

                hi_part(0)
                for k in range(KD):
                    act.activation(x_hi[:, k, :], x[:, k, :], ACT.Copy).then_inc(x_hi_done, 1)
                hi_part(1)
                for i in range(n_slabs - 2):
                    n = 2 * i + 1
                    if n < TILES2:
                        act.wait_ge(projected, n + 1)
                        act.activation(b.f[:, n, :], m.ps[:, n % 4, :], ACT.Copy).then_inc(read_a, 1)
                    hi_part(i + 2)
                act.wait_ge(read_v, 9)
                act.activation(b.gates, b.gates, ACT.Sigmoid)
                for t in (1, 3):
                    act.wait_ge(projected, TILES2 + 2 + t)
                    act.activation(b.v[:, t, :], m.ps[:, 4 + t, :], ACT.Copy)

            @block.vector
            def _(dve):
                def lo_part(i):
                    dve.wait_ge(hi_done, i + 1)
                    dve.tensor_tensor(w_lo[:, i % 2, :], m.ring[:, i % 2, :], w_hi[:, i % 2, :].bitcast(F32),
                                      ALU.subtract).then_inc(split, 1)

                lo_part(0)
                for k in range(KD):
                    dve.wait_ge(x_hi_done, k + 1)
                    dve.tensor_tensor(x_lo[:, k, :], x[:, k, :], x_hi[:, k, :].bitcast(F32), ALU.subtract)\
                        .then_inc(x_done, 1)
                lo_part(1)
                for i in range(n_slabs - 2):
                    n = 2 * i
                    dve.wait_ge(projected, n + 1)
                    dve.tensor_copy(b.f[:, n, :], m.ps[:, n % 4, :]).then_inc(read_v, 1)
                    lo_part(i + 2)
                dve.wait_ge(projected, TILES2 + 1)
                dve.tensor_tensor(b.gates, m.ps[:, 3, 0:NT * GATES].rearrange("p (t n) -> p t n", t=NT),
                                  m.gate_bias.unsqueeze(1).to_broadcast([P, NT, GATES]), ALU.add)\
                    .then_inc(read_v, 1)
                for t in (0, 2):
                    dve.wait_ge(projected, TILES2 + 2 + t)
                    dve.tensor_copy(b.v[:, t, :], m.ps[:, 4 + t, :])


def rope_stage(nc, m, name, tiles, tmp, after=None):
    with stage(nc, m, name) as (block, sem):
        turned, read, scaled, chain, done, swapped = sem(6)

        @block.tensor
        def _(pe):
            for n, (x, turn, _, _) in enumerate(tiles):
                if n >= 4:
                    pe.wait_ge(read, n - 3)
                rows = x.shape[0]
                pe.matmul(m.ps[0:rows, n % 4, :], turn[0:rows, 0:rows], x, start=True, stop=True)\
                    .then_inc(turned, 1)

        @block.gpsimd
        def _(pool):
            for n, (x, _, cos, _) in enumerate(tiles):
                pool.wait_ge(turned, n + 1)
                pool.tensor_tensor(x, x, cos[0:x.shape[0]], ALU.mult).then_inc(scaled, 1)

        @block.vector
        def _(dve):
            for n, (x, _, _, sin) in enumerate(tiles):
                rows = x.shape[0]
                dve.wait_ge(turned, n + 1)
                dve.tensor_tensor(tmp[0:rows, n % 2, :], m.ps[0:rows, n % 4, :], sin[0:rows], ALU.mult)\
                    .then_inc(read, 1)
                dve.wait_ge(read, n + 1)
                dve.wait_ge(scaled, n + 1)
                dve.tensor_tensor(x, x, tmp[0:rows, n % 2, :], ALU.add).then_inc(done, 1)

        if after:
            @block.sync
            def _(sp):
                sp.wait_ge(done, len(tiles))
                for dst, src in after:
                    sp.dma_start(dst, src).then_inc(swapped, 16)
                sp.wait_ge(swapped, 16 * len(after))


def mla_project(nc, m, b, slabs):
    with stage(nc, m, "mla_project") as (block, sem):
        ring = m.ring[:, 0, :]
        landed, projected, read_v, read_a = sem(4)
        w_q = cut(ring, 0, 2, MLA_H * QK)
        w_kv = cut(ring, 2 * MLA_H * QK, MLA_H, NOPE + HD)

        @block.sync
        def _(sp):
            sp.dma_start(m.ring[:, 0, :], slabs[10]).then_inc(landed, 16)

        @block.tensor
        def _(pe):
            pe.wait_ge(landed, 16)
            for n in range(2 * MLA_H):
                h = n // 2
                if n >= 4:
                    pe.wait_ge(read_a if n % 2 else read_v, (n - 4) // 2 + 1)
                if n % 2 == 0:
                    ins = product(pe, m.ps[0:QK, n % 4, :], lambda k: w_q[:, k, h * QK:(h + 1) * QK],
                                  lambda k: b.f[:, C_Q + k, :], 2)
                else:
                    ins = pe.matmul(m.ps[0:NOPE, n % 4, :], w_kv[:, h, 0:NOPE], b.f[:, C_KV, :], start=True,
                                    stop=True)
                ins.then_inc(projected, 1)
            for t in range(NT):
                pe.matmul(m.ps[:, 4 + t, 0:MLA_H * HD].rearrange("p (h n) -> p h n", h=MLA_H),
                          b.f[:, C_KV, tok(t)], w_kv[:, :, NOPE:], start=True, stop=True)\
                    .then_inc(projected, 1)

        @block.vector
        def _(dve):
            for h in range(MLA_H):
                dve.wait_ge(projected, 2 * h + 1)
                dve.tensor_copy(b.q[0:QK, h, :], m.ps[0:QK, 2 * h % 4, :]).then_inc(read_v, 1)
            for t in range(NT):
                dve.wait_ge(projected, 2 * MLA_H + t + 1)
                dve.tensor_copy(b.v_mla[:, t, :], m.ps[:, 4 + t, 0:MLA_H * HD])

        @block.scalar
        def _(act):
            for h in range(MLA_H):
                act.wait_ge(projected, 2 * h + 2)
                act.activation(b.k[0:NOPE, h, :], m.ps[0:NOPE, (2 * h + 1) % 4, :], ACT.Copy).then_inc(read_a, 1)

        @block.gpsimd
        def _(pool):
            for h in range(MLA_H):
                pool.tensor_copy(b.k[NOPE:QK, h, :], b.f[NOPE:QK, K_PE, :])


def compress(nc, m, b, slabs):
    with stage(nc, m, "compress") as (block, sem):
        landed = sem(4)
        blocks_in, hidden_done, cleared, cubed, tanhed, ready, small_done, chain = sem(8)

        @block.sync
        def _(sp):
            for i in range(4):
                sp.dma_start(m.ring[:, i, :], slabs[11 + i]).then_inc(landed[i], 16)

        @block.gpsimd
        def _(pool):
            for n in range(2):
                for g in range(2):
                    pool.memset(b.blocks[g * HD:(g + 1) * HD, n, :, (1 - g) * NCMP:(2 - g) * NCMP], 0.0)\
                        .then_inc(cleared, 1)

        @block.vector
        def _(dve):
            link = Chain(dve, chain)
            for n, (tile, pos) in enumerate(((N_KC, "pos_k"), (N_VC, "pos_v"))):
                x = b.f[:, tile, :].rearrange("p (n l) -> p l n", l=16)
                for g in range(2):
                    rows, at = slice(g * HD, (g + 1) * HD), slice(g * NCMP, (g + 1) * NCMP)
                    for half in range(2):
                        dve.tensor_tensor(b.blocks[rows, n, 16 * half:16 * half + 16, at],
                                          x[rows, :, half:half + NCMP],
                                          b.col[pos][rows, 16 * half:16 * half + 16].unsqueeze(2)
                                          .to_broadcast([HD, 16, NCMP]), ALU.add).then_inc(blocks_in, 1)
            dve.wait_ge(hidden_done, 2)
            hid, tmp = b.hidden, b.tmp
            link(dve.tensor_copy(hid.rearrange("p (n c) -> p n c", n=2), m.ps[:, 0:2, 0:2 * NCMP]))
            link(dve.tensor_tensor(tmp, hid, hid, ALU.mult))
            link(dve.tensor_scalar(tmp, tmp, 0.044715, 1.0, ALU.mult, ALU.add))
            dve.tensor_tensor(tmp, tmp, hid, ALU.mult).then_inc(cubed, 1)
            dve.wait_ge(tanhed, 1)
            link(dve.tensor_scalar(tmp, tmp, 0.5, 0.5, ALU.mult, ALU.add))
            dve.tensor_tensor(hid, hid, tmp, ALU.mult).then_inc(ready, 1)
            dve.wait_ge(small_done, 1)
            dve.tensor_copy(b.kc[:, :, 0:NCMP], m.ps[:, 4, 0:2 * NCMP].rearrange("p (g c) -> p g c", g=2))
            dve.tensor_copy(b.vc[0:NCMP, :, :], m.ps[0:NCMP, 5, 0:2 * HD].rearrange("p (g d) -> p g d", g=2))

        @block.scalar
        def _(act):
            act.wait_ge(cubed, 1)
            act.activation(b.tmp, b.tmp, ACT.Tanh, scale=0.7978845608028654).then_inc(tanhed, 1)

        @block.tensor
        def _(pe):
            for n in range(2):
                pe.wait_ge(blocks_in, 4 * n + 4)
                pe.wait_ge(cleared, 2 * n + 2)
                for l in range(CMP_LEN):
                    if l % 16 == 0:
                        pe.wait_ge(landed[2 * n + l // 16], 16)
                    w = m.ring[:, 2 * n + l // 16, (l % 16) * P:(l % 16 + 1) * P]
                    ins = pe.matmul(m.ps[:, n, 0:2 * NCMP], w, b.blocks[:, n, l, :], start=(l == 0),
                                    stop=(l == CMP_LEN - 1))
                ins.then_inc(hidden_done, 1)
            pe.wait_ge(ready, 1)
            hid = b.hidden.rearrange("p (n c) -> p n c", n=4)
            for g in range(2):
                for base in (0, HD):
                    pe.matmul(m.ps[base:base + HD, 4, g * NCMP:(g + 1) * NCMP], b.col["w2_k"], hid[:, g, :],
                              start=True, stop=True)
                ins = pe.matmul(m.ps[0:NCMP, 5, g * HD:(g + 1) * HD], hid[:, 2 + g, :], b.col["w2_v"],
                                start=True, stop=True)
            ins.then_inc(small_done, 1)


def attention_items(m, b):
    items = []
    for h in range(MLA_H):
        for i in range(NT):
            items.append(dict(
                q=b.q[0:QK, h, tok(i)], k=b.k[0:QK, h, 0:(i + 1) * P], width=(i + 1) * P,
                v=[b.v_mla[:, t, h * HD:(h + 1) * HD] for t in range(i + 1)], mask=(i * P, m.causal),
                scale=QK ** -0.5, out=b.o[:, i, h * HD:(h + 1) * HD], gate=None, first=True))
    for h in range(NSA_H):
        g, rows = h // 3, slice(h % 2 * HD, h % 2 * HD + HD)
        for i in range(NT):
            q = b.f[rows, N_Q + h // 2, tok(i)]
            out = b.o[:, i, (MLA_H + h) * HD:(MLA_H + h + 1) * HD]
            gate = lambda n: b.gates[:, i, 3 * h + n:3 * h + n + 1]
            items.append(dict(
                q=q, k=b.kc[rows, g, 0:NCMP], width=NCMP, v=[b.vc[0:NCMP, g, :]],
                mask=(0, m.cmp_mask.rearrange("p (t c) -> p t c", t=NT)[:, i, 0:NCMP]), scale=HD ** -0.5,
                out=out, gate=gate(0), first=True))
            for n, tile, v in ((1, N_KS, V_SEL), (2, N_KW, V_WIN)):
                src = b.f[rows, tile, :] if g == h % 2 else b.swapped[rows, tile - N_KS, :]
                items.append(dict(
                    q=q, k=src[:, 0:(i + 1) * P], width=(i + 1) * P,
                    v=[b.v[:, t, v + g * HD:v + (g + 1) * HD] for t in range(i + 1)], mask=(i * P, m.causal),
                    scale=HD ** -0.5, out=out, gate=gate(n), first=False))
    return items


def attention(nc, m, b):
    items = attention_items(m, b)
    with stage(nc, m, "attention") as (block, sem):
        scored, maxed, exped, turned, copied, summed, out_done, chain = sem(8)
        n_items = len(items)

        @block.tensor
        def _(pe):
            for step in range(n_items + 3):
                n = step
                if n < n_items:
                    it = items[n]
                    if n >= 4:
                        pe.wait_ge(exped, n - 3)
                    pe.matmul(m.ps[:, n % 4, 0:it["width"]], it["q"], it["k"], start=True, stop=True)\
                        .then_inc(scored, 1)
                n = step - 2
                if 0 <= n < n_items:
                    it = items[n]
                    pe.wait_ge(exped, n + 1)
                    if n >= 2:
                        pe.wait_ge(copied, n - 1)
                    for t in range(len(it["v"])):
                        keys = min(P, it["width"] - t * P)
                        ins = pe.transpose(m.ps[0:keys, 4 + n % 2, tok(t)],
                                           b.prob[:, n % 4, t * P:t * P + keys], m.ident)
                    ins.then_inc(turned, 1)
                n = step - 3
                if 0 <= n < n_items:
                    it = items[n]
                    pe.wait_ge(copied, n + 1)
                    if n >= 2:
                        pe.wait_ge(out_done, n - 1)
                    for t, v in enumerate(it["v"]):
                        keys = min(P, it["width"] - t * P)
                        ins = pe.matmul(m.ps[:, 6 + n % 2, 0:HD], b.prob_t[0:keys, n % 2, tok(t)], v,
                                        start=(t == 0), stop=(t == len(it["v"]) - 1))
                    ins.then_inc(summed, 1)

        @block.scalar
        def _(act):
            for step in range(n_items + 2):
                n = step
                if n < n_items:
                    it = items[n]
                    act.wait_ge(maxed, n + 1)
                    if n >= 4:
                        act.wait_ge(turned, n - 3)
                    if n >= 8:
                        act.wait_ge(out_done, n - 7)
                    act.activation(b.prob[:, n % 4, 0:it["width"]], m.ps[:, n % 4, 0:it["width"]], ACT.Exp,
                                   bias=b.stats[:, n % 8, 0:1], scale=it["scale"],
                                   accum_out=b.stats[:, n % 8, 1:2]).then_inc(exped, 1)
                n = step - 2
                if 0 <= n < n_items:
                    it = items[n]
                    act.wait_ge(turned, n + 1)
                    if n >= 2:
                        act.wait_ge(summed, n - 1)
                    rows, width = min(P, it["width"]), P * len(it["v"])
                    act.activation(b.prob_t[0:rows, n % 2, 0:width], m.ps[0:rows, 4 + n % 2, 0:width],
                                   ACT.Copy).then_inc(copied, 1)

        @block.vector
        def _(dve):
            steps = 0

            def marked(ins):
                nonlocal steps
                ins.then_inc(chain, 1)
                steps += 1
                return steps

            first_gates = b.gates.rearrange("p t (h n) -> p t h n", n=3)[:, :, :, 0]
            gates_done = marked(dve.tensor_tensor(first_gates, first_gates, m.cmp_any.unsqueeze(2)
                                                  .to_broadcast([P, NT, NSA_H]), ALU.mult))
            dve.wait_ge(chain, gates_done)
            for n in range(n_items + 3):
                it = items[n] if n < n_items else None
                old = items[n - 3] if n >= 3 else None
                stats, old_stats = b.stats[:, n % 8, :], b.stats[:, (n - 3) % 8, :]
                if it:
                    at, mask = it["mask"]
                    s = m.ps[:, n % 4, at:at + mask.shape[1]]
                    dve.wait_ge(scored, n + 1)
                    mask_done = marked(dve.tensor_tensor(s, s, mask, ALU.add))
                if old:
                    dve.wait_ge(exped, n - 2)
                    by_done = marked(dve.reciprocal(old_stats[:, 3:4], old_stats[:, 1:2]))
                if it:
                    dve.wait_ge(chain, mask_done)
                    if n >= 8:
                        dve.wait_ge(exped, n - 7)
                    max_done = marked(dve.tensor_reduce(stats[:, 2:3], m.ps[:, n % 4, 0:it["width"]], AX,
                                                        ALU.max))
                if old:
                    dve.wait_ge(chain, by_done)
                    if not old["first"]:
                        by_done = marked(dve.tensor_tensor(old_stats[:, 3:4], old_stats[:, 3:4], old["gate"],
                                                           ALU.mult))
                if it:
                    dve.wait_ge(chain, max_done)
                    dve.tensor_scalar(stats[:, 0:1], stats[:, 2:3], -it["scale"], None, ALU.mult)\
                        .then_inc(maxed, 1)
                if old:
                    dve.wait_ge(chain, by_done)
                    dve.wait_ge(summed, n - 2)
                    src, by = m.ps[:, 6 + (n - 3) % 2, 0:HD], old_stats[:, 3:4]
                    if not old["first"]:
                        dve.wait_ge(out_done, n - 3)
                        ins = dve.scalar_tensor_tensor(old["out"], src, by, old["out"], ALU.mult, ALU.add)
                    elif old["gate"] is not None:
                        ins = dve.tensor_scalar(old["out"], src, by, old["gate"], ALU.mult, ALU.mult)
                    else:
                        ins = dve.tensor_scalar(old["out"], src, by, None, ALU.mult)
                    ins.then_inc(out_done, 1)


def stick_breaking(nc, m, b, pair):
    scale = HD ** -0.5
    strict = m.after_b
    units = [(e, t) for e in range(2) for t in range(NT)]
    n_units = len(units)
    span = lambda t: slice(t * P, T)

    def piece(i, e, t):
        return b.sb[e][i][:, t, span(t)]
    soft = lambda e, t: piece(0, e, t)
    beta = lambda e, t: piece(1, e, t)
    rem = lambda e, t: piece(2, e, t)
    bank = lambda e, t: m.ps[:, NT * e + t, span(t)]
    with stage(nc, m, f"sticks_{pair}") as (block, sem):
        scored, absed, logged, rem_done, suffixed, added, exped, masked, summed, chain, scaled, mins = sem(12)

        @block.tensor
        def _(pe):
            for e, t in units:
                rows = slice(e * HD, (e + 1) * HD)
                q, k = b.f[rows, S_Q + pair, span(t)], b.f[rows, S_K + pair, tok(t)]
                pe.matmul(bank(e, t), k, q, start=True, stop=True).then_inc(scored, 1)
            for e in range(2):
                pe.wait_ge(rem_done, NT * (e + 1))
                for t in range(NT):
                    ins = pe.matmul(bank(e, t), m.after_f, rem(e, t), start=True, stop=(t == NT - 1))
                    for later in range(t + 1, NT):
                        ins = pe.matmul(m.ps[:, NT * e + t, span(later)], m.ones, rem(e, later), start=False,
                                        stop=(later == NT - 1))
                    ins.then_inc(suffixed, 1)
            for e in range(2):
                h = 2 * pair + e
                pe.wait_ge(masked, NT * (e + 1))
                for i in range(NT):
                    for t in range(i + 1):
                        ins = pe.matmul(m.ps[:, NT * e, i * HD:(i + 1) * HD], b.sb[e][1][:, t, tok(i)],
                                        b.v[:, t, V_SB + h * HD:V_SB + (h + 1) * HD], start=(t == 0),
                                        stop=(t == i))
                ins.then_inc(summed, 1)

        @block.scalar
        def _(act):
            for n, (e, t) in enumerate(units):
                act.wait_ge(scored, n + 1)
                act.activation(rem(e, t), bank(e, t), ACT.Copy, scale=scale).then_inc(scaled, 1)
            for n, (e, t) in enumerate(units):
                act.wait_ge(scaled, n + 1)
                act.activation(soft(e, t), rem(e, t), ACT.Abs).then_inc(absed, 1)
            for n, (e, t) in enumerate(units):
                act.wait_ge(absed, n + 1)
                act.activation(soft(e, t), soft(e, t), ACT.Exp, scale=-1.0).then_inc(absed, 1)
            for n, (e, t) in enumerate(units):
                act.wait_ge(absed, n_units + n + 1)
                act.activation(soft(e, t), soft(e, t), ACT.Ln, bias=1.0).then_inc(logged, 1)
            for n, (e, t) in enumerate(units):
                act.wait_ge(added, n + 1)
                act.activation(beta(e, t), beta(e, t), ACT.Exp).then_inc(exped, 1)

        @block.vector
        def _(dve):
            link = Chain(dve, chain)
            for n, (e, t) in enumerate(units):
                dve.wait_ge(scaled, n + 1)
                dve.tensor_scalar(beta(e, t), rem(e, t), 0.0, None, ALU.min).then_inc(mins, 1)
            for n, (e, t) in enumerate(units):
                dve.wait_ge(logged, n + 1)
                dve.wait_ge(mins, n + 1)
                link(dve.tensor_tensor(beta(e, t), beta(e, t), soft(e, t), ALU.subtract))
                link(dve.tensor_tensor(rem(e, t), beta(e, t), rem(e, t), ALU.subtract))
                own = b.sb[e][2][:, t, tok(t)]
                dve.tensor_tensor(own, own, strict, ALU.mult).then_inc(rem_done, 1)
            for n, (e, t) in enumerate(units):
                dve.wait_ge(suffixed, n + 1)
                dve.tensor_tensor(beta(e, t), beta(e, t), bank(e, t), ALU.add).then_inc(added, 1)
            for n, (e, t) in enumerate(units):
                dve.wait_ge(exped, n + 1)
                own = b.sb[e][1][:, t, tok(t)]
                dve.tensor_tensor(own, own, strict, ALU.mult).then_inc(masked, 1)
            for e in range(2):
                dve.wait_ge(summed, e + 1)
                at = (MLA_H + NSA_H + 2 * pair + e) * HD
                dve.tensor_copy(b.o[:, :, at:at + HD],
                                m.ps[:, NT * e, 0:NT * HD].rearrange("p (t n) -> p t n", t=NT))


def turn_stage(nc, m, name, src, dst):
    with stage(nc, m, name) as (block, sem):
        turned = sem()

        @block.tensor
        def _(pe):
            for k in range(KD):
                for t in range(NT):
                    ins = pe.transpose(m.ps[:, k, tok(t)], src[:, t, tok(k)], m.ident)
                ins.then_inc(turned, 1)

        @block.vector
        def _(dve):
            for k in range(0, KD, 2):
                dve.wait_ge(turned, k + 1)
                dve.tensor_copy(dst[:, k, :], m.ps[:, k, :])

        @block.scalar
        def _(act):
            for k in range(1, KD, 2):
                act.wait_ge(turned, k + 1)
                act.activation(dst[:, k, :], m.ps[:, k, :], ACT.Copy)


def mixer2(nc, m, io, l):
    slabs = io["w_mix2"][l]
    with mixer2_memory(nc, m) as b:
        x = m.ring[:, 2:4, :].rearrange("p s n -> p (s n)").rearrange("p (k t) -> p k t", k=KD)
        norm_stage(nc, m, "mix_norm", m.resid, b.col["mix"], x)
        project2(nc, m, b, slabs)
        with nc.sbuf_tensor("mix2_turned", [P, KD, T], F32) as turned:
            with heads_memory(nc, m, b):
                heads2(nc, m, b, slabs, turned)
            down_stage(nc, m, "mix2_out", slabs, 15, turned, KD, 1.0)


def heads2(nc, m, b, slabs, turned):
    f = b.f
    halves = [(b.swapped[0:HD, n, :], f[HD:P, N_KS + n, :]) for n in range(2)] + \
             [(b.swapped[HD:P, n, :], f[0:HD, N_KS + n, :]) for n in range(2)]
    rope_stage(nc, m, "rope", [(f[:, K_PE, :], m.turn_mla, m.cos_mla, m.sin_mla)] +
               [(f[:, n, :], m.turn_nsa, m.cos_nsa, m.sin_nsa) for n in range(N_Q, N_KW + 1)], b.turn_tmp, halves)
    norm_stage(nc, m, "q_norm", f[:, C_Q:C_Q + 2, :], b.col["q_norm"], f[:, C_Q:C_Q + 2, :], 2, 2 * P)
    norm_stage(nc, m, "kv_norm", f[:, C_KV:C_KV + 1, :], b.col["kv_norm"], f[:, C_KV:C_KV + 1, :], 1, P)
    mla_project(nc, m, b, slabs)
    rope_stage(nc, m, "rope_q", [(b.q[0:QK, h, :], m.turn_mla, m.cos_mla, m.sin_mla) for h in range(MLA_H)],
               b.turn_tmp)
    compress(nc, m, b, slabs)
    attention(nc, m, b)
    for pair in range(SB_H // 2):
        stick_breaking(nc, m, b, pair)
    turn_stage(nc, m, "turn_out", b.o, turned)


def layer(nc, m, io, l):
    with stage(nc, m, "layer_in") as (block, sem):
        loaded = sem()

        @block.sync
        def _(sp):
            sp.dma_start(m.layer_cols, io["layer_cols"][l]).then_inc(loaded, 16)
            sp.dma_start(m.gate_bias, io["gate_bias"][l].partition_broadcast(P)).then_inc(loaded, 16)
            sp.wait_ge(loaded, 32)
    ffn_stage(nc, m, "ffn1", m.col["ffn1"], io["w_ffn1"][l], 0.5)
    mixer2(nc, m, io, l)
    ffn_stage(nc, m, "ffn2", m.col["ffn2"], io["w_ffn2"][l], 0.5)



def memory(nc, ctx):
    m = Buffers()

    def sb(name, *shape, dt=F32):
        return ctx.enter_context(nc.sbuf_tensor(name + "_sb", [P, *shape], dt))

    m.signals = [ctx.enter_context(nc.semaphore(f"signal_{i}")) for i in range(24)]
    m.ps = ctx.enter_context(nc.psum_tensor("psum", [P, 8, T], F32))
    m.resid = sb("resid", KD, T)
    floats, _ = constants()
    m.const = sb("const", sum(v.shape[1] for v in floats.values()))
    at = 0
    view = {}
    for n, v in floats.items():
        view[n] = m.const[:, at:at + v.shape[1]]
        at += v.shape[1]
    m.ident, m.ones, m.causal = view["ident"], view["ones"], view["causal"]
    m.upto_f, m.after_f, m.upto_b, m.after_b = (view[n] for n in ("upto_f", "after_f", "upto_b", "after_b"))
    m.turn_mla, m.cos_mla, m.sin_mla = view["turn_mla"], view["cos_mla"], view["sin_mla"]
    m.turn_nsa, m.cos_nsa, m.sin_nsa = view["turn_nsa"], view["cos_nsa"], view["sin_nsa"]
    m.cmp_mask, m.cmp_any, m.slot = view["cmp_mask"], view["cmp_any"], view["slot"]
    m.gain_buf = sb("gains", GAIN_WIDTH)
    m.gains, at = {}, 0
    for n, width in GAINS:
        m.gains[n] = m.gain_buf[:, at:at + width]
        at += width
    m.layer_cols = sb("layer_cols", LAYER_WIDTH)[:, :]
    m.gate_bias = sb("gate_bias", GATES)[:, :]
    m.col, at = {}, 0
    for n, width in LAYER_COLS:
        m.col[n] = m.layer_cols[:, at:at + width]
        at += width
    return m


@contextmanager
def mixer_memory(nc, m, name, first=False):
    with ExitStack() as ctx:
        def sb(what, *shape, dt=F32):
            return ctx.enter_context(nc.sbuf_tensor(f"{name}_{what}", [P, *shape], dt))

        m.xT = sb("normed", KD, T)
        m.ring_flat = sb("ring", SLOTS * SLAB)
        m.ring = m.ring_flat[:, :].rearrange("p (s n) -> p s n", s=SLOTS)
        m.mixed = sb("mixed", 2 * KD, T)
        m.norm_tmp = sb("norm_tmp", 3 * T)
        if first:
            m.cols = sb("group_cols", 64)[:, :]
            m.masks = sb("masks", 14 * P, dt=U8)
            by_level = m.masks[:, :].rearrange("p (l s n) -> p l s n", s=2, n=P)
            m.lower, m.upper = by_level[:, :, 0, :], by_level[:, :, 1, :]
            m.scal_buf = sb("scalars", 4 * 192 + 192 + 2 * 64 + 128)
            m.scal, at = {}, 0
            for n, heads in (("g", NG), ("step", NG), ("from_start", NG), ("to_end", NG), ("total", NG),
                             ("beta", GH), ("beta_decay", GH), ("step_to_end", SH)):
                m.scal[n] = cut(m.scal_buf, at, NT, 2, heads)
                at += NT * 2 * heads
            m.cur_buf = sb("group_scalars", 4 * NT * 2 * 8)
            m.cur = {n: cut(m.cur_buf, i * NT * 2 * 2, NT, 2, 2)
                     for i, n in enumerate(("beta", "beta_decay", "to_end", "total", "g"))}
            m.cur_ssd = {n: cut(m.cur_buf, i * NT * 2 * 8, NT, 2, 8)
                         for i, n in enumerate(("step", "step_to_end", "total", "g"))}
        yield


@contextmanager
def work_memory(nc, m, name, width=41 * T):
    with nc.sbuf_tensor(f"{name}_work", [P, width], F32) as m.work:
        yield


GAINS = (("norm1", KD), ("norm2", KD), ("final", KD), ("gdn_norm", 1), ("final_2", KD))
GAIN_WIDTH = sum(w for _, w in GAINS)


def as_columns(v):
    return np.ascontiguousarray(np.asarray(v).reshape(-1, P).T)


def column_slabs(w, width=256):
    n = w.shape[1] // width
    k = w.shape[0] // P
    return np.ascontiguousarray(w.reshape(k, P, n, width).transpose(2, 1, 0, 3).reshape(n, P, k * width))


def row_slabs(w, rows=2):
    n = w.shape[0] // (rows * P)
    return np.ascontiguousarray(w.reshape(n, rows, P, w.shape[1]).transpose(0, 2, 1, 3).reshape(n, P, -1))


def layout_first(a):
    w_in = a["w_in"][0]
    conv = np.concatenate([a["conv_w"][0], a["conv_b"]], 0)
    q, k, v, xs, b, c = np.split(np.arange(3 * D + D + 512), [D, 2 * D, 3 * D, 4 * D, 4 * D + 256])
    gate, z = 4608 + np.arange(D), 4608 + D + np.arange(D)
    s = 6656
    scal = np.concatenate([s + np.arange(16), s + 16 + np.arange(8), s + 32 + np.arange(16),
                           s + 24 + np.arange(8), s + 48 + np.arange(16)])
    two = lambda x, g: x[g * 256:(g + 1) * 256]
    gdn = [np.concatenate([two(q, g), two(k, g), two(v, g), two(gate, g)]) for g in range(4)]
    ssd = [np.concatenate([b[g * P:(g + 1) * P], c[g * P:(g + 1) * P], xs[g * 512:(g + 1) * 512],
                           z[g * 512:(g + 1) * 512]]) for g in range(2)]

    def conv_cols(cols):
        return conv[:, cols[:6 * P]].reshape(8, 6, P).transpose(2, 1, 0).reshape(P, 48)

    gdn_cols = np.zeros((4, P, 64), np.float32)
    ssd_cols = np.zeros((2, P, 64), np.float32)
    for g in range(4):
        gdn_cols[g, :, :48] = conv_cols(gdn[g])
    for g in range(2):
        ssd_cols[g, :, :48] = conv_cols(ssd[g])
        ssd_cols[g, :, 48:52] = np.repeat(a["ssd_D"][0, 8 * g:8 * g + 8], 64).reshape(4, P).T
        ssd_cols[g, :, 52:56] = as_columns(a["ssd_norm_w"][0, 512 * g:512 * g + 512])
    ga, gb, sa, sb_ = a["gdn_A_log"][0], a["gdn_dt_bias"][0], a["ssd_A_log"][0], a["ssd_dt_bias"][0]
    return {
        "w_gdn": column_slabs(w_in[:, np.concatenate(gdn)]),
        "w_ssd": column_slabs(w_in[:, np.concatenate(ssd)]),
        "w_scal": np.ascontiguousarray(w_in[:, scal].reshape(KD, P, 64).transpose(1, 0, 2)),
        "scal_bias": np.concatenate([np.zeros(16, np.float32), gb[0], sb_[0], gb[1], sb_[1]]),
        "scal_a_log": np.concatenate([ga[0], sa[0], ga[1], sa[1]]),
        "gdn_cols": gdn_cols, "ssd_cols": ssd_cols,
        "w_out_1": row_slabs(a["w_out"][0]),
        "gains": np.concatenate([as_columns(a["norm1_w"][0]), as_columns(a["norm2_w"][0]),
                                 as_columns(a["final_norm_w"]), as_columns(a["gdn_norm_w"][0]),
                                 as_columns(a["final_norm_2"])], 1),
    }


def expert_slabs(gate, up, down):
    e = gate.shape[0]
    g, u = (np.stack([column_slabs(x[i]) for i in range(e)]) for x in (gate, up))
    d = np.stack([row_slabs(down[i]) for i in range(e)])
    g, u, d = (x.reshape(e // 2, 2, 2, P, SLAB) for x in (g, u, d))
    order = [g[:, 0], u[:, 0], g[:, 1], u[:, 1], d[:, 0], d[:, 1]]
    return np.ascontiguousarray(np.stack(order, 1).reshape(e * 6, P, SLAB))


def layout_experts(a):
    return {
        "w_router": np.ascontiguousarray(a["w_router"][0].reshape(KD, P, NE).transpose(1, 0, 2)),
        "w_experts": expert_slabs(a["w_gate"][0], a["w_up"][0], a["w_down"][0]),
    }


def ffn_slabs(gate, up, down):
    k = D // P
    both = np.stack([gate.reshape(k, P, FT, P), up.reshape(k, P, FT, P)], 3)
    return np.concatenate([both.transpose(2, 1, 0, 3, 4).reshape(FT, P, SLAB), row_slabs(down)])


def layout_second(a):
    mix, cols = [], []
    z = lambda *s: np.zeros(s, np.float32)
    for l in range(LAYERS):
        w = a["w_in_2"][l]
        part = dict(zip(("c_q", "c_kv", "k_pe", "q", "kc", "vc", "ks", "vs", "kw", "vw", "gate", "sq", "sk", "sv"),
                        np.split(w, np.cumsum([256, 128, 32, 384, 128, 128, 128, 128, 128, 128, 18, 256, 256]), 1)))
        k_pe = np.concatenate([z(D, NOPE), part["k_pe"], z(D, P - QK)], 1)
        gate = np.concatenate([part["gate"], z(D, P - GATES)], 1)
        tiles = np.concatenate([part["c_q"], part["c_kv"], k_pe, part["q"], part["kc"], part["ks"], part["kw"],
                                part["vc"], part["sq"], part["sk"], gate], 1)
        by_token = np.concatenate([part["vs"], part["vw"], part["sv"]], 1)
        by_token = by_token.reshape(2, 4, P, T).transpose(0, 2, 1, 3).reshape(2, P, SLAB)
        uq = a["mla_w_uq_2"][l].reshape(2, P, MLA_H * QK).transpose(1, 0, 2).reshape(P, -1)
        mla = np.concatenate([uq, a["mla_w_ukv_2"][l], z(P, SLAB - 1920)], 1)[None]
        cmp = []
        for n in ("k", "v"):
            w1 = a[f"nsa_cmp_w1_{n}_2"][l].reshape(2, 16, HD, P).transpose(0, 2, 1, 3).reshape(2, HD, SLAB)
            cmp.append(np.concatenate([w1, w1], 1))
        mix.append(np.concatenate([column_slabs(tiles), by_token, mla, *cmp, row_slabs(a["w_out_2"][l])]))
        twice = lambda x: np.concatenate([x.T, x.T], 0)
        cols.append(np.concatenate([
            as_columns(a["ffn1_norm_2"][l]), as_columns(a["mix_norm_2"][l]), as_columns(a["ffn2_norm_2"][l]),
            as_columns(a["mla_q_norm_2"][l]), as_columns(a["mla_kv_norm_2"][l]),
            twice(a["nsa_cmp_pos_k_2"][l]), twice(a["nsa_cmp_pos_v_2"][l]),
            a["nsa_cmp_w2_k_2"][l], a["nsa_cmp_w2_v_2"][l]], 1))
    return {
        "w_ffn1": np.stack([ffn_slabs(a["ffn1_w_gate_2"][l], a["ffn1_w_up_2"][l], a["ffn1_w_down_2"][l])
                            for l in range(LAYERS)]),
        "w_ffn2": np.stack([ffn_slabs(a["ffn2_w_gate_2"][l], a["ffn2_w_up_2"][l], a["ffn2_w_down_2"][l])
                            for l in range(LAYERS)]),
        "w_mix2": np.stack(mix), "layer_cols": np.stack(cols), "gate_bias": a["nsa_gate_bias_2"],
    }


def layout_consts():
    floats, bytes_ = constants()
    return {"const_f": np.concatenate(list(floats.values()), 1), "level_masks": bytes_}


def start_stage(nc, m, io):
    x = cut(m.work, 0, NT, D)
    mask_in = cut(m.work, NT * D, m.masks.shape[1])
    with stage(nc, m, "start") as (block, sem):
        x_in, const_in, turned, turned_b = sem(4)

        @block.sync
        def _(sp):
            sp.dma_start(m.const[:, :], io["const_f"]).then_inc(const_in, 16)
            sp.dma_start(x, io["x_in"].rearrange("(t p) d -> p t d", p=P)).then_inc(x_in, 16)
            sp.dma_start(mask_in, io["level_masks"]).then_inc(const_in, 16)
            sp.dma_start(m.gain_buf[:, :], io["gains"]).then_inc(const_in, 16)
            sp.wait_ge(const_in, 48)

        @block.tensor
        def _(pe):
            pe.wait_ge(const_in, 48)
            pe.wait_ge(x_in, 16)
            for k in range(KD):
                for t in range(NT):
                    ins = pe.transpose(m.ps[:, k, tok(t)], x[:, t, tok(k)], m.ident)
                ins.then_inc(turned, 1)

        @block.gpsimd
        def _(pool):
            pool.wait_ge(const_in, 48)
            pool.tensor_copy(m.masks[:, :], mask_in)

        @block.vector
        def _(dve):
            for k in range(0, KD, 2):
                dve.wait_ge(turned, k + 1)
                dve.tensor_copy(m.resid[:, k, :], m.ps[:, k, :])

        @block.scalar
        def _(act):
            for k in range(1, KD, 2):
                act.wait_ge(turned, k + 1)
                act.activation(m.resid[:, k, :], m.ps[:, k, :], ACT.Copy)



def end_stage(nc, m, out):
    by_token = cut(m.work, 0, NT, D)
    with stage(nc, m, "end") as (block, sem):
        turned, copied_v, copied_a, stored = sem(4)

        @block.tensor
        def _(pe):
            for n in range(2 * NT):
                t, half = divmod(n, 2)
                for k in range(4):
                    ins = pe.transpose(m.ps[:, n, tok(k)], m.resid[:, 4 * half + k, tok(t)], m.ident)
                ins.then_inc(turned, 1)

        @block.vector
        def _(dve):
            for t in range(NT):
                dve.wait_ge(turned, 2 * t + 1)
                dve.tensor_copy(by_token[:, t, 0:T], m.ps[:, 2 * t, :]).then_inc(copied_v, 1)

        @block.scalar
        def _(act):
            for t in range(NT):
                act.wait_ge(turned, 2 * t + 2)
                act.activation(by_token[:, t, T:D], m.ps[:, 2 * t + 1, :], ACT.Copy).then_inc(copied_a, 1)

        @block.sync
        def _(sp):
            for t in range(NT):
                sp.wait_ge(copied_v, t + 1)
                sp.wait_ge(copied_a, t + 1)
                sp.dma_start(out[t * P:(t + 1) * P, :], by_token[:, t, :]).then_inc(stored, 16)
            sp.wait_ge(stored, 16 * NT)


def program(nc, io):
    with ExitStack() as ctx:
        m = memory(nc, ctx)
        with mixer_memory(nc, m, "mix1", True):
            with work_memory(nc, m, "recurrences"):
                start_stage(nc, m, io)
                norm_stage(nc, m, "norm1", m.resid, m.gains["norm1"], m.xT)
                scalars_stage(nc, m, io)
                with nc.Fori(0, GH // 2) as pair:
                    gdn_pair(nc, m, io, pair)
                with nc.Fori(0, SG) as g:
                    ssd_group(nc, m, io, g)
            down_stage(nc, m, "mix1_out", io["w_out_1"], 0, m.mixed, 2 * KD, 1.0)
            norm_stage(nc, m, "norm2", m.resid, m.gains["norm2"], m.xT)
            with work_memory(nc, m, "experts"):
                experts(nc, m, io)
            norm_stage(nc, m, "final", m.resid, m.gains["final"], m.resid)
        with nc.Fori(0, LAYERS) as l:
            layer(nc, m, io, l)
        with mixer_memory(nc, m, "out"), work_memory(nc, m, "out", NT * D):
            norm_stage(nc, m, "final_2", m.resid, m.gains["final_2"], m.resid)
            end_stage(nc, m, io["out"])


def layout(inputs):
    a = {n: np.asarray(v) for n, v in inputs.items()}
    return {"x_in": a["x"][0], **layout_consts(), **layout_first(a), **layout_experts(a), **layout_second(a)}


def kernel(**inputs):
    import concourse.bacc as bacc
    from concourse.bass_utils import run_bass_kernel_spmd

    nc = bacc.Bacc("TRN2", target_bir_lowering=False, num_devices=1)
    arrays = {n: np.ascontiguousarray(v) for n, v in layout(inputs).items()}
    io = {n: nc.dram_tensor(n, v.shape, mybir.dt.from_np(v.dtype), kind="ExternalInput").ap()
          for n, v in arrays.items()}
    io["out"] = nc.dram_tensor("out", (T, D), F32, kind="ExternalOutput").ap()
    program(nc, io)
    r = run_bass_kernel_spmd(nc, [arrays], core_ids=[0])
    return r.results[0]["out"].reshape(1, T, D)
```
